# Optimizing a Trainium2 kernel written in Bass

```python
import jax
import jax.numpy as jnp
from jax import lax
import numpy as np

D_MODEL = 1024
BATCH = 1
SEQ = 1024
DEPTH = 2

CTX_LEN = 256
GRID_W = 64

NA_HEADS = 4
NA_HEAD_DIM = 64
NA_WIN_R = 8
NA_WIN_C = 16

WA_HEADS = 4
WA_KV_HEADS = 2
WA_HEAD_DIM = 64
WA_WINDOW = 128
WA_BLOCK = 128

GLA_HEADS = 4
GLA_DK = 64
GLA_DV = 128
GLA_GATE_RANK = 16
GLA_GATE_TAU = 16.0
GLA_CHUNK = 64

NA_WIDTH = NA_HEADS * NA_HEAD_DIM
WA_Q_WIDTH = WA_HEADS * WA_HEAD_DIM
WA_KV_WIDTH = WA_KV_HEADS * WA_HEAD_DIM
GLA_QK_WIDTH = GLA_HEADS * GLA_DK
GLA_V_WIDTH = GLA_HEADS * GLA_DV
MIX_WIDTH = NA_WIDTH + WA_Q_WIDTH + GLA_V_WIDTH
IN_WIDTH = 3 * NA_WIDTH + WA_Q_WIDTH + 2 * WA_KV_WIDTH + 2 * GLA_QK_WIDTH + 2 * GLA_V_WIDTH + 2 * GLA_GATE_RANK

FF_DIM = 2816
FF_CONV = 3

ROPE_THETA = 10000.0
EPS = 1e-6

kernel_name = 'hybrid_na_swa_gla_dit_trunk'

def rms_norm(x, g):
    xf = x.astype(jnp.float32)
    y = xf * lax.rsqrt(jnp.mean(xf * xf, axis=-1, keepdims=True) + EPS)
    return (y * g.astype(jnp.float32)).astype(x.dtype)

def modulate(x, g, shift, scale):
    return rms_norm(x, g) * (1 + scale) + shift

def split_heads(a, n_heads):
    return a.reshape(a.shape[0], a.shape[1], n_heads, a.shape[2] // n_heads)

def in_split_points():
    widths = (NA_WIDTH, NA_WIDTH, NA_WIDTH, WA_Q_WIDTH, WA_KV_WIDTH, WA_KV_WIDTH,
              GLA_QK_WIDTH, GLA_QK_WIDTH, GLA_V_WIDTH, GLA_V_WIDTH, GLA_GATE_RANK)
    points, acc = [], 0
    for w in widths:
        acc += w
        points.append(acc)
    return points

def mixer_inputs(h, w_in, gate_w, gate_b):
    (na_q, na_k, na_v, wa_q, wa_k, wa_v, g_q, g_k, g_v, g_out, lr_f, lr_b) = jnp.split(
        h @ w_in, in_split_points(), axis=-1)

    def log_decay(lr, d):
        logit = (lr @ gate_w[d] + gate_b[d]).astype(jnp.float32)
        return split_heads(jax.nn.log_sigmoid(logit) / GLA_GATE_TAU, GLA_HEADS)

    return dict(
        na_q=split_heads(na_q, NA_HEADS), na_k=split_heads(na_k, NA_HEADS), na_v=split_heads(na_v, NA_HEADS),
        wa_q=split_heads(wa_q, WA_HEADS), wa_k=split_heads(wa_k, WA_KV_HEADS), wa_v=split_heads(wa_v, WA_KV_HEADS),
        g_q=split_heads(g_q, GLA_HEADS) * GLA_DK ** -0.5, g_k=split_heads(g_k, GLA_HEADS),
        g_v=split_heads(g_v, GLA_HEADS), g_out=g_out,
        la_f=log_decay(lr_f, 0), la_b=log_decay(lr_b, 1))

def axial_rope(n_tokens, head_dim):
    t = jnp.arange(n_tokens)
    row = (t // GRID_W).astype(jnp.float32)
    col = (t % GRID_W).astype(jnp.float32)
    n_freq = head_dim // 4
    inv = ROPE_THETA ** (-jnp.arange(n_freq, dtype=jnp.float32) / n_freq)
    ang = jnp.concatenate([row[:, None] * inv, col[:, None] * inv], axis=-1)
    return jnp.cos(ang), jnp.sin(ang)

def apply_rope(x, cos, sin):
    x1, x2 = jnp.split(x.astype(jnp.float32), 2, axis=-1)
    c, s = cos[:, None, :], sin[:, None, :]
    return jnp.concatenate([x1 * c - x2 * s, x1 * s + x2 * c], axis=-1).astype(x.dtype)

def context_attention(q, k, v, sink=None):
    B, L, H, Dh = q.shape
    Lk, Hkv = k.shape[1], k.shape[2]
    G = H // Hkv
    qg = q.reshape(B, L, Hkv, G, Dh)
    s = jnp.einsum('bqkgd,blkd->bkgql', qg, k).astype(jnp.float32) * Dh ** -0.5
    if sink is not None:
        s_sink = jnp.broadcast_to(sink.astype(jnp.float32).reshape(1, Hkv, G, 1, 1), s.shape[:-1] + (1,))
        s = jnp.concatenate([s, s_sink], axis=-1)
    p = jax.nn.softmax(s, axis=-1)[..., :Lk].astype(v.dtype)
    return jnp.einsum('bkgql,blkd->bqkgd', p, v).reshape(B, L, H, Dh)

def neighbourhood_attention(q, k, v, k_ctx, v_ctx, rpb):
    B, S, H, Dh = q.shape
    rows = S // GRID_W
    win_r = min(NA_WIN_R, rows)
    scale = Dh ** -0.5
    qg = q.reshape(B, rows, GRID_W, H, Dh)
    kg = k.reshape(B, rows, GRID_W, H, Dh)
    vg = v.reshape(B, rows, GRID_W, H, Dh)
    col = jnp.arange(GRID_W)
    col_start = jnp.clip(col - NA_WIN_C // 2, 0, GRID_W - NA_WIN_C)
    col_idx = col_start[:, None] + jnp.arange(NA_WIN_C)[None, :]
    col_off = col_idx - col[:, None] + (NA_WIN_C - 1)
    n_nb = win_r * NA_WIN_C

    def one_row(r):
        rs = jnp.clip(r - win_r // 2, 0, rows - win_r)
        kn = lax.dynamic_slice_in_dim(kg, rs, win_r, axis=1)[:, :, col_idx]
        vn = lax.dynamic_slice_in_dim(vg, rs, win_r, axis=1)[:, :, col_idx]
        qr = lax.dynamic_index_in_dim(qg, r, axis=1, keepdims=False)
        row_off = rs + jnp.arange(win_r) - r + (NA_WIN_R - 1)
        bias = rpb[:, row_off][:, :, col_off].transpose(0, 2, 1, 3).astype(jnp.float32)
        s_nb = jnp.einsum('bqhd,brqjhd->bhqrj', qr, kn).astype(jnp.float32) * scale + bias[None]
        s_ctx = jnp.einsum('bqhd,blhd->bhql', qr, k_ctx).astype(jnp.float32) * scale
        s = jnp.concatenate([s_nb.reshape(B, H, GRID_W, n_nb), s_ctx], axis=-1)
        p = jax.nn.softmax(s, axis=-1).astype(v.dtype)
        p_nb = p[..., :n_nb].reshape(B, H, GRID_W, win_r, NA_WIN_C)
        return (jnp.einsum('bhqrj,brqjhd->bqhd', p_nb, vn)
                + jnp.einsum('bhql,blhd->bqhd', p[..., n_nb:], v_ctx))

    out = lax.map(one_row, jnp.arange(rows))
    return out.transpose(1, 0, 2, 3, 4).reshape(B, S, H, Dh)

def window_attention(q, k, v, k_ctx, v_ctx, sink):
    B, S, H, Dh = q.shape
    Hkv = k.shape[2]
    G = H // Hkv
    nb = S // WA_BLOCK
    n_loc = 3 * WA_BLOCK
    L = k_ctx.shape[1]
    scale = Dh ** -0.5

    def band(a):
        ap = jnp.pad(a, ((0, 0), (WA_BLOCK, WA_BLOCK), (0, 0), (0, 0))).reshape(B, nb + 2, WA_BLOCK, Hkv, Dh)
        return jnp.concatenate([ap[:, :-2], ap[:, 1:-1], ap[:, 2:]], axis=2)

    kb, vb = band(k), band(v)
    qb = q.reshape(B, nb, WA_BLOCK, Hkv, G, Dh)
    s_loc = jnp.einsum('bnqkgd,bnskd->bnkgqs', qb, kb).astype(jnp.float32) * scale
    q_pos = jnp.arange(nb)[:, None] * WA_BLOCK + jnp.arange(WA_BLOCK)[None, :]
    k_pos = jnp.arange(nb)[:, None] * WA_BLOCK - WA_BLOCK + jnp.arange(n_loc)[None, :]
    valid = ((jnp.abs(q_pos[:, :, None] - k_pos[:, None, :]) <= WA_WINDOW)
             & (k_pos[:, None, :] >= 0) & (k_pos[:, None, :] < S))
    s_loc = jnp.where(valid[None, :, None, None], s_loc, -jnp.inf)
    s_ctx = jnp.einsum('bnqkgd,blkd->bnkgql', qb, k_ctx).astype(jnp.float32) * scale
    s_sink = jnp.broadcast_to(sink.astype(jnp.float32).reshape(1, 1, Hkv, G, 1, 1), s_loc.shape[:-1] + (1,))
    p = jax.nn.softmax(jnp.concatenate([s_loc, s_ctx, s_sink], axis=-1), axis=-1).astype(v.dtype)
    o = (jnp.einsum('bnkgqs,bnskd->bnqkgd', p[..., :n_loc], vb)
         + jnp.einsum('bnkgql,blkd->bnqkgd', p[..., n_loc:n_loc + L], v_ctx))
    return o.reshape(B, S, H, Dh)

def gla_chunk_scan(q, k, v, log_a, state0):
    B, T, H, Dk = q.shape
    Dv = v.shape[-1]
    n = T // GLA_CHUNK

    def to_chunks(a):
        return a.astype(jnp.float32).reshape(B, n, GLA_CHUNK, H, a.shape[-1]).transpose(1, 0, 3, 2, 4)

    lower_tri = jnp.tril(jnp.ones((GLA_CHUNK, GLA_CHUNK), dtype=bool))[:, :, None]

    def step(state, inp):
        qc, kc, vc, gc = inp
        b = jnp.cumsum(gc, axis=2)
        b_last = b[:, :, -1:, :]
        o_inter = jnp.einsum('bhck,bhkv->bhcv', qc * jnp.exp(b), state)
        rel = jnp.exp(jnp.where(lower_tri, b[:, :, :, None, :] - b[:, :, None, :, :], -jnp.inf))
        att = jnp.einsum('bhtk,bhsk,bhtsk->bhts', qc, kc, rel)
        o_intra = jnp.einsum('bhts,bhsv->bhtv', att, vc)
        new_state = (jnp.exp(b_last[:, :, 0, :])[..., None] * state
                     + jnp.einsum('bhsk,bhsv->bhkv', kc * jnp.exp(b_last - b), vc))
        return new_state, o_inter + o_intra

    state, o = lax.scan(step, state0, (to_chunks(q), to_chunks(k), to_chunks(v), to_chunks(log_a)))
    o = o.transpose(1, 0, 3, 2, 4).reshape(B, T, H, Dv)
    return o.astype(v.dtype), state

def gla_final_state(k, v, log_a):
    b = jnp.cumsum(log_a.astype(jnp.float32), axis=1)
    w = jnp.exp(b[:, -1:] - b)
    return jnp.einsum('bthk,bthv->bhkv', k.astype(jnp.float32) * w, v.astype(jnp.float32))

def bidirectional_gla(q, k, v, la_f, la_b, q_c, k_c, v_c, la_f_c, la_b_c, need_ctx_out):
    B = k_c.shape[0]
    zero = jnp.zeros((B, GLA_HEADS, GLA_DK, GLA_DV), jnp.float32)
    rev = lambda a: jnp.flip(a, axis=1)
    if need_ctx_out:
        oc_f, s_f = gla_chunk_scan(q_c, k_c, v_c, la_f_c, zero)
        oc_b, s_b = gla_chunk_scan(rev(q_c), rev(k_c), rev(v_c), rev(la_b_c), zero)
        o_ctx = oc_f + rev(oc_b)
    else:
        s_f = gla_final_state(k_c, v_c, la_f_c)
        s_b = gla_final_state(rev(k_c), rev(v_c), rev(la_b_c))
        o_ctx = None
    o_f, _ = gla_chunk_scan(q, k, v, la_f, s_f)
    o_b, _ = gla_chunk_scan(rev(q), rev(k), rev(v), rev(la_b), s_b)
    return o_f + rev(o_b), o_ctx

def merge_groups(o_na, o_wa, o_gla, g_out, gla_norm_g, w_out):
    B, T = o_na.shape[:2]
    o_gla = rms_norm(o_gla, gla_norm_g).reshape(B, T, GLA_V_WIDTH) * jax.nn.silu(g_out)
    y = jnp.concatenate([o_na.reshape(B, T, NA_WIDTH), o_wa.reshape(B, T, WA_Q_WIDTH), o_gla], axis=-1)
    return y @ w_out

def conv_ffn(h, w_up, conv_w, conv_b, w_down):
    value, gate = jnp.split(h @ w_up, 2, axis=-1)
    gate = lax.conv_general_dilated(
        gate, conv_w[:, None, :].astype(gate.dtype), window_strides=(1,),
        padding=((FF_CONV // 2, FF_CONV // 2),), dimension_numbers=('NWC', 'WIO', 'NWC'),
        feature_group_count=FF_DIM) + conv_b
    return (jax.nn.gelu(gate, approximate=False) * value) @ w_down

def setup_inputs(seed: int = 0) -> dict:
    key = jax.random.key(seed)
    ks = jax.random.split(key, 20)

    def nrm(k, shape, scale):
        return jax.random.normal(k, shape, jnp.float32) * scale

    return {
        'x': nrm(ks[0], (BATCH, SEQ, D_MODEL), 1.0),
        'c': nrm(ks[1], (BATCH, D_MODEL), 1.0),
        'ctx': nrm(ks[2], (BATCH, CTX_LEN, D_MODEL), 1.0),
        'c_ctx': nrm(ks[3], (D_MODEL,), 1.0),
        'w_mod': nrm(ks[4], (DEPTH, D_MODEL, 6 * D_MODEL), 0.5 * D_MODEL ** -0.5),
        'b_mod': nrm(ks[5], (DEPTH, 6 * D_MODEL), 0.02),
        'norm1_g': 1.0 + nrm(ks[6], (DEPTH, D_MODEL), 0.05),
        'norm2_g': 1.0 + nrm(ks[7], (DEPTH, D_MODEL), 0.05),
        'w_in': nrm(ks[8], (DEPTH, D_MODEL, IN_WIDTH), D_MODEL ** -0.5),
        'na_rpb': nrm(ks[9], (DEPTH, NA_HEADS, 2 * NA_WIN_R - 1, 2 * NA_WIN_C - 1), 0.1),
        'wa_sink': nrm(ks[10], (DEPTH, WA_HEADS), 0.5),
        'gla_gate_w': nrm(ks[11], (DEPTH, 2, GLA_GATE_RANK, GLA_QK_WIDTH), GLA_GATE_RANK ** -0.5),
        'gla_gate_b': nrm(ks[12], (DEPTH, 2, GLA_QK_WIDTH), 0.1),
        'gla_norm_g': 1.0 + nrm(ks[13], (DEPTH, GLA_DV), 0.05),
        'w_out': nrm(ks[14], (DEPTH, MIX_WIDTH, D_MODEL), MIX_WIDTH ** -0.5),
        'ffn_w_up': nrm(ks[15], (DEPTH, D_MODEL, 2 * FF_DIM), D_MODEL ** -0.5),
        'ffn_conv_w': nrm(ks[16], (DEPTH, FF_CONV, FF_DIM), FF_CONV ** -0.5),
        'ffn_conv_b': nrm(ks[17], (DEPTH, FF_DIM), 0.02),
        'ffn_w_down': nrm(ks[18], (DEPTH, FF_DIM, D_MODEL), FF_DIM ** -0.5),
        'final_norm_g': 1.0 + nrm(ks[19], (D_MODEL,), 0.05),
    }

def reference(x, c, ctx, c_ctx, w_mod, b_mod, norm1_g, norm2_g, w_in, na_rpb, wa_sink,
              gla_gate_w, gla_gate_b, gla_norm_g, w_out, ffn_w_up, ffn_conv_w, ffn_conv_b,
              ffn_w_down, final_norm_g):
    S = x.shape[1]
    cos, sin = axial_rope(S, WA_HEAD_DIM)
    xc = ctx
    silu_c = jax.nn.silu(c)
    silu_cc = jax.nn.silu(c_ctx)
    for i in range(DEPTH):
        last = i == DEPTH - 1
        sh1, sc1, gt1, sh2, sc2, gt2 = jnp.split((silu_c @ w_mod[i] + b_mod[i])[:, None, :], 6, axis=-1)
        csh1, csc1, cgt1, csh2, csc2, cgt2 = jnp.split(silu_cc @ w_mod[i] + b_mod[i], 6, axis=-1)

        lat = mixer_inputs(modulate(x, norm1_g[i], sh1, sc1), w_in[i], gla_gate_w[i], gla_gate_b[i])
        cx = mixer_inputs(modulate(xc, norm1_g[i], csh1, csc1), w_in[i], gla_gate_w[i], gla_gate_b[i])

        o_na = neighbourhood_attention(lat['na_q'], lat['na_k'], lat['na_v'], cx['na_k'], cx['na_v'], na_rpb[i])
        o_wa = window_attention(apply_rope(lat['wa_q'], cos, sin), apply_rope(lat['wa_k'], cos, sin),
                                lat['wa_v'], cx['wa_k'], cx['wa_v'], wa_sink[i])
        o_gla, oc_gla = bidirectional_gla(lat['g_q'], lat['g_k'], lat['g_v'], lat['la_f'], lat['la_b'],
                                          cx['g_q'], cx['g_k'], cx['g_v'], cx['la_f'], cx['la_b'],
                                          not last)
        x = x + gt1 * merge_groups(o_na, o_wa, o_gla, lat['g_out'], gla_norm_g[i], w_out[i])

        x = x + gt2 * conv_ffn(modulate(x, norm2_g[i], sh2, sc2), ffn_w_up[i], ffn_conv_w[i], ffn_conv_b[i], ffn_w_down[i])

        if not last:
            oc_na = context_attention(cx['na_q'], cx['na_k'], cx['na_v'])
            oc_wa = context_attention(cx['wa_q'], cx['wa_k'], cx['wa_v'], wa_sink[i])
            xc = xc + cgt1 * merge_groups(oc_na, oc_wa, oc_gla, cx['g_out'], gla_norm_g[i], w_out[i])
            xc = xc + cgt2 * conv_ffn(modulate(xc, norm2_g[i], csh2, csc2), ffn_w_up[i], ffn_conv_w[i],
                                      ffn_conv_b[i], ffn_w_down[i])
    return rms_norm(x, final_norm_g)


_drawn_inputs = setup_inputs


def setup_inputs(seed=0):
    import zlib

    import numpy as np

    out = dict(_drawn_inputs(seed))
    spreads = {}
    factors = {'norm1_g': 2.794,
     'na_rpb': 8.0,
     'wa_sink': 64.0,
     'gla_gate_b': 6.297,
     'gla_norm_g': 5.349,
     'ffn_conv_b': 8.0,
     'norm2_g': 4.789}
    for name, (base, spread) in spreads.items():
        noise = np.random.default_rng([zlib.crc32(name.encode()), seed]).standard_normal(out[name].shape)
        drawn = base * np.exp(spread * noise) if base else spread * noise
        out[name] = jnp.asarray(drawn.astype(out[name].dtype))
    for name, factor in factors.items():
        out[name] = (out[name] * factor).astype(out[name].dtype)
    return out
```

```python
from contextlib import ExitStack

import numpy as np

import concourse.bass as bass
from concourse import mybir

F32 = mybir.dt.float32
F32R = mybir.dt.float32r
ALU = mybir.AluOpType
ACT = mybir.ActivationFunctionType
AX = mybir.AxisListType.X

P = 128
D = 1024
KT = D // P
DEPTH = 2
SEQ = 1024
CTX = 256
T = SEQ + CTX
NTOK = T // P
FF = 2816
NFF = FF // P
EPS = 1e-6
TAU = 16.0
HEADS = 4
CHUNK = 64
NCH = T // CHUNK
NCH_LAT = SEQ // CHUNK
NA_K, WA_K, G_K, LR, NA_Q, WA_Q, G_Q, G_OUT, NFM = 0, 2, 3, 5, 6, 8, 10, 12, 16
NA_V, WA_V, G_V, NTM = 0, 256, 384, 896
HALF = NTM // 2
MASKED = -1e30
CLAMP = 80.0 * TAU


def chunks(n):
    return [(c, min(512, n - c)) for c in range(0, n, 512)]


def segments(n):
    return [(0, SEQ, 0)] + ([(SEQ, CTX, 1)] if n > SEQ else [])


def build(nc, io, out):
    ctx = ExitStack()
    with ctx:
        def sb(name, shape, dt=F32):
            return ctx.enter_context(nc.sbuf_tensor(name, shape, dt))

        def shared(*specs):
            with ExitStack() as s:
                return [s.enter_context(nc.sbuf_tensor(n, shp, dt)) for n, shp, dt in specs]

        RUNS = [r for l in range(DEPTH)
                for r in (f"n{l}0", f"p{l}", f"a{l}0", f"g{l}", f"f{l}", f"a{l}1", f"o{l}", f"n{l}1", f"u{l}")]
        sems = {}
        banks = ([], [])

        def sem(name):
            if name not in sems:
                run = name.split("_")[0]
                if run in RUNS:
                    bank = banks[RUNS.index(run) % 2]
                    used = sum(1 for k in sems if k.split("_")[0] == run)
                    if used == len(bank):
                        bank.append(ctx.enter_context(nc.semaphore(f"bank{RUNS.index(run) % 2}_{used}")))
                    sems[name] = bank[used]
                else:
                    sems[name] = ctx.enter_context(nc.semaphore(name))
            return sems[name]

        proj_fm = nc.dram_tensor("proj_fm", (NFM * P, T), F32, kind="Internal").ap()
        proj_tm = nc.dram_tensor("proj_tm", (NTOK, P, NTM), F32, kind="Internal").ap()
        mix_fm = nc.dram_tensor("mix_fm", (KT, P, T), F32, kind="Internal").ap()

        x = sb("x", [P, KT, T])
        mod = sb("mod", [P, DEPTH * 48, 2])
        bmod = sb("bmod", [P, DEPTH * 48])
        gains = sb("gains", [P, 2 * DEPTH + 1, KT])
        coef = sb("coef", [P, DEPTH * 2, KT, 2])
        silu_c = sb("silu_c", [P, KT, 2])
        ident = sb("ident", [P, P])
        ones = sb("ones", [P, P])
        sinks = sb("sinks", [P, DEPTH, 2, HEADS])
        gla_gain = sb("gla_gain", [P, DEPTH])
        conv_w = sb("conv_w", [P, DEPTH, NFF, 3])
        conv_b = sb("conv_b", [P, DEPTH, NFF])

        wm, rows = shared(("wm", [P, 3, KT, 512], F32), ("rows", [2, DEPTH * 48 * P], F32))
        dense = ctx.enter_context(ExitStack())
        h_hi = dense.enter_context(nc.sbuf_tensor("h_hi", [P, KT, T], F32R))
        h_lo = dense.enter_context(nc.sbuf_tensor("h_lo", [P, KT, T], F32R))
        (sq, rstd, nt, nfull, fo) = shared(
            ("sq", [P, 2, T], F32),
            ("rstd", [P, T], F32), ("nt", [P, 2, T], F32), ("nfull", [P, 2, T], F32), ("fo", [P, 2, T], F32))
        (w_raw, w_hi, w_lo, stage, w2_raw, w2_hi, w2_lo, stage2) = shared(
            ("w_raw", [P, 2, KT * P], F32),
            ("w_hi", [P, 2, KT * P], F32R), ("w_lo", [P, 2, KT * P], F32R), ("stage", [P, 2, T], F32),
            ("w2_raw", [P, KT, HALF], F32), ("w2_hi", [P, KT, HALF], F32R), ("w2_lo", [P, KT, HALF], F32R),
            ("stage2", [P, 2, HALF], F32))
        (fw_raw, fw_hi, fw_lo, hid_hi, hid_lo, G, cv) = shared(
            ("fw_raw", [P, 3, KT * P], F32),
            ("fw_hi", [P, 4, KT * P], F32R), ("fw_lo", [P, 4, KT * P], F32R),
            ("hid_hi", [P, 2, T], F32R), ("hid_lo", [P, 2, T], F32R), ("G", [P, T + 4], F32), ("cv", [P, T + 4], F32))
        dense.close()
        (q_raw, k_raw, qs, k_hi, k_lo, v_att, bias_t, Pm, PT, qb, mx, nmax, sums, tot, rec, o_att, o_st,
         rope_c, rope_s, q_sw) = shared(
            ("q_raw", [P, HEADS, T], F32), ("k_raw", [P, HEADS, T], F32), ("qs", [P, HEADS, T], F32R),
            ("k_hi", [P, HEADS, T], F32R), ("k_lo", [P, HEADS, T], F32R), ("v_att", [P, NTOK, 256], F32),
            ("bias_t", [P, 2, HEADS * 640], F32), ("Pm", [P, 2, 896], F32), ("PT", [P, 2, 896], F32),
            ("qb", [P, 2, HEADS, P], F32R), ("mx", [P, HEADS, 4], F32), ("nmax", [P, HEADS], F32),
            ("sums", [P, HEADS, 3], F32), ("tot", [P, HEADS], F32), ("rec", [P, HEADS], F32),
            ("o_att", [P, 2, 256], F32), ("o_st", [P, 2, 2, P], F32),
            ("rope_c", [P, SEQ], F32), ("rope_s", [P, SEQ], F32), ("q_sw", [P, SEQ], F32))
        (qd, kd, v_g, gw, gb, lr, t1, t2, b, xr, eq, ek, qp, kp, qpp, kT, att_f, att_b, U, S, oT, mask_f,
         mask_b, smask, c_ref, b_last, dif, d_last, d_ref, d_lr) = shared(
            ("qd", [P, 2, T], F32), ("kd", [P, 2, T], F32), ("v_g", [P, 2, NTOK, P], F32),
            ("gw", [32, 2, P], F32), ("gb", [P, 2, 1], F32), ("lr", [32, T], F32),
            ("t1", [P, T], F32), ("t2", [P, T], F32), ("b", [P, T], F32), ("xr", [P, T], F32),
            ("eq", [P, T], F32), ("ek", [P, T], F32), ("qp", [P, T], F32), ("kp", [P, T], F32),
            ("qpp", [P, T], F32), ("kT", [P, NTOK, P], F32), ("att_f", [P, NTOK, P], F32),
            ("att_b", [P, NTOK, P], F32), ("U", [P, NCH, P], F32), ("S", [P, NCH, P], F32),
            ("oT", [P, HEADS, T], F32), ("mask_f", [CHUNK, CHUNK], F32), ("mask_b", [CHUNK, CHUNK], F32),
            ("smask", [P, T], F32), ("c_ref", [P, NCH], F32), ("b_last", [P, NCH], F32),
            ("dif", [P, NCH], F32), ("d_last", [P, NCH], F32), ("d_ref", [P, NCH], F32), ("d_lr", [P, NCH], F32))
        ps = ctx.enter_context(nc.psum_tensor("ps", [P, 8, 512], F32))
        flat = ps[:, :, :].rearrange("p b n -> p (b n)")

        phase_done = sem("phase_done")
        count = {}

        def end_phase(eng, name, run=None):
            count[name] = count.get(name, 0) + 5
            eng.drain().then_inc(phase_done, 1)
            eng.wait_ge(phase_done, count[name])
            if name == "pool" and run:
                for handle in banks[RUNS.index(run) % 2]:
                    eng.sem_clear(handle)

        block = ctx.enter_context(nc.Block())

        NU = DEPTH * 12

        def mod_sp(sp):
            for dst, src in ((x[:], io["xT"]), (silu_c[:], io["cc"]), (bmod[:], io["b_mod"]), (gains[:], io["gains"]),
                             (sinks[:], io["sinks"]), (gla_gain[:], io["gla_gain"]), (conv_w[:], io["conv_w"]),
                             (conv_b[:], io["conv_b"])):
                sp.dma_start(dst, src).then_inc(sem("small_in"), 16)
            with sp.Fori(0, NU // 3) as i:
                for u in range(3):
                    sp.wait_ge(sem("row_done"), i * 3 + u + 1)
                    sp.dma_start(wm[:, u:u + 1], io["w_mod"][bass.ts(i * 3 + u, 1)].rearrange("o p k n -> p o k n"))\
                      .then_inc(sem(f"wm_in{u}"), 16)

        def mod_act(act):
            act.sem_inc(sem("row_out"), 3)
            act.wait_ge(sem("small_in"), 16 * 8)
            act.activation(silu_c[:], silu_c[:], ACT.Silu).then_inc(sem("silu_ready"), 1)
            with act.Fori(0, NU // 3) as i:
                for u in range(3):
                    act.wait_ge(sem("row_done"), i * 3 + u + 4)
                    act.copy(rows[:, bass.ts(i * 3 + u, 512)], ps[0:2, u, :]).then_inc(sem("row_out"), 1)

        def mod_pe(pe):
            pe.sem_inc(sem("row_done"), 3)
            pe.wait_ge(sem("silu_ready"), 1)
            with pe.Fori(0, NU // 3) as i:
                for u in range(3):
                    pe.wait_ge(sem(f"wm_in{u}"), i * 16 + 16)
                    pe.wait_ge(sem("row_out"), i * 3 + u + 1)
                    for k in range(KT):
                        mm = pe.matmul(ps[0:2, u, :], silu_c[:, k, :], wm[:, u, k, :], start=(k == 0), stop=(k == KT - 1))
                    mm.then_inc(sem("row_done"), 1)
            pe.wait_ge(sem("row_out"), 3 + NU)
            pe.wait_ge(sem("consts"), 1)
            for t in range(DEPTH * 48):
                mm = pe.transpose(ps[:, 4, 2 * t:2 * t + 2], rows[:, t * P:(t + 1) * P], ident[0:2, 0:2])
            mm.then_inc(sem("mod_t"), 1)

        def mod_dve(dve):
            dve.wait_ge(sem("mod_t"), 1)
            dve.tensor_tensor(mod[:], ps[:, 4, 0:DEPTH * 96].rearrange("p (t s) -> p t s", s=2),
                              bmod[:].unsqueeze(2).broadcast_to([P, DEPTH * 48, 2]), ALU.add).then_inc(sem("mod_v"), 1)
            dve.wait_ge(sem("mod_v"), 1)
            for l in range(DEPTH):
                for w in range(2):
                    t0 = l * 48 + (3 * w + 1) * KT
                    dve.scalar_tensor_tensor(coef[:, 2 * l + w], mod[:, t0:t0 + KT, :], 1.0,
                                             gains[:, 2 * l + w, :].unsqueeze(2).broadcast_to([P, KT, 2]),
                                             ALU.add, ALU.mult)

        def mod_pool(pool):
            pool.memset(ident[:], 0.0).then_inc(sem("ident_0"), 1)
            pool.memset(ones[:], 1.0)
            pool.wait_ge(sem("ident_0"), 1)
            pool.affine_select(out=ident[:], in_=ident[:], compare_op=ALU.not_equal, fill=1.0, base=0,
                               pattern=[[-1, P]], channel_multiplier=1).then_inc(sem("consts"), 1)

        def norm_pe(pe, s, tn):
            for k in range(KT):
                pe.wait_ge(sem(s + "sq"), k + 1)
                for c, n in chunks(tn):
                    mm = pe.matmul(flat[:, c:c + n], ones[:], sq[:, k % 2, c:c + n], start=(k == 0), stop=(k == KT - 1))
                mm.then_inc(sem(s + "sq_used"), 1)

        def norm_act_head(act, s, tn):
            for k in range(KT):
                if k >= 2:
                    act.wait_ge(sem(s + "sq_used"), k - 1)
                act.activation(sq[:, k % 2, :tn], x[:, k, :tn], ACT.Square).then_inc(sem(s + "sq"), 1)
            act.wait_ge(sem(s + "var"), 1)
            act.activation(rstd[:, :tn], rstd[:, :tn], ACT.Sqrt).then_inc(sem(s + "std"), 1)

        def norm_dve_head(dve, s, tn):
            dve.wait_ge(sem(s + "sq_used"), KT)
            dve.tensor_scalar(rstd[:, :tn], flat[:, :tn], 1.0 / D, EPS, ALU.mult, ALU.add).then_inc(sem(s + "var"), 1)
            dve.wait_ge(sem(s + "std"), 1)
            dve.reciprocal(rstd[:, :tn], rstd[:, :tn]).then_inc(sem(s + "rstd"), 1)
            dve.wait_ge(sem(s + "rstd"), 1)

        def norm_act(act, l, w):
            s, tn = f"n{l}{w}_", T if (l == 0 or w == 0) else SEQ
            norm_act_head(act, s, tn)
            for k in range(KT):
                act.wait_ge(sem(s + "xn"), k + 1)
                if k >= 2:
                    act.wait_ge(sem(s + "lo"), k - 1)
                for c, n, g in segments(tn):
                    a = act.activation(nfull[:, k % 2, c:c + n], nt[:, k % 2, c:c + n], ACT.Identity,
                                       bias=mod[:, l * 48 + 3 * w * KT + k, g:g + 1], scale=coef[:, 2 * l + w, k, g:g + 1])
                a.then_inc(sem(s + "full"), 1)
                act.wait_ge(sem(s + "full"), k + 1)
                act.copy(h_hi[:, k, :tn], nfull[:, k % 2, :tn]).then_inc(sem(s + "hi"), 1)

        def norm_dve(dve, l, w):
            s, tn = f"n{l}{w}_", T if (l == 0 or w == 0) else SEQ
            norm_dve_head(dve, s, tn)
            for k in range(KT):
                if k >= 2:
                    dve.wait_ge(sem(s + "full"), k - 1)
                dve.tensor_tensor(nt[:, k % 2, :tn], x[:, k, :tn], rstd[:, :tn], ALU.mult).then_inc(sem(s + "xn"), 1)

        def norm_pool(pool, l, w):
            s, tn = f"n{l}{w}_", T if (l == 0 or w == 0) else SEQ
            for k in range(KT):
                pool.wait_ge(sem(s + "hi"), k + 1)
                pool.tensor_tensor(h_lo[:, k, :tn], nfull[:, k % 2, :tn], h_hi[:, k, :tn], ALU.subtract)\
                    .then_inc(sem(s + "lo"), 1)

        def tile_split_act(act, s, t, u):
            act.wait_ge(sem(f"{s}w_in{u}"), 8 * t + (16 if u == 0 else 8))
            act.wait_ge(sem(s + "w_free"), t + 1)
            act.copy(w_hi[:, u, :], w_raw[:, u, :]).then_inc(sem(s + "w_hi"), 1)

        def tile_split_pool(pool, s, t, u):
            pool.wait_ge(sem(s + "w_hi"), t + 1)
            pool.tensor_tensor(w_lo[:, u, :], w_raw[:, u, :], w_hi[:, u, :], ALU.subtract).then_inc(sem(s + "w_lo"), 1)

        def tile_load(sp, s, t, u, src, raw_free):
            if raw_free is not None:
                sp.wait_ge(sem(s + "w_lo"), raw_free)
            sp.dma_start(w_raw[:, u:u + 1, :], src[bass.ts(t, 1)].rearrange("o p n -> p o n"))\
              .then_inc(sem(f"{s}w_in{u}"), 16)

        def tile_pe(pe, s, t, u, tn):
            pe.wait_ge(sem(s + "w_lo"), t + 1)
            pe.wait_ge(sem(s + "evac"), t + 1)
            wh = w_hi[:, u, :].rearrange("p (k m) -> p k m", m=P)
            wl = w_lo[:, u, :].rearrange("p (k m) -> p k m", m=P)
            cs = chunks(tn)
            for c, n in cs:
                o = flat[:, u * 1536 + c:u * 1536 + c + n]
                for k in range(KT):
                    pe.matmul(o, wh[:, k], h_hi[:, k, c:c + n], start=(k == 0), stop=False)
                    pe.matmul(o, wh[:, k], h_lo[:, k, c:c + n], start=False, stop=False)
                    mm = pe.matmul(o, wl[:, k], h_hi[:, k, c:c + n], start=False, stop=(k == KT - 1))
            mm.then_inc(sem(s + "w_free"), 1)

        def proj_sp(sp, l):
            s = f"p{l}_"
            wfm = io["w_fm"][l]

            def store(t, u):
                sp.wait_ge(sem(s + "staged"), t + 1)
                sp.dma_start(proj_fm.rearrange("(t p) n -> t p n", p=P)[bass.ts(t, 1)].rearrange("o p n -> p o n"),
                             stage[:, u:u + 1, :]).then_inc(sem(f"{s}st_out{u}"), 16)

            def load_half(hf):
                if hf:
                    sp.wait_ge(sem(s + "w2_lo"), hf)
                sp.dma_start(w2_raw[:], io["w_tm"][l, hf]).then_inc(sem(s + "w2_in"), 16)

            def store_half(hf):
                for j in range(NTOK):
                    sp.wait_ge(sem(s + "staged2"), hf * NTOK + j + 1)
                    sp.dma_start(proj_tm[j, :, hf * HALF:(hf + 1) * HALF], stage2[:, j % 2, :])\
                      .then_inc(sem(f"{s}st2_out{j % 2}"), 16)

            tile_load(sp, s, 0, 0, wfm, None)
            tile_load(sp, s, 1, 1, wfm, None)
            load_half(0)
            with sp.Fori(0, 4) as i:
                for u in range(2):
                    tile_load(sp, s, i * 2 + u + 2, u, wfm, i * 2 + u + 1)
                    store(i * 2 + u, u)
            store_half(0)
            load_half(1)
            with sp.Fori(4, 7) as i:
                for u in range(2):
                    tile_load(sp, s, i * 2 + u + 2, u, wfm, i * 2 + u + 1)
                    store(i * 2 + u, u)
            for t in (NFM - 2, NFM - 1):
                store(t, t % 2)
            store_half(1)
            for u in range(2):
                sp.wait_ge(sem(f"{s}st_out{u}"), 16 * NFM // 2)
                sp.wait_ge(sem(f"{s}st2_out{u}"), 16 * NTOK)

        def proj_act(act, l):
            s = f"p{l}_"
            for half in range(2):
                with act.Fori(4 * half, 4 * half + 4) as i:
                    for u in range(2):
                        tile_split_act(act, s, i * 2 + u, u)
                act.wait_ge(sem(s + "w2_in"), 16 * (half + 1))
                if half:
                    act.wait_ge(sem(s + "w2_free"), 1)
                act.copy(w2_hi[:], w2_raw[:]).then_inc(sem(s + "w2_hi"), 1)

        def proj_pool(pool, l):
            s = f"p{l}_"
            for half in range(2):
                with pool.Fori(4 * half, 4 * half + 4) as i:
                    for u in range(2):
                        tile_split_pool(pool, s, i * 2 + u, u)
                pool.wait_ge(sem(s + "w2_hi"), half + 1)
                pool.tensor_tensor(w2_lo[:], w2_raw[:], w2_hi[:], ALU.subtract).then_inc(sem(s + "w2_lo"), 1)

        def proj_pe(pe, l):
            s = f"p{l}_"
            pe.sem_inc(sem(s + "w_free"), 2)
            for half in range(2):
                with pe.Fori(4 * half, 4 * half + 4) as i:
                    for u in range(2):
                        tile_pe(pe, s, i * 2 + u, u, T)
                pe.wait_ge(sem(s + "w2_lo"), half + 1)
                for j in range(NTOK):
                    pe.wait_ge(sem(s + "evac2"), half * NTOK + j + 1)
                    tok = slice(j * P, (j + 1) * P)
                    o = ps[:, 6 + j % 2, 0:HALF]
                    for k in range(KT):
                        pe.matmul(o, h_hi[:, k, tok], w2_hi[:, k, :], start=(k == 0), stop=False)
                        pe.matmul(o, h_lo[:, k, tok], w2_hi[:, k, :], start=False, stop=False)
                        mm = pe.matmul(o, h_hi[:, k, tok], w2_lo[:, k, :], start=False, stop=(k == KT - 1))
                    mm.then_inc(sem(s + "done2"), 1)
                pe.wait_ge(sem(s + "done2"), NTOK * (half + 1))
                pe.sem_inc(sem(s + "w2_free"), 1)

        def proj_dve(dve, l):
            s = f"p{l}_"
            dve.sem_inc(sem(s + "evac"), 2)
            dve.sem_inc(sem(s + "evac2"), 2)

            def tile(t, u, first):
                dve.wait_ge(sem(s + "w_free"), t + 3)
                if not first:
                    dve.wait_ge(sem(f"{s}st_out{u}"), 8 * t + (0 if u == 0 else -8))
                dve.tensor_copy(stage[:, u, :], flat[:, u * 1536:u * 1536 + T]).then_inc(sem(s + "staged"), 1)
                dve.wait_ge(sem(s + "staged"), t + 1)
                dve.sem_inc(sem(s + "evac"), 1)

            for half in range(2):
                if half == 0:
                    tile(0, 0, True)
                    tile(1, 1, True)
                with dve.Fori(4 * half + (half == 0), 4 * half + 4) as i:
                    for u in range(2):
                        tile(i * 2 + u, u, False)
                for j in range(NTOK):
                    n = half * NTOK + j
                    dve.wait_ge(sem(s + "done2"), n + 1)
                    if n >= 2:
                        dve.wait_ge(sem(f"{s}st2_out{j % 2}"), 16 * (n // 2))
                    dve.tensor_copy(stage2[:, j % 2, :], ps[:, 6 + j % 2, 0:HALF]).then_inc(sem(s + "staged2"), 1)
                    dve.wait_ge(sem(s + "staged2"), n + 1)
                    dve.sem_inc(sem(s + "evac2"), 1)

        KW = (5, 3)
        PIECES = ([(512, 256, 384), (0, 0, 256)], [(512, 0, 384)])

        def att_name(l, kind):
            return f"a{l}{kind}_"

        def att_each(eng, l, kind, body):
            last, off = SEQ // P - KW[kind], 2 - kind
            for u in range(2):
                body(u, u, 0, True)
            with eng.Fori(1, 3) as i:
                for u in range(2):
                    body(i * 2 + u, u, i * 2 + u - off, True)
            for u in range(2):
                body(6 + u, u, last, True)
            if l == 0:
                for u in range(2):
                    body(8 + u, u, 0, False)

        def att_sp(sp, l, kind):
            s = att_name(l, kind)
            kv = 64 if kind == 0 else 128
            for dup in range(2):
                half = slice(64 * dup, 64 * dup + 64)
                for dst, base, nh in ((q_raw, (NA_Q, WA_Q)[kind], 4), (k_raw, (NA_K, WA_K)[kind], (4, 2)[kind])):
                    sp.dma_start(dst[half, 0:nh, :],
                                 proj_fm[base * P:base * P + nh * 64, :].rearrange("(h d) t -> d h t", d=64))\
                      .then_inc(sem(s + "qk_in"), 16)
            vc, vn = ((NA_V, 256), (WA_V, 128))[kind]
            sp.dma_start(v_att[:, :, 0:vn], proj_tm[:, :, vc:vc + vn].rearrange("j p c -> p j c")).then_inc(sem(s + "qk_in"), 16)
            if kind == 1:
                sp.dma_start(rope_c[:], io["rope"][0]).then_inc(sem(s + "qk_in"), 16)
                sp.dma_start(rope_s[:], io["rope"][1]).then_inc(sem(s + "qk_in"), 16)
                for h in range(6):
                    base = WA_Q * P + 64 * h if h < 4 else WA_K * P + 64 * (h - 4)
                    if h:
                        sp.wait_ge(sem(s + "sw_used"), h)
                    for dup in range(2):
                        for r in range(2):
                            at = 64 * dup + 32 * r
                            sp.dma_start(q_sw[at:at + 32, :], proj_fm[base + 32 * (1 - r):base + 32 * (1 - r) + 32, 0:SEQ])\
                              .then_inc(sem(s + "sw_in"), 16)

            def bias(n, u, w0, local):
                if local:
                    sp.wait_ge(sem(s + "bias_free"), n + 1)
                    if kind == 0:
                        sp.dma_start(bias_t[:, u:u + 1, :], io["na_bias"][l, bass.ts(n, 1)].rearrange("o p n -> p o n"))\
                          .then_inc(sem(f"{s}bias_in{u}"), 16)
                    else:
                        sp.dma_start(bias_t[:, u:u + 1, 0:384], io["wa_mask"][bass.ts(n, 1)].rearrange("o p n -> p o n"))\
                          .then_inc(sem(f"{s}bias_in{u}"), 16)

            def store(n, u, w0, local):
                sp.wait_ge(sem(s + "o_staged"), n + 1)
                sp.dma_start(mix_fm[2 * kind:2 * kind + 2, :, bass.ts(n, P)].rearrange("o p t -> p o t"), o_st[:, u])\
                  .then_inc(sem(f"{s}o_out{u}"), 16)

            def both(n, u, w0, local):
                bias(n, u, w0, local)
                store(n, u, w0, local)
            for u in range(2):
                bias(u, u, 0, True)
            with sp.Fori(0, 3) as i:
                for u in range(2):
                    bias(i * 2 + u + 2, u, 0, True)
                    store(i * 2 + u, u, 0, True)
            for u in range(2):
                store(6 + u, u, 0, True)
            nb = 8
            if l == 0:
                nb = 10
                for u in range(2):
                    store(8 + u, u, 0, False)
            for u in range(2):
                sp.wait_ge(sem(f"{s}o_out{u}"), 16 * nb // 2)

        def att_act(act, l, kind):
            s = att_name(l, kind)
            act.sem_inc(sem(s + "s_free"), 2)
            act.wait_ge(sem("small_in"), 16 * 8)
            act.copy(mx[:, :, 3], sinks[:, l, kind, :]).then_inc(sem(s + "sink"), 1)
            act.wait_ge(sem(s + "sink"), 1)

            def body(n, u, w0, local):
                nl = KW[kind] * P if local else 0
                nt_ = nl + CTX

                def exps(h):
                    p = h % 2
                    act.wait_ge(sem(s + "max"), n * HEADS + h + 1)
                    if nl:
                        act.activation(Pm[:, p, 0:nl], Pm[:, p, 0:nl], ACT.Exp, bias=nmax[:, h:h + 1],
                                       accum_out=sums[:, h, 0:1])
                    act.activation(Pm[:, p, nl:nt_], ps[:, 2 * p, 256:512], ACT.Exp, bias=nmax[:, h:h + 1],
                                   accum_out=sums[:, h, 1:2])
                    act.activation(sums[:, h, 2:3], mx[:, h, 3:4], ACT.Exp, bias=nmax[:, h:h + 1])\
                       .then_inc(sem(s + "p_ready"), 1)

                def turned(h):
                    act.wait_ge(sem(s + "turned"), n * HEADS + h + 1)
                    act.copy(PT[:, h % 2, 0:min(512, nt_)], ps[:, 4, 0:min(512, nt_)]).then_inc(sem(s + "pt_a"), 1)

                exps(0)
                for h in range(HEADS):
                    if h + 1 < HEADS:
                        exps(h + 1)
                    turned(h)
                act.wait_ge(sem(s + "o_turned"), n + 1)
                act.wait_ge(sem(s + "o_free"), n + 1)
                act.copy(o_st[:, u], ps[:, 7, 0:256].rearrange("p (o t) -> p o t", o=2)).then_inc(sem(s + "o_staged"), 1)
            att_each(act, l, kind, body)

        def att_dve(dve, l, kind):
            s = att_name(l, kind)
            dve.wait_ge(sem(s + "qk_in"), 16 * (5 + 2 * kind))
            step = [0]

            def chain(ins):
                step[0] += 1
                ins.then_inc(sem(s + "dve_step"), 1)
                dve.wait_ge(sem(s + "dve_step"), step[0])
            if kind == 1:
                for h in range(6):
                    r = q_raw[:, h, 0:SEQ] if h < 4 else k_raw[:, h - 4, 0:SEQ]
                    chain(dve.tensor_tensor(r, r, rope_c[:], ALU.mult))
                    dve.wait_ge(sem(s + "sw_in"), 64 * (h + 1))
                    chain(dve.tensor_tensor(q_sw[:], q_sw[:], rope_s[:], ALU.mult))
                    chain(dve.tensor_tensor(r, r, q_sw[:], ALU.add))
                    dve.sem_inc(sem(s + "sw_used"), 1)
            chain(dve.tensor_scalar(qs[:], q_raw[:], 0.125, None, ALU.mult))
            chain(dve.scalar_tensor_tensor(qs[64:P], q_raw[64:P], 0.125, qs[64:P], ALU.mult, ALU.subtract))
            nk = (4, 2)[kind]
            chain(dve.tensor_copy(k_hi[:, 0:nk], k_raw[:, 0:nk]))
            dve.tensor_tensor(k_lo[:, 0:nk], k_raw[:, 0:nk], k_hi[:, 0:nk], ALU.subtract).then_inc(sem(s + "split"), 1)

            def body(n, u, w0, local):
                nl = KW[kind] * P if local else 0
                if nl:
                    dve.wait_ge(sem(f"{s}bias_in{u}"), 8 * n + (16 if u == 0 else 8))

                def maxes(h):
                    p = h % 2
                    unit = n * HEADS + h
                    dve.wait_ge(sem(s + "s_done"), unit + 1)
                    dve.wait_ge(sem(s + "p_free"), unit + 1)
                    bt = bias_t[:, u, :]
                    k = len(PIECES[kind]) if nl else 0
                    for kk in range(k, 3):
                        dve.tensor_reduce(mx[:, h, kk:kk + 1], ps[:, 2 * p, 256:512], AX, ALU.max).then_inc(sem(s + "mx"), 1)
                    k = 0
                    if nl:
                        for col, off, cnt in PIECES[kind]:
                            bo = h * 640 + off if kind == 0 else off
                            dve.tensor_tensor_reduce(Pm[:, p, off:off + cnt], flat[:, 1024 * p + col:1024 * p + col + cnt],
                                                     bt[:, bo:bo + cnt], 1.0, MASKED, ALU.add, ALU.max,
                                                     mx[:, h, k:k + 1]).then_inc(sem(s + "mx"), 1)
                            k += 1
                    dve.wait_ge(sem(s + "mx"), unit * 3 + 3)
                    dve.wait_ge(sem(s + "sink"), 1)
                    dve.tensor_reduce(nmax[:, h:h + 1], mx[:, h, :], AX, ALU.max, negate=True).then_inc(sem(s + "max"), 1)

                def turned(h):
                    if nl + CTX > 512:
                        dve.wait_ge(sem(s + "turned"), n * HEADS + h + 1)
                        dve.tensor_copy(PT[:, h % 2, 512:nl + CTX], ps[:, 5, 0:nl + CTX - 512]).then_inc(sem(s + "pt_b"), 1)

                maxes(0)
                maxes(1)
                for h in range(HEADS):
                    turned(h)
                    if h + 2 < HEADS:
                        maxes(h + 2)
                dve.wait_ge(sem(s + "p_ready"), n * HEADS + HEADS)
                dve.tensor_reduce(tot[:], sums[:, :, 0 if local else 1:3], AX, ALU.add).then_inc(sem(s + "tot"), 1)
                dve.wait_ge(sem(s + "tot"), n + 1)
                dve.reciprocal(rec[:], tot[:]).then_inc(sem(s + "rec"), 1)
                dve.wait_ge(sem(s + "rec"), n + 1)
                dve.wait_ge(sem(s + "o_done"), n + 1)
                dve.tensor_tensor(o_att[:, u, :].rearrange("p (h d) -> p h d", h=HEADS),
                                  ps[:, 6, 0:256].rearrange("p (h d) -> p h d", h=HEADS),
                                  rec[:].unsqueeze(2).broadcast_to([P, HEADS, 64]), ALU.mult).then_inc(sem(s + "o_norm"), 1)
            att_each(dve, l, kind, body)

        def att_pool(pool, l, kind):
            s = att_name(l, kind)
            pool.sem_inc(sem(s + "bias_free"), 2)
            pool.sem_inc(sem(s + "o_free"), 2)
            pool.wait_ge(sem(s + "split"), 1)

            def body(n, u, w0, local):
                pool.wait_ge(sem(s + "qb_free"), n + 1)
                pool.tensor_copy(qb[:, u], qs[:, :, bass.ts(n, P)]).then_inc(sem(s + "qb"), 1)
                if local:
                    pool.wait_ge(sem(s + "max"), n * HEADS + HEADS)
                    pool.sem_inc(sem(s + "bias_free"), 1)

            def release(n, u):
                pool.wait_ge(sem(f"{s}o_out{u}"), 8 * n + (16 if u == 0 else 8))
                pool.sem_inc(sem(s + "o_free"), 1)

            for u in range(2):
                body(u, u, 0, True)
            with pool.Fori(1, 4) as i:
                for u in range(2):
                    body(i * 2 + u, u, 0, True)
                    release(i * 2 + u - 2, u)
            if l == 0:
                for u in range(2):
                    body(8 + u, u, 0, False)
                    release(6 + u, u)

        def att_pe(pe, l, kind):
            s = att_name(l, kind)
            pe.sem_inc(sem(s + "qb_free"), 2)
            pe.sem_inc(sem(s + "p_free"), 2)
            pe.wait_ge(sem(s + "split"), 1)

            def body(n, u, w0, local):
                nl = KW[kind] * P if local else 0
                pe.wait_ge(sem(s + "qb"), n + 1)

                def scores(h):
                    p = h % 2
                    pe.wait_ge(sem(s + "s_free"), n * HEADS + h + 1)
                    kh = h if kind == 0 else h // 2
                    lhs = qb[:, u, h, :]
                    pieces = [(256, SEQ, 256)]
                    if nl:
                        pieces += [(col, w0 * P + off, cnt) for col, off, cnt in PIECES[kind]]
                    for col, k0, cnt in pieces:
                        o = flat[:, 1024 * p + col:1024 * p + col + cnt]
                        pe.matmul(o, lhs, k_hi[:, kh, bass.ds(k0, cnt)], start=True, stop=False)
                        mm = pe.matmul(o, lhs, k_lo[:, kh, bass.ds(k0, cnt)], start=False, stop=True)
                    mm.then_inc(sem(s + "s_done"), 1)

                def turn_and_sum(h):
                    p = h % 2
                    unit = n * HEADS + h
                    ntile = nl // P + 2
                    pe.wait_ge(sem(s + "p_ready"), unit + 1)
                    for t in range(ntile):
                        mm = pe.transpose(ps[:, 4 + t // 4, (t % 4) * P:(t % 4 + 1) * P], Pm[:, p, t * P:(t + 1) * P], ident[:])
                    mm.then_inc(sem(s + "turned"), 1)
                    pe.wait_ge(sem(s + "turned"), unit + 1)
                    pe.sem_inc(sem(s + "p_free"), 1)
                    pe.sem_inc(sem(s + "s_free"), 1)
                    pe.wait_ge(sem(s + "pt_a"), unit + 1)
                    if ntile > 4:
                        pe.wait_ge(sem(s + "pt_b"), unit + 1)
                    if h == 0:
                        pe.wait_ge(sem(s + "o_norm"), n) if not isinstance(n, int) or n > 0 else None
                    vc = (h if kind == 0 else h // 2) * 64
                    for t in range(ntile):
                        kt = (w0 + t) if t < nl // P else SEQ // P + t - nl // P
                        mm = pe.matmul(ps[:, 6, h * 64:(h + 1) * 64], PT[:, p, t * P:(t + 1) * P],
                                       v_att[:, bass.ds(kt, 1), vc:vc + 64].rearrange("p o d -> p (o d)"),
                                       start=(t == 0), stop=(t == ntile - 1))
                    if h == HEADS - 1:
                        mm.then_inc(sem(s + "o_done"), 1)

                scores(0)
                scores(1)
                for h in range(HEADS):
                    turn_and_sum(h)
                    if h + 2 < HEADS:
                        scores(h + 2)
                pe.sem_inc(sem(s + "qb_free"), 1)
                pe.wait_ge(sem(s + "o_norm"), n + 1)
                if not isinstance(n, int) or n > 0:
                    pe.wait_ge(sem(s + "o_staged"), n)
                for g in range(2):
                    mm = pe.transpose(ps[:, 7, g * P:(g + 1) * P], o_att[:, u, g * P:(g + 1) * P], ident[:])
                mm.then_inc(sem(s + "o_turned"), 1)
            att_each(pe, l, kind, body)

        def gla_sp(sp, l):
            s = f"g{l}_"
            sp.dma_start(lr[:], proj_fm[LR * P:LR * P + 32, :]).then_inc(sem(s + "lr_in"), 16)
            sp.dma_start(smask[:], io["smask"]).then_inc(sem(s + "lr_in"), 16)
            sp.dma_start(mask_f[:], io["tri"][0]).then_inc(sem(s + "lr_in"), 16)
            sp.dma_start(mask_b[:], io["tri"][1]).then_inc(sem(s + "lr_in"), 16)
            with sp.Fori(0, 2) as i:
                for u in range(2):
                    h = i * 2 + u
                    sp.wait_ge(sem(s + "in_free"), h + 1)
                    for dup in range(2):
                        half = slice(64 * dup, 64 * dup + 64)
                        for dst, base in ((qd, G_Q), (kd, G_K)):
                            sp.dma_start(dst[half, u, :], proj_fm[bass.ds(h * 64 + base * P, 64), :]).then_inc(sem(f"{s}in{u}"), 16)
                    sp.dma_start(v_g[:, u], proj_tm[:, :, bass.ds(h * P + G_V, P)].rearrange("j p c -> p j c")).then_inc(sem(f"{s}in{u}"), 16)
                    sp.dma_start(gw[:, u:u + 1, :], io["gate_w"][l, bass.ts(h, 1)].rearrange("o r c -> r o c")).then_inc(sem(f"{s}in{u}"), 16)
                    sp.dma_start(gb[:, u:u + 1, :], io["gate_b"][l, bass.ts(h, 1)].rearrange("o p c -> p o c")).then_inc(sem(f"{s}in{u}"), 16)
        GIN = 16 * 7

        def gla_act(act, l):
            s = f"g{l}_"
            to = T if l == 0 else SEQ
            act.wait_ge(sem(s + "lr_in"), 64)
            with act.Fori(0, 2) as i:
                for u in range(2):
                    h = i * 2 + u
                    act.wait_ge(sem(s + "logit"), h + 1)
                    act.activation(t1[:], flat[:, 0:T], ACT.Abs, bias=gb[:, u, :]).then_inc(sem(s + "act_a"), 1)
                    act.wait_ge(sem(s + "act_a"), h * 3 + 1)
                    act.activation(t1[:], t1[:], ACT.Exp, scale=-1.0).then_inc(sem(s + "act_a"), 1)
                    act.wait_ge(sem(s + "act_a"), h * 3 + 2)
                    act.activation(t1[:], t1[:], ACT.Ln, bias=1.0).then_inc(sem(s + "act_a"), 1)
                    act.wait_ge(sem(s + "x"), h + 1)
                    act.activation(eq[:], xr[:], ACT.Exp, scale=1.0 / TAU).then_inc(sem(s + "eq"), 1)
                    act.activation(ek[:], xr[:], ACT.Exp, scale=-1.0 / TAU).then_inc(sem(s + "ek"), 1)
                    act.activation(d_last[:], b_last[:], ACT.Exp, scale=1.0 / TAU)
                    act.activation(d_ref[:], c_ref[:], ACT.Exp, scale=1.0 / TAU)
                    act.activation(d_lr[:], dif[:], ACT.Exp, scale=1.0 / TAU).then_inc(sem(s + "decay"), 1)
                    for r, n in enumerate((4, 4, 2)):
                        act.wait_ge(sem(s + "kt"), h * 3 + r + 1)
                        act.copy(kT[:, 4 * r:4 * r + n, :], ps[:, 5, 0:n * P].rearrange("p (j c) -> p j c", c=P))\
                           .then_inc(sem(s + "kt_out"), 1)
                    act.wait_ge(sem(s + "o"), h + 1)
                    act.copy(oT[:, bass.ts(h, 1), 0:to], flat[:, 0:to].unsqueeze(1)).then_inc(sem(s + "o_out"), 1)

        def gla_pe(pe, l):
            s = f"g{l}_"
            no = (T if l == 0 else SEQ) // P
            pe.sem_inc(sem(s + "in_free"), 2)
            pe.wait_ge(sem(s + "lr_in"), 64)
            pe.wait_ge(sem(s + "zeroed"), 2)
            with pe.Fori(0, 2) as i:
                for u in range(2):
                    h = i * 2 + u
                    pe.wait_ge(sem(f"{s}in{u}"), i * GIN + GIN)
                    pe.wait_ge(sem(s + "o_out"), h + 1)
                    for c, n in chunks(T):
                        mm = pe.matmul(flat[:, c:c + n], gw[:, u, :], lr[:, c:c + n], start=True, stop=True)
                    mm.then_inc(sem(s + "logit"), 1)
                    pe.wait_ge(sem(s + "kp"), h + 1)
                    for r, n in enumerate((4, 4, 2)):
                        pe.wait_ge(sem(s + "kt_out"), h * 3 + r + 1)
                        for j in range(n):
                            t = 4 * r + j
                            mm = pe.transpose(ps[:, 5, j * P:(j + 1) * P], kp[:, t * P:(t + 1) * P], ident[:])
                        mm.then_inc(sem(s + "kt"), 1)
                    pe.wait_ge(sem(s + "qp"), h + 1)
                    for r, n in enumerate((4, 4, 2)):
                        pe.wait_ge(sem(s + "att_out"), h * 3 + r + 1)
                        pe.wait_ge(sem(s + "kt_out"), h * 3 + r + 2)
                        pe.wait_ge(sem(s + "u_out"), h * 3 + r + 1)
                        for j in range(n):
                            t = 4 * r + j
                            pe.matmul(ps[:, 3, j * P:(j + 1) * P], kT[0:64, t, :], v_g[0:64, u, t, :], start=True, stop=True)
                            mm = pe.matmul(ps[:, 4, j * P:(j + 1) * P], kT[64:P, t, :], v_g[64:P, u, t, :], start=True, stop=True)
                        mm.then_inc(sem(s + "u"), 1)
                        for j in range(2 * n):
                            ch = 8 * r + j
                            cols = slice(ch * CHUNK, (ch + 1) * CHUNK)
                            pe.matmul(ps[0:CHUNK, 6, j * CHUNK:(j + 1) * CHUNK], kp[0:64, cols], qp[0:64, cols], start=True, stop=True)
                            mm = pe.matmul(ps[0:CHUNK, 7, j * CHUNK:(j + 1) * CHUNK], kp[64:P, cols], qp[64:P, cols], start=True, stop=True)
                        mm.then_inc(sem(s + "att"), 1)
                    pe.wait_ge(sem(s + "att_out"), h * 3 + 4)
                    pe.wait_ge(sem(s + "state"), h + 1)
                    pe.wait_ge(sem(s + "qpp"), h + 1)
                    for t in range(no):
                        o = flat[:, t * P:(t + 1) * P]
                        pe.matmul(o, v_g[:, u, t, :], att_f[:, t, :], start=True, stop=False)
                        pe.matmul(o, v_g[:, u, t, :], att_b[:, t, :], start=False, stop=False)
                        for e in range(2):
                            ch = 2 * t + e
                            mm = pe.matmul(flat[:, ch * CHUNK:(ch + 1) * CHUNK], S[:, ch, :],
                                           qpp[:, ch * CHUNK:(ch + 1) * CHUNK], start=False, stop=(e == 1))
                    mm.then_inc(sem(s + "o"), 1)
                    pe.wait_ge(sem(s + "o"), h + 1)
                    pe.sem_inc(sem(s + "in_free"), 1)

        def gla_pool(pool, l):
            s = f"g{l}_"
            pool.memset(att_f[:], 0.0).then_inc(sem(s + "zeroed"), 1)
            pool.memset(att_b[:], 0.0).then_inc(sem(s + "zeroed"), 1)
            pool.sem_inc(sem(s + "o_out"), 1)
            pool.sem_inc(sem(s + "kt_out"), 1)
            pool.sem_inc(sem(s + "att_out"), 1)
            pool.sem_inc(sem(s + "u_out"), 1)
            with pool.Fori(0, 2) as i:
                for u in range(2):
                    h = i * 2 + u
                    pool.wait_ge(sem(f"{s}in{u}"), i * GIN + GIN)
                    pool.wait_ge(sem(s + "o_out"), h + 1)
                    pool.wait_ge(sem(s + "ek"), h + 1)
                    pool.tensor_tensor(kp[:], kd[:, u, :], ek[:], ALU.mult).then_inc(sem(s + "kp"), 1)
                    pool.wait_ge(sem(s + "qp"), h + 1)
                    pool.wait_ge(sem(s + "decay"), h + 1)
                    pool.tensor_tensor(qpp[:].rearrange("p (n c) -> p n c", c=CHUNK), qp[:].rearrange("p (n c) -> p n c", c=CHUNK),
                                       d_ref[:].unsqueeze(2).broadcast_to([P, NCH, CHUNK]), ALU.mult).then_inc(sem(s + "qpp"), 1)

        def gla_dve(dve, l):
            s = f"g{l}_"
            no = (T if l == 0 else SEQ) // P
            dve.wait_ge(sem(s + "lr_in"), 64)
            dve.wait_ge(sem(s + "zeroed"), 2)
            order_f = list(range(NCH_LAT, NCH)) + list(range(NCH_LAT))
            order_b = list(range(NCH - 1, NCH_LAT - 1, -1)) + list(range(NCH_LAT - 1, -1, -1))
            dve.memset(S[0:64, order_f[0], :], 0.0).then_inc(sem(s + "s0"), 1)
            dve.memset(S[64:P, order_b[0], :], 0.0).then_inc(sem(s + "s0"), 1)
            dve.wait_ge(sem(s + "s0"), 2)
            bc = b[:].rearrange("p (n c) -> p n c", c=CHUNK)
            mid = CHUNK // 2
            per_head = 4 + 4 + 3
            with dve.Fori(0, 2) as i:
                for u in range(2):
                    h = i * 2 + u
                    st = [0]

                    def chain(ins):
                        st[0] += 1
                        ins.then_inc(sem(s + "dve_step"), 1)
                        dve.wait_ge(sem(s + "dve_step"), h * per_head + st[0])
                    dve.wait_ge(sem(s + "logit"), h + 1)
                    dve.wait_ge(sem(s + "act_a"), h * 3 + 1)
                    chain(dve.tensor_scalar(t2[:], flat[:, 0:T], gb[:, u, :], 0.0, ALU.add, ALU.min))
                    dve.wait_ge(sem(s + "act_a"), h * 3 + 3)
                    chain(dve.tensor_tensor(t2[:], t2[:], t1[:], ALU.subtract))
                    chain(dve.tensor_tensor_scan(b[0:64, :], smask[0:64, :], t2[0:64, :], 0.0, ALU.mult, ALU.add))
                    chain(dve.tensor_tensor_scan(b[64:P, ::-1], smask[64:P, ::-1], t2[64:P, ::-1], 0.0, ALU.mult, ALU.add))
                    chain(dve.tensor_copy(c_ref[0:64, :], bc[0:64, :, mid - 1]))
                    chain(dve.tensor_copy(c_ref[64:P, :], bc[64:P, :, mid]))
                    chain(dve.tensor_copy(b_last[0:64, :], bc[0:64, :, CHUNK - 1]))
                    chain(dve.tensor_copy(b_last[64:P, :], bc[64:P, :, 0]))
                    chain(dve.tensor_tensor(dif[:], b_last[:], c_ref[:], ALU.subtract))
                    chain(dve.tensor_tensor(xr[:].rearrange("p (n c) -> p n c", c=CHUNK), bc,
                                            c_ref[:].unsqueeze(2).broadcast_to([P, NCH, CHUNK]), ALU.subtract))
                    chain(dve.tensor_scalar(xr[:], xr[:], -CLAMP, CLAMP, ALU.max, ALU.min))
                    assert st[0] == per_head
                    dve.sem_inc(sem(s + "x"), 1)
                    dve.wait_ge(sem(f"{s}in{u}"), i * GIN + GIN)
                    dve.wait_ge(sem(s + "eq"), h + 1)
                    dve.scalar_tensor_tensor(qp[:], qd[:, u, :], 0.125, eq[:], ALU.mult, ALU.mult).then_inc(sem(s + "qp"), 1)
                    dve.wait_ge(sem(s + "decay"), h + 1)
                    U2 = U[:].rearrange("p (j e) c -> p j e c", e=2)
                    d2 = d_lr[:].rearrange("p (j e) -> p j e", e=2)
                    for r, n in enumerate((4, 4, 2)):
                        dve.wait_ge(sem(s + "att"), h * 3 + r + 1)
                        for dst, bank, m in ((att_f, 6, mask_f), (att_b, 7, mask_b)):
                            src = ps[0:CHUNK, bank, 0:2 * n * CHUNK].rearrange("p (j e c) -> p j e c", e=2, c=CHUNK)
                            for e in range(2):
                                ins = dve.tensor_tensor(dst[64 * e:64 * e + 64, 4 * r:4 * r + n, 64 * e:64 * e + 64],
                                                        src[:, :, e, :], m[:].unsqueeze(1).broadcast_to([CHUNK, n, CHUNK]), ALU.mult)
                        ins.then_inc(sem(s + "att_out"), 1)
                        dve.wait_ge(sem(s + "u"), h * 3 + r + 1)
                        for e in range(2):
                            ins = dve.tensor_tensor(U2[:, 4 * r:4 * r + n, e, :],
                                                    ps[:, 3 + e, 0:n * P].rearrange("p (j c) -> p j c", c=P),
                                                    d2[:, 4 * r:4 * r + n, e].unsqueeze(2).broadcast_to([P, n, P]), ALU.mult)
                        ins.then_inc(sem(s + "u_out"), 1)
                    dve.wait_ge(sem(s + "u_out"), h * 3 + 4)
                    for m in range(NCH - 1):
                        if m:
                            dve.wait_ge(sem(s + "s_step"), (h * (NCH - 1) + m) * 2 - 1)
                        dve.scalar_tensor_tensor(S[0:64, order_f[m + 1], :], S[0:64, order_f[m], :], d_last[0:64, order_f[m]:order_f[m] + 1],
                                                 U[0:64, order_f[m], :], ALU.mult, ALU.add).then_inc(sem(s + "s_step"), 1)
                        if m:
                            dve.wait_ge(sem(s + "s_step"), (h * (NCH - 1) + m) * 2)
                        dve.scalar_tensor_tensor(S[64:P, order_b[m + 1], :], S[64:P, order_b[m], :], d_last[64:P, order_b[m]:order_b[m] + 1],
                                                 U[64:P, order_b[m], :], ALU.mult, ALU.add).then_inc(sem(s + "s_step"), 1)
                    dve.wait_ge(sem(s + "s_step"), (h + 1) * (NCH - 1) * 2)
                    dve.sem_inc(sem(s + "state"), 1)
                    dve.wait_ge(sem(s + "o_out"), h + 2)

        gate_t = [U[:].rearrange("p n c -> p (n c)")[:, 0:T], U[:].rearrange("p n c -> p (n c)")[:, T:2 * T],
                  S[:].rearrange("p n c -> p (n c)")[:, 0:T], S[:].rearrange("p n c -> p (n c)")[:, T:2 * T]]
        var_t = [eq[:], ek[:], qp[:], kp[:]]

        def fin_sp(sp, l):
            s = f"f{l}_"
            to = T if l == 0 else SEQ
            for h in range(HEADS):
                sp.dma_start(gate_t[h][:, 0:to], proj_fm[(G_OUT + h) * P:(G_OUT + h + 1) * P, 0:to]).then_inc(sem(s + "gate_in"), 16)
            for h in range(HEADS):
                sp.wait_ge(sem(s + "y"), h + 1)
                sp.dma_start(mix_fm[4 + h, :, 0:to], oT[:, h, 0:to]).then_inc(sem(s + "y_out"), 16)
            sp.wait_ge(sem(s + "y_out"), 16 * HEADS)

        def fin_act(act, l):
            s = f"f{l}_"
            to = T if l == 0 else SEQ
            for h in range(HEADS):
                if h >= 2:
                    act.wait_ge(sem(s + "ssq"), h - 1)
                act.activation(qd[:, h % 2, 0:to], oT[:, h, 0:to], ACT.Square).then_inc(sem(s + "sq"), 1)
            for h in range(HEADS):
                act.wait_ge(sem(s + "var"), h + 1)
                act.activation(var_t[h][:, 0:to], var_t[h][:, 0:to], ACT.Sqrt).then_inc(sem(s + "std"), 1)
            act.wait_ge(sem(s + "gate_in"), 16 * HEADS)
            for h in range(HEADS):
                act.activation(gate_t[h][:, 0:to], gate_t[h][:, 0:to], ACT.Silu).then_inc(sem(s + "gate"), 1)

        def fin_pe(pe, l):
            s = f"f{l}_"
            to = T if l == 0 else SEQ
            for h in range(HEADS):
                pe.wait_ge(sem(s + "sq"), h + 1)
                if h >= 2:
                    pe.wait_ge(sem(s + "var"), h - 1)
                for c, n in chunks(to):
                    at = 1536 * (h % 2) + c
                    mm = pe.matmul(flat[:, at:at + n], ones[:], qd[:, h % 2, c:c + n], start=True, stop=True)
                mm.then_inc(sem(s + "ssq"), 1)

        def fin_dve(dve, l):
            s = f"f{l}_"
            to = T if l == 0 else SEQ
            for h in range(HEADS):
                dve.wait_ge(sem(s + "ssq"), h + 1)
                at = 1536 * (h % 2)
                dve.tensor_scalar(var_t[h][:, 0:to], flat[:, at:at + to], 1.0 / P, EPS, ALU.mult, ALU.add).then_inc(sem(s + "var"), 1)
            for h in range(HEADS):
                dve.wait_ge(sem(s + "std"), h + 1)
                dve.reciprocal(var_t[h][:, 0:to], var_t[h][:, 0:to]).then_inc(sem(s + "fd"), 1)
                dve.wait_ge(sem(s + "fd"), 2 * h + 1)
                dve.tensor_tensor(oT[:, h, 0:to], oT[:, h, 0:to], var_t[h][:, 0:to], ALU.mult).then_inc(sem(s + "fd"), 1)
                dve.wait_ge(sem(s + "fd"), 2 * h + 2)
                dve.wait_ge(sem(s + "gate"), h + 1)
                dve.scalar_tensor_tensor(oT[:, h, 0:to], oT[:, h, 0:to], gla_gain[:, l:l + 1], gate_t[h][:, 0:to],
                                         ALU.mult, ALU.mult).then_inc(sem(s + "y"), 1)

        def wo_tn(l):
            return T if l == 0 else SEQ

        def wo_sp(sp, l):
            s = f"o{l}_"
            tn = wo_tn(l)
            tile_load(sp, s, 0, 0, io["w_out"][l], None)
            tile_load(sp, s, 1, 1, io["w_out"][l], None)
            for k in range(KT):
                if k >= 2:
                    sp.wait_ge(sem(s + "y_lo"), k - 1)
                sp.dma_start(stage[:, k % 2, 0:tn], mix_fm[k, :, 0:tn]).then_inc(sem(f"{s}y_in{k % 2}"), 16)
            with sp.Fori(0, 3) as i:
                for u in range(2):
                    tile_load(sp, s, i * 2 + u + 2, u, io["w_out"][l], i * 2 + u + 1)

        def wo_act(act, l):
            s = f"o{l}_"
            tn = wo_tn(l)
            for t in range(2):
                tile_split_act(act, s, t, t)
            for k in range(KT):
                act.wait_ge(sem(f"{s}y_in{k % 2}"), 16 * (k // 2 + 1))
                act.copy(h_hi[:, k, 0:tn], stage[:, k % 2, 0:tn]).then_inc(sem(s + "y_hi"), 1)
            with act.Fori(1, 4) as i:
                for u in range(2):
                    tile_split_act(act, s, i * 2 + u, u)

        def wo_pool(pool, l):
            s = f"o{l}_"
            tn = wo_tn(l)
            for t in range(2):
                tile_split_pool(pool, s, t, t)
            with pool.Fori(1, 4) as i:
                for u in range(2):
                    tile_split_pool(pool, s, i * 2 + u, u)

        def wo_pe(pe, l):
            s = f"o{l}_"
            pe.sem_inc(sem(s + "w_free"), 2)
            pe.wait_ge(sem(s + "y_lo"), KT)
            with pe.Fori(0, 4) as i:
                for u in range(2):
                    tile_pe(pe, s, i * 2 + u, u, wo_tn(l))

        def wo_dve(dve, l):
            s = f"o{l}_"
            tn = wo_tn(l)
            dve.sem_inc(sem(s + "evac"), 2)
            for k in range(KT):
                dve.wait_ge(sem(s + "y_hi"), k + 1)
                dve.tensor_tensor(h_lo[:, k, 0:tn], stage[:, k % 2, 0:tn], h_hi[:, k, 0:tn], ALU.subtract)\
                   .then_inc(sem(s + "y_lo"), 1)
            with dve.Fori(0, 4) as i:
                for u in range(2):
                    t = i * 2 + u
                    dve.wait_ge(sem(s + "w_free"), t + 3)
                    for c, n, g in segments(tn):
                        xs = x[:, bass.ts(t, 1), c:c + n].rearrange("p o n -> p (o n)")
                        ins = dve.scalar_tensor_tensor(xs, flat[:, u * 1536 + c:u * 1536 + c + n],
                                                       mod[:, bass.ds(t + l * 48 + 2 * KT, 1), g:g + 1].rearrange("p o n -> p (o n)"),
                                                       xs, ALU.mult, ALU.add)
                    ins.then_inc(sem(s + "evac"), 1)

        GATE, VALUE, DOWN = 0, 1, 2

        def ffn_downs(tn):
            return [(m, c, n) for c, n in chunks(tn) for m in range(KT)]

        def ffn_sp(sp, l):
            s = f"u{l}_"
            with sp.Fori(0, NFF) as i:
                for kind in range(3):
                    src = io["w_up"][l] if kind < 2 else io["w_down"][l]
                    at = i * 2 + kind if kind < 2 else i
                    sp.wait_ge(sem(f"{s}raw_free{kind}"), i + 1)
                    sp.dma_start(fw_raw[:, kind:kind + 1, :], src[bass.ts(at, 1)].rearrange("o p n -> p o n"))\
                      .then_inc(sem(f"{s}w_in{kind}"), 16)

        def ffn_loop(eng, tile):
            tile(0, 0, False, False)
            with eng.Fori(0, NFF // 2 - 1) as i:
                tile(i * 2 + 1, 1, True, False)
                tile(i * 2 + 2, 0, True, False)
            tile(NFF - 1, 1, True, True)

        def ffn_act(act, l):
            s = f"u{l}_"
            tn = wo_tn(l)

            def split(i, kind, slot):
                act.wait_ge(sem(f"{s}w_in{kind}"), i * 16 + 16)
                act.wait_ge(sem(f"{s}w_free{kind}"), i + 1)
                act.copy(fw_hi[:, slot, :], fw_raw[:, kind, :]).then_inc(sem(f"{s}w_hi{kind}"), 1)

            def tile(i, u, down, last):
                split(i, VALUE, 1)
                split(i, DOWN, 2 + u)
                for j, (c, n) in enumerate(chunks(tn)):
                    act.wait_ge(sem(f"{s}gate{j}"), i + 1)
                    act.wait_ge(sem(s + "conv_free"), i + 1) if j == 0 else None
                    at = c + 1 if c < SEQ else c + 3
                    act.copy(G[:, at:at + n], ps[:, j, 0:n]).then_inc(sem(s + "g_out"), 1)
                if not last:
                    split(i + 1, GATE, 0)
                act.wait_ge(sem(s + "conv"), i + 1)
                act.activation(cv[:, 1:tn + 3 if tn > SEQ else tn + 1], cv[:, 1:tn + 3 if tn > SEQ else tn + 1], ACT.Gelu,
                               bias=conv_b[:, l, bass.ds(i, 1)]).then_inc(sem(s + "gelu"), 1)
                for j, (c, n) in enumerate(chunks(tn)):
                    act.wait_ge(sem(f"{s}hid{j}"), i + 1)
                    act.wait_ge(sem(s + "hid_free"), i + 1) if j == 0 else None
                    at = c + 1 if c < SEQ else c + 3
                    act.copy(hid_hi[:, u, c:c + n], cv[:, at:at + n]).then_inc(sem(f"{s}hid_hi{j}"), 1)

            act.wait_ge(sem(s + "pads"), 1)
            split(0, GATE, 0)
            ffn_loop(act, tile)

        def ffn_pool(pool, l):
            s = f"u{l}_"
            tn = wo_tn(l)
            pool.memset(G[:], 0.0).then_inc(sem(s + "pads"), 1)
            pool.sem_inc(sem(s + "conv_free"), 1)
            for kind in range(3):
                pool.sem_inc(sem(f"{s}raw_free{kind}"), 1)

            def split(i, kind, slot):
                pool.wait_ge(sem(f"{s}w_hi{kind}"), i + 1)
                pool.tensor_tensor(fw_lo[:, slot, :], fw_raw[:, kind, :], fw_hi[:, slot, :], ALU.subtract)\
                    .then_inc(sem(f"{s}w_lo{kind}"), 1)
                pool.wait_ge(sem(f"{s}w_lo{kind}"), i + 1)
                pool.sem_inc(sem(f"{s}raw_free{kind}"), 1)

            def tile(i, u, down, last):
                split(i, VALUE, 1)
                split(i, DOWN, 2 + u)
                if not last:
                    split(i + 1, GATE, 0)
                for j, (c, n) in enumerate(chunks(tn)):
                    at = c + 1 if c < SEQ else c + 3
                    pool.wait_ge(sem(f"{s}hid_hi{j}"), i + 1)
                    pool.tensor_tensor(hid_lo[:, u, c:c + n], cv[:, at:at + n], hid_hi[:, u, c:c + n], ALU.subtract)\
                        .then_inc(sem(f"{s}hid_lo{j}"), 1)
                pool.wait_ge(sem(f"{s}hid_lo{len(chunks(tn)) - 1}"), i + 1)
                pool.sem_inc(sem(s + "conv_free"), 1)

            split(0, GATE, 0)
            ffn_loop(pool, tile)

        def ffn_pe(pe, l):
            s = f"u{l}_"
            tn = wo_tn(l)
            cs = chunks(tn)
            downs = ffn_downs(tn)
            nd = len(downs)
            pe.sem_inc(sem(f"{s}w_free0"), 1)
            pe.sem_inc(sem(f"{s}w_free1"), 1)
            pe.sem_inc(sem(f"{s}w_free2"), 2)
            pe.sem_inc(sem(s + "hid_free"), 2)

            def down(i, u, d):
                m, c, n = downs[d]
                if d == 0:
                    pe.wait_ge(sem(f"{s}w_lo{DOWN}"), i + 1)
                if m == 0:
                    pe.wait_ge(sem(f"{s}hid_lo{c // 512}"), i + 1)
                pe.wait_ge(sem(s + "down_out"), i * nd + d + 1)
                o = ps[:, 6 + d % 2, 0:n]
                wc = slice(m * P, (m + 1) * P)
                pe.matmul(o, fw_hi[:, 2 + u, wc], hid_hi[:, u, c:c + n], start=True, stop=False)
                pe.matmul(o, fw_hi[:, 2 + u, wc], hid_lo[:, u, c:c + n], start=False, stop=False)
                pe.matmul(o, fw_lo[:, 2 + u, wc], hid_hi[:, u, c:c + n], start=False, stop=True).then_inc(sem(s + "down"), 1)
                if d == nd - 1:
                    pe.wait_ge(sem(s + "down"), i * nd + nd)
                    pe.sem_inc(sem(f"{s}w_free2"), 1)
                    pe.sem_inc(sem(s + "hid_free"), 1)

            def tile(i, u, with_down, last):
                d = 0
                for kind in (GATE, VALUE):
                    pe.wait_ge(sem(f"{s}w_lo{kind}"), i + 1)
                    wh = fw_hi[:, kind, :].rearrange("p (k m) -> p k m", m=P)
                    wl = fw_lo[:, kind, :].rearrange("p (k m) -> p k m", m=P)
                    for j, (c, n) in enumerate(cs):
                        if kind == GATE:
                            if not isinstance(i, int) or i > 0:
                                pe.wait_ge(sem(s + "g_out"), i * len(cs) - len(cs) + j + 1)
                        elif not isinstance(i, int) or i > 0:
                            pe.wait_ge(sem(f"{s}hid{j}"), i)
                        o = ps[:, 3 * kind + j, 0:n]
                        for k in range(KT):
                            pe.matmul(o, wh[:, k], h_hi[:, k, c:c + n], start=(k == 0), stop=False)
                            pe.matmul(o, wh[:, k], h_lo[:, k, c:c + n], start=False, stop=False)
                            mm = pe.matmul(o, wl[:, k], h_hi[:, k, c:c + n], start=False, stop=(k == KT - 1))
                            if k == KT - 1:
                                mm.then_inc(sem(f"{s}gate{j}" if kind == GATE else f"{s}value{j}"), 1)
                            if k % 2 and with_down:
                                down(i - 1, 1 - u, d)
                                d += 1
                    pe.wait_ge(sem(f"{s}gate{len(cs) - 1}" if kind == GATE else f"{s}value{len(cs) - 1}"), i + 1)
                    pe.sem_inc(sem(f"{s}w_free{kind}"), 1)
            ffn_loop(pe, tile)
            for d in range(nd):
                down(NFF - 1, 1, d)

        def ffn_dve(dve, l):
            s = f"u{l}_"
            tn = wo_tn(l)
            cs = chunks(tn)
            downs = ffn_downs(tn)
            nd = len(downs)
            wide = tn + 2 if tn > SEQ else tn
            dve.sem_inc(sem(s + "down_out"), 2)

            def down(i, d):
                m, c, n = downs[d]
                g = int(c >= SEQ)
                dve.wait_ge(sem(s + "down"), i * nd + d + 1)
                at = l * 48 + 5 * KT + m
                dve.scalar_tensor_tensor(x[:, m, c:c + n], ps[:, 6 + d % 2, 0:n], mod[:, at, g:g + 1], x[:, m, c:c + n],
                                         ALU.mult, ALU.add).then_inc(sem(s + "down_out"), 1)

            def tile(i, u, with_down, last):
                todo = list(range(nd)) if with_down else []

                def some(k):
                    for _ in range(min(k, len(todo))):
                        down(i - 1, todo.pop(0))
                some(nd // 2)
                dve.wait_ge(sem(s + "g_out"), i * len(cs) + len(cs))
                dve.wait_ge(sem(s + "conv_free"), i + 1)
                for tap, src in ((1, 1), (0, 0), (2, 2)):
                    wt = conv_w[:, l, bass.ds(i, 1), tap:tap + 1].rearrange("p o n -> p (o n)")
                    if tap == 1:
                        ins = dve.tensor_scalar(cv[:, 1:1 + wide], G[:, src:src + wide], wt, None, ALU.mult)
                    else:
                        ins = dve.scalar_tensor_tensor(cv[:, 1:1 + wide], G[:, src:src + wide], wt, cv[:, 1:1 + wide],
                                                       ALU.mult, ALU.add)
                    if tap == 2:
                        ins.then_inc(sem(s + "conv"), 1)
                    else:
                        ins.then_inc(sem(s + "conv_step"), 1)
                        dve.wait_ge(sem(s + "conv_step"), i * 2 + 1 + (tap == 0))
                    some(1)
                some(1)
                for j, (c, n) in enumerate(cs):
                    at = c + 1 if c < SEQ else c + 3
                    dve.wait_ge(sem(f"{s}value{j}"), i + 1)
                    dve.wait_ge(sem(s + "gelu"), i + 1)
                    dve.tensor_tensor(cv[:, at:at + n], cv[:, at:at + n], ps[:, 3 + j, 0:n], ALU.mult)\
                       .then_inc(sem(f"{s}hid{j}"), 1)
                    some(4 if j < len(cs) - 1 else nd)
            ffn_loop(dve, tile)
            for d in range(nd):
                down(NFF - 1, d)

        def last_pe(pe):
            norm_pe(pe, "last_", SEQ)

        def last_act(act):
            norm_act_head(act, "last_", SEQ)

        def last_dve(dve):
            norm_dve_head(dve, "last_", SEQ)
            for k in range(KT):
                if k >= 2:
                    dve.wait_ge(sem(f"last_out{k % 2}"), 16 * (k // 2))
                dve.scalar_tensor_tensor(fo[:, k % 2, 0:SEQ], x[:, k, 0:SEQ], gains[:, 2 * DEPTH, k:k + 1], rstd[:, 0:SEQ],
                                         ALU.mult, ALU.mult).then_inc(sem("last_y"), 1)

        def last_sp(sp):
            for k in range(KT):
                sp.wait_ge(sem("last_y"), k + 1)
                sp.dma_start(out[k], fo[:, k % 2, 0:SEQ]).then_inc(sem(f"last_out{k % 2}"), 16)
            for u in range(2):
                sp.wait_ge(sem(f"last_out{u}"), 16 * KT // 2)

        @block.sync
        def _(sp):
            mod_sp(sp)
            end_phase(sp, "sp")
            for l in range(DEPTH):
                end_phase(sp, "sp", f"n{l}0")
                proj_sp(sp, l)
                end_phase(sp, "sp", f"p{l}")
                att_sp(sp, l, 0)
                end_phase(sp, "sp", f"a{l}0")
                gla_sp(sp, l)
                end_phase(sp, "sp", f"g{l}")
                fin_sp(sp, l)
                end_phase(sp, "sp", f"f{l}")
                att_sp(sp, l, 1)
                end_phase(sp, "sp", f"a{l}1")
                wo_sp(sp, l)
                end_phase(sp, "sp", f"o{l}")
                end_phase(sp, "sp", f"n{l}1")
                ffn_sp(sp, l)
                end_phase(sp, "sp", f"u{l}")
            last_sp(sp)


        @block.scalar
        def _(act):
            mod_act(act)
            end_phase(act, "act")
            for l in range(DEPTH):
                norm_act(act, l, 0)
                end_phase(act, "act", f"n{l}0")
                proj_act(act, l)
                end_phase(act, "act", f"p{l}")
                att_act(act, l, 0)
                end_phase(act, "act", f"a{l}0")
                gla_act(act, l)
                end_phase(act, "act", f"g{l}")
                fin_act(act, l)
                end_phase(act, "act", f"f{l}")
                att_act(act, l, 1)
                end_phase(act, "act", f"a{l}1")
                wo_act(act, l)
                end_phase(act, "act", f"o{l}")
                norm_act(act, l, 1)
                end_phase(act, "act", f"n{l}1")
                ffn_act(act, l)
                end_phase(act, "act", f"u{l}")
            last_act(act)


        @block.tensor
        def _(pe):
            mod_pe(pe)
            end_phase(pe, "pe")
            for l in range(DEPTH):
                norm_pe(pe, f"n{l}0_", T)
                end_phase(pe, "pe", f"n{l}0")
                proj_pe(pe, l)
                end_phase(pe, "pe", f"p{l}")
                att_pe(pe, l, 0)
                end_phase(pe, "pe", f"a{l}0")
                gla_pe(pe, l)
                end_phase(pe, "pe", f"g{l}")
                fin_pe(pe, l)
                end_phase(pe, "pe", f"f{l}")
                att_pe(pe, l, 1)
                end_phase(pe, "pe", f"a{l}1")
                wo_pe(pe, l)
                end_phase(pe, "pe", f"o{l}")
                norm_pe(pe, f"n{l}1_", wo_tn(l))
                end_phase(pe, "pe", f"n{l}1")
                ffn_pe(pe, l)
                end_phase(pe, "pe", f"u{l}")
            last_pe(pe)


        @block.vector
        def _(dve):
            mod_dve(dve)
            end_phase(dve, "dve")
            for l in range(DEPTH):
                norm_dve(dve, l, 0)
                end_phase(dve, "dve", f"n{l}0")
                proj_dve(dve, l)
                end_phase(dve, "dve", f"p{l}")
                att_dve(dve, l, 0)
                end_phase(dve, "dve", f"a{l}0")
                gla_dve(dve, l)
                end_phase(dve, "dve", f"g{l}")
                fin_dve(dve, l)
                end_phase(dve, "dve", f"f{l}")
                att_dve(dve, l, 1)
                end_phase(dve, "dve", f"a{l}1")
                wo_dve(dve, l)
                end_phase(dve, "dve", f"o{l}")
                norm_dve(dve, l, 1)
                end_phase(dve, "dve", f"n{l}1")
                ffn_dve(dve, l)
                end_phase(dve, "dve", f"u{l}")
            last_dve(dve)


        @block.gpsimd
        def _(pool):
            mod_pool(pool)
            end_phase(pool, "pool")
            for l in range(DEPTH):
                norm_pool(pool, l, 0)
                end_phase(pool, "pool", f"n{l}0")
                proj_pool(pool, l)
                end_phase(pool, "pool", f"p{l}")
                att_pool(pool, l, 0)
                end_phase(pool, "pool", f"a{l}0")
                gla_pool(pool, l)
                end_phase(pool, "pool", f"g{l}")
                end_phase(pool, "pool", f"f{l}")
                att_pool(pool, l, 1)
                end_phase(pool, "pool", f"a{l}1")
                wo_pool(pool, l)
                end_phase(pool, "pool", f"o{l}")
                norm_pool(pool, l, 1)
                end_phase(pool, "pool", f"n{l}1")
                ffn_pool(pool, l)
                end_phase(pool, "pool", f"u{l}")


def lay_out(inp):
    a = {k: np.asarray(v) for k, v in inp.items()}
    c = np.ascontiguousarray
    L = DEPTH
    io = {}
    io["xT"] = c(np.concatenate([a["x"][0], a["ctx"][0]], 0).T.reshape(KT, P, T).transpose(1, 0, 2))
    io["cc"] = c(np.stack([a["c"][0], a["c_ctx"]], -1).reshape(KT, P, 2).transpose(1, 0, 2))
    io["w_mod"] = c(a["w_mod"].reshape(L, KT, P, 12, 512).transpose(0, 3, 2, 1, 4).reshape(L * 12, P, KT, 512))
    io["b_mod"] = c(a["b_mod"].reshape(L * 48, P).T)
    g = np.stack([a[n][l] for l in range(L) for n in ("norm1_g", "norm2_g")] + [a["final_norm_g"]])
    io["gains"] = c(g.reshape(2 * L + 1, KT, P).transpose(2, 0, 1))
    w = a["w_in"]
    at, cut = 0, {}
    for name, n in (("na_q", 256), ("na_k", 256), ("na_v", 256), ("wa_q", 256), ("wa_k", 128), ("wa_v", 128),
                    ("g_q", 256), ("g_k", 256), ("g_v", 512), ("g_out", 512), ("lr", 32)):
        cut[name] = w[:, :, at:at + n]
        at += n
    pad = np.zeros((L, D, P - 32), w.dtype)
    fm = np.concatenate([cut["na_k"], cut["wa_k"], cut["g_k"], cut["lr"], pad, cut["na_q"], cut["wa_q"], cut["g_q"], cut["g_out"]], -1)
    io["w_fm"] = c(fm.reshape(L, KT, P, NFM, P).transpose(0, 3, 2, 1, 4).reshape(L, NFM, P, KT * P))
    tm = np.concatenate([cut["na_v"], cut["wa_v"], cut["g_v"]], -1)
    io["w_tm"] = c(tm.reshape(L, KT, P, 2, HALF).transpose(0, 3, 2, 1, 4))
    io["w_out"] = c(a["w_out"].reshape(L, KT, P, KT, P).transpose(0, 3, 2, 1, 4).reshape(L, KT, P, KT * P))
    up = a["ffn_w_up"].reshape(L, KT, P, 2, NFF, P)[:, :, :, ::-1]
    io["w_up"] = c(up.transpose(0, 4, 3, 2, 1, 5).reshape(L, NFF * 2, P, KT * P))
    io["w_down"] = c(a["ffn_w_down"].reshape(L, NFF, P, D))
    io["conv_w"] = c(a["ffn_conv_w"].reshape(L, 3, NFF, P).transpose(3, 0, 2, 1))
    io["conv_b"] = c(a["ffn_conv_b"].reshape(L, NFF, P).transpose(2, 0, 1))
    io["gla_gain"] = c(a["gla_norm_g"].T)
    gw = np.zeros((L, HEADS, 32, P), np.float32)
    gb = np.zeros((L, HEADS, P, 1), np.float32)
    for h in range(HEADS):
        for d in range(2):
            gw[:, h, 16 * d:16 * d + 16, 64 * d:64 * d + 64] = a["gla_gate_w"][:, d, :, 64 * h:64 * h + 64]
            gb[:, h, 64 * d:64 * d + 64, 0] = a["gla_gate_b"][:, d, 64 * h:64 * h + 64]
    io["gate_w"], io["gate_b"] = gw, gb
    sk = np.full((L, 2, HEADS), MASKED, np.float32)
    sk[:, 1] = a["wa_sink"]
    io["sinks"] = c(np.broadcast_to(sk[None], (P, L, 2, HEADS)))
    rpb = a["na_rpb"]
    nb = np.full((L, 8, P, HEADS, 10, 64), MASKED, np.float32)
    col = np.arange(64)
    cs = np.clip(col - 8, 0, 48)
    inside = (col[None, :] >= cs[:, None]) & (col[None, :] < cs[:, None] + 16)
    off = np.where(inside, col[None, :] - col[:, None] + 15, 0)
    for j in range(8):
        w0 = min(max(j - 2, 0), 3) * 2
        for e in range(2):
            r = 2 * j + e
            rs = min(max(r - 4, 0), 8)
            for kr in range(rs, rs + 8):
                v = rpb[:, :, kr - r + 7, :][:, :, off]
                nb[:, j, 64 * e:64 * e + 64, :, kr - w0, :] = np.where(inside, v, np.float32(MASKED)).transpose(0, 2, 1, 3)
    io["na_bias"] = nb.reshape(L, 8, P, HEADS * 640)
    wm = np.full((8, P, 384), MASKED, np.float32)
    for n in range(8):
        w0 = min(max(n - 1, 0), 5)
        q = n * P + np.arange(P)[:, None]
        k = w0 * P + np.arange(384)[None, :]
        wm[n][np.abs(q - k) <= 128] = 0.0
    io["wa_mask"] = wm
    t = np.arange(SEQ)
    inv = (np.float32(10000.0) ** (-np.arange(16, dtype=np.float32) / np.float32(16)))
    ang = np.concatenate([(t // 64).astype(np.float32)[:, None] * inv, (t % 64).astype(np.float32)[:, None] * inv], -1).T
    cos, sin = np.cos(ang).astype(np.float32), np.sin(ang).astype(np.float32)
    io["rope"] = c(np.stack([np.tile(cos, (4, 1)), np.tile(np.concatenate([-sin, sin]), (2, 1))]))
    sm = np.ones((P, T), np.float32)
    sm[0:64, 0::CHUNK] = 0
    sm[64:, CHUNK - 1::CHUNK] = 0
    io["smask"] = sm
    tri = np.tril(np.ones((CHUNK, CHUNK), np.float32))
    io["tri"] = c(np.stack([tri.T, tri]))
    return io


def kernel(**inputs):
    import concourse.bacc as bacc
    from concourse.bass_utils import run_bass_kernel_spmd
    arrays = lay_out(inputs)
    nc = bacc.Bacc("TRN2", target_bir_lowering=False, num_devices=1)
    io = {k: nc.dram_tensor(f"in_{k}", v.shape, F32, kind="ExternalInput").ap() for k, v in arrays.items()}
    out = nc.dram_tensor("out_0", (KT, P, SEQ), F32, kind="ExternalOutput").ap()
    build(nc, io, out)
    r = run_bass_kernel_spmd(nc, [{f"in_{k}": v for k, v in arrays.items()}], core_ids=[0])
    return r.results[0]["out_0"].reshape(KT * P, SEQ).T[None].copy()
```

```python
from contextlib import ExitStack

import numpy as np

import concourse.bass as bass
from concourse import mybir

F32 = mybir.dt.float32
F32R = mybir.dt.float32r
ALU = mybir.AluOpType
ACT = mybir.ActivationFunctionType
AX = mybir.AxisListType.X

P = 128
D = 1024
KT = D // P
DEPTH = 2
SEQ = 1024
CTX = 256
T = SEQ + CTX
NTOK = T // P
FF = 2816
NFF = FF // P
EPS = 1e-6
TAU = 16.0
HEADS = 4
CHUNK = 64
NCH = T // CHUNK
NCH_LAT = SEQ // CHUNK
NA_K, WA_K, G_K, LR, NA_Q, WA_Q, G_Q, G_OUT, NFM = 0, 2, 3, 5, 6, 8, 10, 12, 16
NA_V, WA_V, G_V, NTM = 0, 256, 384, 896
HALF = NTM // 2
MASKED = -1e30
CLAMP = 40.0 * TAU


def chunks(n):
    return [(c, min(512, n - c)) for c in range(0, n, 512)]


def segments(n):
    return [(0, SEQ, 0)] + ([(SEQ, CTX, 1)] if n > SEQ else [])


def build(nc, io, out):
    ctx = ExitStack()
    with ctx:
        def sb(name, shape, dt=F32):
            return ctx.enter_context(nc.sbuf_tensor(name, shape, dt))

        def shared(*specs):
            with ExitStack() as s:
                return [s.enter_context(nc.sbuf_tensor(n, shp, dt)) for n, shp, dt in specs]

        RUNS = [r for l in range(DEPTH)
                for r in (f"n{l}0", f"p{l}", f"a{l}0", f"g{l}", f"a{l}1", f"o{l}", f"n{l}1", f"u{l}")]
        sems = {}
        banks = ([], [])

        def sem(name):
            if name not in sems:
                run = name.split("_")[0]
                if run in RUNS:
                    bank = banks[RUNS.index(run) % 2]
                    used = sum(1 for k in sems if k.split("_")[0] == run)
                    if used == len(bank):
                        bank.append(ctx.enter_context(nc.semaphore(f"bank{RUNS.index(run) % 2}_{used}")))
                    sems[name] = bank[used]
                else:
                    sems[name] = ctx.enter_context(nc.semaphore(name))
            return sems[name]

        proj_fm = nc.dram_tensor("proj_fm", (NFM * P, T), F32, kind="Internal").ap()
        proj_tm = nc.dram_tensor("proj_tm", (NTOK, P, NTM), F32, kind="Internal").ap()
        mix_fm = nc.dram_tensor("mix_fm", (KT, P, T), F32, kind="Internal").ap()

        x = sb("x", [P, KT, T])
        mod = sb("mod", [P, DEPTH * 48, 2])
        bmod = sb("bmod", [P, DEPTH * 48])
        gains = sb("gains", [P, 2 * DEPTH + 1, KT])
        coef = sb("coef", [P, DEPTH * 2, KT, 2])
        silu_c = sb("silu_c", [P, KT, 2])
        ident = sb("ident", [P, P])
        ones = sb("ones", [P, P])
        sinks = sb("sinks", [P, DEPTH, 2, HEADS])
        gla_gain = sb("gla_gain", [P, DEPTH])
        conv_w = sb("conv_w", [P, DEPTH, NFF, 3])
        conv_b = sb("conv_b", [P, DEPTH, NFF])

        wm, rows = shared(("wm", [P, 3, KT, 512], F32), ("rows", [2, DEPTH * 48 * P], F32))
        dense = ctx.enter_context(ExitStack())
        h_hi = dense.enter_context(nc.sbuf_tensor("h_hi", [P, KT, T], F32R))
        h_lo = dense.enter_context(nc.sbuf_tensor("h_lo", [P, KT, T], F32R))
        (sq, rstd, nt, nfull, fo) = shared(
            ("sq", [P, 2, T], F32),
            ("rstd", [P, T], F32), ("nt", [P, 2, T], F32), ("nfull", [P, 2, T], F32), ("fo", [P, 2, T], F32))
        (w_raw, w_hi, w_lo, stage, w2_raw, w2_hi, w2_lo, stage2) = shared(
            ("w_raw", [P, 2, KT * P], F32),
            ("w_hi", [P, 2, KT * P], F32R), ("w_lo", [P, 2, KT * P], F32R), ("stage", [P, 2, T], F32),
            ("w2_raw", [P, KT, HALF], F32), ("w2_hi", [P, KT, HALF], F32R), ("w2_lo", [P, KT, HALF], F32R),
            ("stage2", [P, 2, HALF], F32))
        (fw_raw, fw_hi, fw_lo, hid_hi, hid_lo, G, cv) = shared(
            ("fw_raw", [P, 3, KT * P], F32),
            ("fw_hi", [P, 4, KT * P], F32R), ("fw_lo", [P, 4, KT * P], F32R),
            ("hid_hi", [P, 2, T], F32R), ("hid_lo", [P, 2, T], F32R), ("G", [P, T + 4], F32), ("cv", [P, T + 4], F32))
        dense.close()
        (k_raw, k_sw, k_hi, k_lo, v_att, bias_t, Pm, PT, q_blk, q_swb, qb, mx, nmax, sums, tot, rec, o_att, o_st,
         rope_c, rope_s) = shared(
            ("k_raw", [P, 2, T], F32), ("k_sw", [P, 2, SEQ], F32),
            ("k_hi", [P, HEADS, T], F32R), ("k_lo", [P, HEADS, T], F32R), ("v_att", [P, NTOK, 256], F32),
            ("bias_t", [P, 2, HEADS * 640], F32), ("Pm", [P, 2, 896], F32), ("PT", [P, 2, 896], F32),
            ("q_blk", [P, 2, HEADS, P], F32), ("q_swb", [P, 2, HEADS, P], F32),
            ("qb", [P, 2, HEADS, P], F32R), ("mx", [P, HEADS, 4], F32), ("nmax", [P, HEADS], F32),
            ("sums", [P, 2, HEADS, 3], F32), ("tot", [P, HEADS], F32), ("rec", [P, HEADS], F32),
            ("o_att", [P, 2, 256], F32), ("o_st", [P, 2, 2, P], F32),
            ("rope_c", [P, SEQ], F32), ("rope_s", [P, SEQ], F32))
        (qd, kd, v_g, gw, gb, b, eq, ek, qp, kp, qpp, kT, att_f, att_b, U, S, oT, mask_f,
         mask_b, smask, c_ref, b_last, dif, d_last, d_ref, d_lr, var, gate) = shared(
            ("qd", [P, 2, T], F32), ("kd", [P, 2, T], F32), ("v_g", [P, 2, NTOK, P], F32),
            ("gw", [32, HEADS, P], F32), ("gb", [P, HEADS, 1], F32), ("b", [P, T], F32),
            ("eq", [P, T], F32), ("ek", [P, T], F32), ("qp", [P, 2, T], F32), ("kp", [P, 2, T], F32),
            ("qpp", [P, 2, T], F32), ("kT", [P, 2, NTOK, P], F32), ("att_f", [P, NTOK, P], F32),
            ("att_b", [P, NTOK, P], F32), ("U", [P, NCH, P], F32), ("S", [P, NCH, P], F32),
            ("oT", [P, HEADS, T], F32), ("mask_f", [CHUNK, CHUNK], F32), ("mask_b", [CHUNK, CHUNK], F32),
            ("smask", [P, T], F32), ("c_ref", [P, NCH], F32), ("b_last", [P, NCH], F32),
            ("dif", [P, NCH], F32), ("d_last", [P, 2, NCH], F32), ("d_ref", [P, 2, NCH], F32), ("d_lr", [P, 2, NCH], F32),
            ("var", [P, T], F32), ("gate", [P, 2, T], F32))

        ps = ctx.enter_context(nc.psum_tensor("ps", [P, 8, 512], F32))
        flat = ps[:, :, :].rearrange("p b n -> p (b n)")

        phase_done = sem("phase_done")
        count = {}

        def end_phase(eng, name, run=None):
            count[name] = count.get(name, 0) + 5
            eng.drain().then_inc(phase_done, 1)
            eng.wait_ge(phase_done, count[name])
            eng.drain()
            if name == "pool" and run:
                for handle in banks[RUNS.index(run) % 2]:
                    eng.sem_clear(handle)

        block = ctx.enter_context(nc.Block())

        NU = DEPTH * 12

        def mod_sp(sp):
            for dst, src in ((x[:], io["xT"]), (silu_c[:], io["cc"]), (bmod[:], io["b_mod"]), (gains[:], io["gains"]),
                             (sinks[:], io["sinks"]), (gla_gain[:], io["gla_gain"]), (conv_w[:], io["conv_w"]),
                             (conv_b[:], io["conv_b"])):
                sp.dma_start(dst, src).then_inc(sem("small_in"), 16)
            with sp.Fori(0, NU // 3) as i:
                for u in range(3):
                    sp.wait_ge(sem("row_done"), i * 3 + u + 1)
                    sp.dma_start(wm[:, u:u + 1], io["w_mod"][bass.ts(i * 3 + u, 1)].rearrange("o p k n -> p o k n"))\
                      .then_inc(sem(f"wm_in{u}"), 16)

        def mod_act(act):
            act.sem_inc(sem("row_out"), 3)
            act.wait_ge(sem("small_in"), 16 * 8)
            act.activation(silu_c[:], silu_c[:], ACT.Silu).then_inc(sem("silu_ready"), 1)
            with act.Fori(0, NU // 3) as i:
                for u in range(3):
                    act.wait_ge(sem("row_done"), i * 3 + u + 4)
                    act.copy(rows[:, bass.ts(i * 3 + u, 512)], ps[0:2, u, :]).then_inc(sem("row_out"), 1)

        def mod_pe(pe):
            pe.sem_inc(sem("row_done"), 3)
            pe.wait_ge(sem("silu_ready"), 1)
            with pe.Fori(0, NU // 3) as i:
                for u in range(3):
                    pe.wait_ge(sem(f"wm_in{u}"), i * 16 + 16)
                    pe.wait_ge(sem("row_out"), i * 3 + u + 1)
                    for k in range(KT):
                        mm = pe.matmul(ps[0:2, u, :], silu_c[:, k, :], wm[:, u, k, :], start=(k == 0), stop=(k == KT - 1))
                    mm.then_inc(sem("row_done"), 1)
            pe.wait_ge(sem("row_out"), 3 + NU)
            pe.wait_ge(sem("consts"), 1)
            for t in range(DEPTH * 48):
                mm = pe.transpose(ps[:, 4, 2 * t:2 * t + 2], rows[:, t * P:(t + 1) * P], ident[0:2, 0:2])
            mm.then_inc(sem("mod_t"), 1)

        def mod_dve(dve):
            dve.wait_ge(sem("mod_t"), 1)
            dve.tensor_tensor(mod[:], ps[:, 4, 0:DEPTH * 96].rearrange("p (t s) -> p t s", s=2),
                              bmod[:].unsqueeze(2).broadcast_to([P, DEPTH * 48, 2]), ALU.add).then_inc(sem("mod_v"), 1)
            dve.wait_ge(sem("mod_v"), 1)
            for l in range(DEPTH):
                for w in range(2):
                    t0 = l * 48 + (3 * w + 1) * KT
                    dve.scalar_tensor_tensor(coef[:, 2 * l + w], mod[:, t0:t0 + KT, :], 1.0,
                                             gains[:, 2 * l + w, :].unsqueeze(2).broadcast_to([P, KT, 2]),
                                             ALU.add, ALU.mult)

        def mod_pool(pool):
            pool.memset(ident[:], 0.0).then_inc(sem("ident_0"), 1)
            pool.memset(ones[:], 1.0)
            pool.wait_ge(sem("ident_0"), 1)
            pool.affine_select(out=ident[:], in_=ident[:], compare_op=ALU.not_equal, fill=1.0, base=0,
                               pattern=[[-1, P]], channel_multiplier=1).then_inc(sem("consts"), 1)

        def norm_pe(pe, s, tn):
            for k in range(KT):
                pe.wait_ge(sem(s + "sq"), k + 1)
                for c, n in chunks(tn):
                    mm = pe.matmul(flat[:, c:c + n], ones[:], sq[:, k % 2, c:c + n], start=(k == 0), stop=(k == KT - 1))
                mm.then_inc(sem(s + "sq_used"), 1)

        def norm_act_head(act, s, tn):
            for k in range(KT):
                if k >= 2:
                    act.wait_ge(sem(s + "sq_used"), k - 1)
                act.activation(sq[:, k % 2, :tn], x[:, k, :tn], ACT.Square).then_inc(sem(s + "sq"), 1)
            act.wait_ge(sem(s + "var"), 1)
            act.activation(rstd[:, :tn], rstd[:, :tn], ACT.Sqrt).then_inc(sem(s + "std"), 1)

        def norm_dve_head(dve, s, tn):
            dve.wait_ge(sem(s + "sq_used"), KT)
            dve.tensor_scalar(rstd[:, :tn], flat[:, :tn], 1.0 / D, EPS, ALU.mult, ALU.add).then_inc(sem(s + "var"), 1)
            dve.wait_ge(sem(s + "std"), 1)
            dve.reciprocal(rstd[:, :tn], rstd[:, :tn]).then_inc(sem(s + "rstd"), 1)
            dve.wait_ge(sem(s + "rstd"), 1)

        def norm_act(act, l, w):
            s, tn = f"n{l}{w}_", T if (l == 0 or w == 0) else SEQ
            norm_act_head(act, s, tn)
            for k in range(KT):
                act.wait_ge(sem(s + "xn"), k + 1)
                if k >= 2:
                    act.wait_ge(sem(s + "lo"), k - 1)
                for c, n, g in segments(tn):
                    a = act.activation(nfull[:, k % 2, c:c + n], nt[:, k % 2, c:c + n], ACT.Identity,
                                       bias=mod[:, l * 48 + 3 * w * KT + k, g:g + 1], scale=coef[:, 2 * l + w, k, g:g + 1])
                a.then_inc(sem(s + "full"), 1)
                act.wait_ge(sem(s + "full"), k + 1)
                act.copy(h_hi[:, k, :tn], nfull[:, k % 2, :tn]).then_inc(sem(s + "hi"), 1)

        def norm_dve(dve, l, w):
            s, tn = f"n{l}{w}_", T if (l == 0 or w == 0) else SEQ
            norm_dve_head(dve, s, tn)
            for k in range(KT):
                if k >= 2:
                    dve.wait_ge(sem(s + "full"), k - 1)
                dve.tensor_tensor(nt[:, k % 2, :tn], x[:, k, :tn], rstd[:, :tn], ALU.mult).then_inc(sem(s + "xn"), 1)

        def norm_pool(pool, l, w):
            s, tn = f"n{l}{w}_", T if (l == 0 or w == 0) else SEQ
            for k in range(KT):
                pool.wait_ge(sem(s + "hi"), k + 1)
                pool.tensor_tensor(h_lo[:, k, :tn], nfull[:, k % 2, :tn], h_hi[:, k, :tn], ALU.subtract)\
                    .then_inc(sem(s + "lo"), 1)

        def tile_split_act(act, s, t, u):
            act.wait_ge(sem(f"{s}w_in{u}"), 8 * t + (16 if u == 0 else 8))
            act.wait_ge(sem(s + "w_free"), t + 1)
            act.copy(w_hi[:, u, :], w_raw[:, u, :]).then_inc(sem(s + "w_hi"), 1)

        def tile_split_pool(pool, s, t, u):
            pool.wait_ge(sem(s + "w_hi"), t + 1)
            pool.tensor_tensor(w_lo[:, u, :], w_raw[:, u, :], w_hi[:, u, :], ALU.subtract).then_inc(sem(s + "w_lo"), 1)

        def tile_load(sp, s, t, u, src, raw_free):
            if raw_free is not None:
                sp.wait_ge(sem(s + "w_lo"), raw_free)
            sp.dma_start(w_raw[:, u:u + 1, :], src[bass.ts(t, 1)].rearrange("o p n -> p o n"))\
              .then_inc(sem(f"{s}w_in{u}"), 16)

        def tile_pe(pe, s, t, u, tn):
            pe.wait_ge(sem(s + "w_lo"), t + 1)
            pe.wait_ge(sem(s + "evac"), t + 1)
            wh = w_hi[:, u, :].rearrange("p (k m) -> p k m", m=P)
            wl = w_lo[:, u, :].rearrange("p (k m) -> p k m", m=P)
            cs = chunks(tn)
            for c, n in cs:
                o = flat[:, u * 1536 + c:u * 1536 + c + n]
                for k in range(KT):
                    pe.matmul(o, wh[:, k], h_hi[:, k, c:c + n], start=(k == 0), stop=False)
                    pe.matmul(o, wh[:, k], h_lo[:, k, c:c + n], start=False, stop=False)
                    mm = pe.matmul(o, wl[:, k], h_hi[:, k, c:c + n], start=False, stop=(k == KT - 1))
            mm.then_inc(sem(s + "w_free"), 1)

        def proj_sp(sp, l):
            s = f"p{l}_"
            wfm = io["w_fm"][l]

            def store(t, u):
                sp.wait_ge(sem(s + "staged"), t + 1)
                sp.dma_start(proj_fm.rearrange("(t p) n -> t p n", p=P)[bass.ts(t, 1)].rearrange("o p n -> p o n"),
                             stage[:, u:u + 1, :]).then_inc(sem(f"{s}st_out{u}"), 16)

            def load_half(hf):
                if hf:
                    sp.wait_ge(sem(s + "w2_lo"), hf)
                sp.dma_start(w2_raw[:], io["w_tm"][l, hf]).then_inc(sem(s + "w2_in"), 16)

            def store_half(hf):
                for j in range(NTOK):
                    sp.wait_ge(sem(s + "staged2"), hf * NTOK + j + 1)
                    sp.dma_start(proj_tm[j, :, hf * HALF:(hf + 1) * HALF], stage2[:, j % 2, :])\
                      .then_inc(sem(f"{s}st2_out{j % 2}"), 16)

            tile_load(sp, s, 0, 0, wfm, None)
            tile_load(sp, s, 1, 1, wfm, None)
            load_half(0)
            with sp.Fori(0, 4) as i:
                for u in range(2):
                    tile_load(sp, s, i * 2 + u + 2, u, wfm, i * 2 + u + 1)
                    store(i * 2 + u, u)
            store_half(0)
            load_half(1)
            with sp.Fori(4, 7) as i:
                for u in range(2):
                    tile_load(sp, s, i * 2 + u + 2, u, wfm, i * 2 + u + 1)
                    store(i * 2 + u, u)
            for t in (NFM - 2, NFM - 1):
                store(t, t % 2)
            store_half(1)
            for u in range(2):
                sp.wait_ge(sem(f"{s}st_out{u}"), 16 * NFM // 2)
                sp.wait_ge(sem(f"{s}st2_out{u}"), 16 * NTOK)

        def proj_act(act, l):
            s = f"p{l}_"
            for half in range(2):
                with act.Fori(4 * half, 4 * half + 4) as i:
                    for u in range(2):
                        tile_split_act(act, s, i * 2 + u, u)
                act.wait_ge(sem(s + "w2_in"), 16 * (half + 1))
                if half:
                    act.wait_ge(sem(s + "w2_free"), 1)
                act.copy(w2_hi[:], w2_raw[:]).then_inc(sem(s + "w2_hi"), 1)

        def proj_pool(pool, l):
            s = f"p{l}_"
            for half in range(2):
                with pool.Fori(4 * half, 4 * half + 4) as i:
                    for u in range(2):
                        tile_split_pool(pool, s, i * 2 + u, u)
                pool.wait_ge(sem(s + "w2_hi"), half + 1)
                pool.tensor_tensor(w2_lo[:], w2_raw[:], w2_hi[:], ALU.subtract).then_inc(sem(s + "w2_lo"), 1)

        def proj_pe(pe, l):
            s = f"p{l}_"
            pe.sem_inc(sem(s + "w_free"), 2)
            for half in range(2):
                with pe.Fori(4 * half, 4 * half + 4) as i:
                    for u in range(2):
                        tile_pe(pe, s, i * 2 + u, u, T)
                pe.wait_ge(sem(s + "w2_lo"), half + 1)
                for j in range(NTOK):
                    pe.wait_ge(sem(s + "evac2"), half * NTOK + j + 1)
                    tok = slice(j * P, (j + 1) * P)
                    o = ps[:, 6 + j % 2, 0:HALF]
                    for k in range(KT):
                        pe.matmul(o, h_hi[:, k, tok], w2_hi[:, k, :], start=(k == 0), stop=False)
                        pe.matmul(o, h_lo[:, k, tok], w2_hi[:, k, :], start=False, stop=False)
                        mm = pe.matmul(o, h_hi[:, k, tok], w2_lo[:, k, :], start=False, stop=(k == KT - 1))
                    mm.then_inc(sem(s + "done2"), 1)
                pe.wait_ge(sem(s + "done2"), NTOK * (half + 1))
                pe.sem_inc(sem(s + "w2_free"), 1)

        def proj_dve(dve, l):
            s = f"p{l}_"
            dve.sem_inc(sem(s + "evac"), 2)
            dve.sem_inc(sem(s + "evac2"), 2)

            def tile(t, u, first):
                dve.wait_ge(sem(s + "w_free"), t + 3)
                if not first:
                    dve.wait_ge(sem(f"{s}st_out{u}"), 8 * t + (0 if u == 0 else -8))
                dve.tensor_copy(stage[:, u, :], flat[:, u * 1536:u * 1536 + T]).then_inc(sem(s + "staged"), 1)
                dve.wait_ge(sem(s + "staged"), t + 1)
                dve.sem_inc(sem(s + "evac"), 1)

            for half in range(2):
                if half == 0:
                    tile(0, 0, True)
                    tile(1, 1, True)
                with dve.Fori(4 * half + (half == 0), 4 * half + 4) as i:
                    for u in range(2):
                        tile(i * 2 + u, u, False)
                for j in range(NTOK):
                    n = half * NTOK + j
                    dve.wait_ge(sem(s + "done2"), n + 1)
                    if n >= 2:
                        dve.wait_ge(sem(f"{s}st2_out{j % 2}"), 16 * (n // 2))
                    dve.tensor_copy(stage2[:, j % 2, :], ps[:, 6 + j % 2, 0:HALF]).then_inc(sem(s + "staged2"), 1)
                    dve.wait_ge(sem(s + "staged2"), n + 1)
                    dve.sem_inc(sem(s + "evac2"), 1)

        KW = (5, 3)
        PIECES = ([(512, 256, 384), (0, 0, 256)], [(512, 0, 384)])
        KH = (4, 2)

        def att_name(l, kind):
            return f"a{l}{kind}_"

        def att_window(kind, n):
            last, off = (4, 5)[kind], 2 - kind
            return min(max(n - off, 0), last)

        def att_each(eng, l, kind, body):
            def geom(n):
                if n >= (10 if l == 0 else 8):
                    return None
                return (att_window(kind, n), True) if n < 8 else (0, False)
            for n in range(2):
                body(n, n, geom(n), geom(n + 1))
            with eng.Fori(1, 3) as i:
                for u in range(2):
                    n = i * 2 + u
                    body(n, u, (n - (2 - kind), True), (n + 1 - (2 - kind), True))
            for n in range(6, 10 if l == 0 else 8):
                body(n, n % 2, geom(n), geom(n + 1))

        def att_sp(sp, l, kind):
            s = att_name(l, kind)
            qbase, kbase = (NA_Q, WA_Q)[kind] * P, (NA_K, WA_K)[kind] * P
            nblk = 10 if l == 0 else 8

            def keys(h):
                if h >= 2:
                    sp.wait_ge(sem(s + "k_free"), h - 1)
                for dup in range(2):
                    sp.dma_start(k_raw[64 * dup:64 * dup + 64, h % 2, :], proj_fm[kbase + 64 * h:kbase + 64 * h + 64, :])\
                      .then_inc(sem(f"{s}k_in{h}"), 16)
                if kind == 1:
                    for dup in range(2):
                        for r in range(2):
                            src = kbase + 64 * h + 32 * (1 - r)
                            sp.dma_start(k_sw[64 * dup + 32 * r:64 * dup + 32 * r + 32, h, :], proj_fm[src:src + 32, 0:SEQ])\
                              .then_inc(sem(f"{s}k_in{h}"), 16)

            def queries(n, u, local):
                qsrc = proj_fm[qbase:qbase + 256, :].rearrange("(h r d) t -> r d h t", d=32, r=2)
                for dup in range(2):
                    sp.dma_start(q_blk[64 * dup:64 * dup + 64, u],
                                 proj_fm[qbase:qbase + 256, bass.ts(n, P)].rearrange("(h d) t -> d h t", d=64))\
                      .then_inc(sem(f"{s}q_in{u}"), 16)
                if kind == 1:
                    for dup in range(2):
                        for r in range(2):
                            sp.dma_start(q_swb[64 * dup + 32 * r:64 * dup + 32 * r + 32, u], qsrc[1 - r][:, :, bass.ts(n, P)])\
                              .then_inc(sem(f"{s}q_in{u}"), 16)

            def bias(n, u):
                if kind == 0:
                    sp.dma_start(bias_t[:, u:u + 1, :], io["na_bias"][l, bass.ts(n, 1)].rearrange("o p n -> p o n"))\
                      .then_inc(sem(f"{s}bias_in{u}"), 16)
                else:
                    sp.dma_start(bias_t[:, u:u + 1, 0:384], io["wa_mask"][bass.ts(n, 1)].rearrange("o p n -> p o n"))\
                      .then_inc(sem(f"{s}bias_in{u}"), 16)

            def store(n, u):
                sp.wait_ge(sem(s + "o_staged"), n + 1)
                sp.dma_start(mix_fm[2 * kind:2 * kind + 2, :, bass.ts(n, P)].rearrange("o p t -> p o t"), o_st[:, u])\
                  .then_inc(sem(f"{s}o_out{u}"), 16)

            def step(n, u, more_q, more_bias):
                if more_q:
                    sp.wait_ge(sem(s + "q_split"), n + 1)
                    queries(n + 2, u, True)
                if more_bias:
                    sp.wait_ge(sem(s + "max"), n * HEADS + HEADS)
                    bias(n + 2, u)
                store(n, u)

            keys(0)
            if kind == 1:
                sp.dma_start(rope_c[:], io["rope"][0]).then_inc(sem(s + "rope_in"), 16)
                sp.dma_start(rope_s[:], io["rope"][1]).then_inc(sem(s + "rope_in"), 16)
            queries(0, 0, True)
            bias(0, 0)
            vc, vn = ((NA_V, 256), (WA_V, 128))[kind]
            sp.dma_start(v_att[:, :, 0:vn], proj_tm[:, :, vc:vc + vn].rearrange("j p c -> p j c")).then_inc(sem(s + "v_in"), 16)
            keys(1)
            queries(1, 1, True)
            bias(1, 1)
            for h in range(2, KH[kind]):
                keys(h)
            with sp.Fori(0, 3) as i:
                for u in range(2):
                    step(i * 2 + u, u, True, True)
            for n in range(6, nblk):
                step(n, n % 2, n + 2 < nblk, False)
            for u in range(2):
                sp.wait_ge(sem(f"{s}o_out{u}"), 16 * nblk // 2)

        def att_act(act, l, kind):
            s = att_name(l, kind)
            if kind == 1:
                act.wait_ge(sem("small_in"), 16 * 8)
                act.copy(mx[:, :, 3], sinks[:, l, kind, :]).then_inc(sem(s + "sink"), 1)
                act.wait_ge(sem(s + "sink"), 1)
            for h in range(KH[kind]):
                if kind == 0:
                    act.wait_ge(sem(f"{s}k_in{h}"), 32)
                else:
                    act.wait_ge(sem(s + "k_rot"), h + 1)
                act.mul(k_hi[:, h, :], k_raw[:, h % 2, :], 0.125).then_inc(sem(s + "k_hi"), 1)

            def exps(n, u, h, nl):
                p = h % 2
                act.wait_ge(sem(s + "max"), n * HEADS + h + 1)
                if nl:
                    act.activation(Pm[:, p, 0:nl], Pm[:, p, 0:nl], ACT.Exp, bias=nmax[:, h:h + 1],
                                   accum_out=sums[:, u, h, 0:1])
                a = act.activation(Pm[:, p, nl:nl + CTX], ps[:, 2 * p, 256:512], ACT.Exp, bias=nmax[:, h:h + 1],
                                   accum_out=sums[:, u, h, 1:2])
                if kind == 1:
                    a = act.activation(sums[:, u, h, 2:3], mx[:, h, 3:4], ACT.Exp, bias=nmax[:, h:h + 1])
                a.then_inc(sem(s + "p_ready"), 1)

            def out_block(n, u):
                act.wait_ge(sem(s + "o_turned"), n + 1)
                if not isinstance(n, int) or n >= 2:
                    act.wait_ge(sem(f"{s}o_out{u}"), 8 * n - 8 * u)
                act.copy(o_st[:, u], ps[:, 7, 0:256].rearrange("p (o t) -> p o t", o=2)).then_inc(sem(s + "o_staged"), 1)

            def body(n, u, here, nxt):
                nl = KW[kind] * P if here[1] else 0
                for h in range(HEADS):
                    act.wait_ge(sem(s + "turned"), n * HEADS + h + 1)
                    act.copy(PT[:, h % 2, 0:min(512, nl + CTX)], ps[:, 4, 0:min(512, nl + CTX)]).then_inc(sem(s + "pt_a"), 1)
                    if h + 2 < HEADS:
                        exps(n, u, h + 2, nl)
                    elif nxt:
                        exps(n + 1, 1 - u, h - 2, KW[kind] * P if nxt[1] else 0)
                    if h == 1 and not (isinstance(n, int) and n == 0):
                        out_block(n - 1, 1 - u)

            for h in range(2):
                exps(0, 0, h, KW[kind] * P)
            att_each(act, l, kind, body)
            nb = 10 if l == 0 else 8
            out_block(nb - 1, 1)

        def att_dve(dve, l, kind):
            s = att_name(l, kind)
            for h in range(KH[kind]):
                if kind == 1:
                    dve.wait_ge(sem(s + "rope_in"), 32)
                    dve.wait_ge(sem(f"{s}k_in{h}"), 96)
                    k = k_raw[:, h, 0:SEQ]
                    dve.tensor_tensor(k, k, rope_c[:], ALU.mult).then_inc(sem(s + "k_step"), 1)
                    dve.tensor_tensor(k_sw[:, h], k_sw[:, h], rope_s[:], ALU.mult).then_inc(sem(s + "k_step"), 1)
                    dve.wait_ge(sem(s + "k_step"), 2 * h + 2)
                    dve.tensor_tensor(k, k, k_sw[:, h], ALU.add).then_inc(sem(s + "k_rot"), 1)
                dve.wait_ge(sem(s + "k_hi"), h + 1)
                if kind == 1:
                    dve.wait_ge(sem(s + "k_rot"), h + 1)
                dve.scalar_tensor_tensor(k_lo[:, h], k_raw[:, h % 2], 0.125, k_hi[:, h], ALU.mult, ALU.subtract)\
                   .then_inc(sem(s + "k_lo"), 1)
                if h < KH[kind] - 2:
                    dve.wait_ge(sem(s + "k_lo"), h + 1)
                    dve.sem_inc(sem(s + "k_free"), 1)

            def maxes(n, u, h, nl):
                p = h % 2
                unit = n * HEADS + h
                if nl and h == 0:
                    dve.wait_ge(sem(f"{s}bias_in{u}"), 8 * n + (16 if u == 0 else 8))
                dve.wait_ge(sem(s + "s_done"), unit + 1)
                if not isinstance(n, int) or unit >= 2:
                    dve.wait_ge(sem(s + "turned"), unit - 1)
                dve.tensor_reduce(mx[:, h, 2:3], ps[:, 2 * p, 256:512], AX, ALU.max).then_inc(sem(s + "mx"), 1)
                k = 0
                if nl:
                    for col, off, cnt in PIECES[kind]:
                        bo = h * 640 + off if kind == 0 else off
                        dve.tensor_tensor_reduce(Pm[:, p, off:off + cnt], flat[:, 1024 * p + col:1024 * p + col + cnt],
                                                 bias_t[:, u, bo:bo + cnt], 1.0, MASKED, ALU.add, ALU.max,
                                                 mx[:, h, 1 - k:2 - k]).then_inc(sem(s + "mx"), 1)
                        k += 1
                for _ in range(2 - k):
                    dve.sem_inc(sem(s + "mx"), 1)
                dve.wait_ge(sem(s + "mx"), unit * 3 + 3)
                dve.tensor_reduce(nmax[:, h:h + 1], mx[:, h, 2 - k:3 + kind], AX, ALU.max, negate=True).then_inc(sem(s + "max"), 1)

            def body(n, u, here, nxt):
                nl = KW[kind] * P if here[1] else 0
                for h in range(HEADS):
                    if nl + CTX > 512:
                        dve.wait_ge(sem(s + "turned"), n * HEADS + h + 1)
                        dve.tensor_copy(PT[:, h % 2, 512:nl + CTX], ps[:, 5, 0:nl + CTX - 512]).then_inc(sem(s + "pt_b"), 1)
                    else:
                        dve.sem_inc(sem(s + "pt_b"), 1)
                    if h + 2 < HEADS:
                        maxes(n, u, h + 2, nl)
                    elif nxt:
                        maxes(n + 1, 1 - u, h - 2, KW[kind] * P if nxt[1] else 0)
                dve.wait_ge(sem(s + "p_ready"), n * HEADS + HEADS)
                dve.tensor_reduce(tot[:], sums[:, u, :, 0 if here[1] else 1:2 + kind], AX, ALU.add).then_inc(sem(s + "tot"), 1)
                dve.wait_ge(sem(s + "tot"), n + 1)
                dve.reciprocal(rec[:], tot[:]).then_inc(sem(s + "rec"), 1)
                dve.wait_ge(sem(s + "rec"), n + 1)
                dve.wait_ge(sem(s + "o_done"), n + 1)
                dve.tensor_tensor(o_att[:, u, :].rearrange("p (h d) -> p h d", h=HEADS),
                                  ps[:, 6, 256 * u:256 * u + 256].rearrange("p (h d) -> p h d", h=HEADS),
                                  rec[:].unsqueeze(2).broadcast_to([P, HEADS, 64]), ALU.mult).then_inc(sem(s + "o_norm"), 1)

            for h in range(2):
                maxes(0, 0, h, KW[kind] * P)
            att_each(dve, l, kind, body)

        def att_pool(pool, l, kind):
            s = att_name(l, kind)
            steps = 3 + 3 * kind
            nin = 16 * (2 + 4 * kind)
            if kind == 1:
                pool.wait_ge(sem(s + "rope_in"), 32)

            def body(n, u, here, nxt):
                st = [0]

                def chain(ins=None):
                    st[0] += 1
                    if ins is None:
                        pool.sem_inc(sem(s + "q_step"), 1)
                    else:
                        ins.then_inc(sem(s + "q_step"), 1)
                        pool.wait_ge(sem(s + "q_step"), n * steps + st[0])
                q, qsw = q_blk[:, u], q_swb[:, u]
                pool.wait_ge(sem(f"{s}q_in{u}"), (n - u) * (nin // 2) + nin)
                if kind == 1:
                    if here[1]:
                        cols = bass.ts(n, P)
                        chain(pool.tensor_tensor(q, q, rope_c[:, cols].unsqueeze(1).broadcast_to([P, HEADS, P]), ALU.mult))
                        chain(pool.tensor_tensor(qsw, qsw, rope_s[:, cols].unsqueeze(1).broadcast_to([P, HEADS, P]), ALU.mult))
                        chain(pool.tensor_tensor(q, q, qsw, ALU.add))
                    else:
                        for _ in range(3):
                            chain()
                if not isinstance(n, int) or n >= 2:
                    pool.wait_ge(sem(s + "s_done"), n * HEADS - HEADS)
                chain()
                chain(pool.tensor_copy(qb[:, u], q))
                chain(pool.tensor_tensor(qb[64:P, u], q[64:P], qb[64:P, u], ALU.subtract))
                assert st[0] == steps
                pool.sem_inc(sem(s + "q_split"), 1)
            att_each(pool, l, kind, body)

        def att_pe(pe, l, kind):
            s = att_name(l, kind)
            gqa = HEADS // KH[kind]

            def scores(n, u, h, geom):
                p = h % 2
                w0, local = geom
                kh = h // gqa
                if isinstance(n, int) and n == 0:
                    pe.wait_ge(sem(s + "k_lo"), kh + 1)
                if h == 0:
                    pe.wait_ge(sem(s + "q_split"), n + 1)
                lhs = qb[:, u, h, :]
                pieces = [(256, SEQ, 256)]
                if local:
                    pieces += [(col, w0 * P + off, cnt) for col, off, cnt in PIECES[kind]]
                for col, k0, cnt in pieces:
                    o = flat[:, 1024 * p + col:1024 * p + col + cnt]
                    pe.matmul(o, lhs, k_hi[:, kh, bass.ds(k0, cnt)], start=True, stop=False)
                    mm = pe.matmul(o, lhs, k_lo[:, kh, bass.ds(k0, cnt)], start=False, stop=True)
                mm.then_inc(sem(s + "s_done"), 1)

            def turn(n, h, nl):
                unit = n * HEADS + h
                pe.wait_ge(sem(s + "p_ready"), unit + 1)
                if not isinstance(n, int) or unit > 0:
                    pe.wait_ge(sem(s + "pt_a"), unit)
                    pe.wait_ge(sem(s + "pt_b"), unit)
                for t in range(nl // P + 2):
                    mm = pe.transpose(ps[:, 4 + t // 4, (t % 4) * P:(t % 4 + 1) * P], Pm[:, h % 2, t * P:(t + 1) * P], ident[:])
                mm.then_inc(sem(s + "turned"), 1)

            def weigh(n, u, h, geom):
                unit = n * HEADS + h
                w0, local = geom
                nl = KW[kind] * P if local else 0
                pe.wait_ge(sem(s + "pt_a"), unit + 1)
                if h == 0:
                    pe.wait_ge(sem(s + "v_in"), 16)
                    if not isinstance(n, int) or n >= 2:
                        pe.wait_ge(sem(s + "o_norm"), n - 1)
                pe.wait_ge(sem(s + "pt_b"), unit + 1)
                vc = (h // gqa) * 64
                at = 256 * u + h * 64
                ntile = nl // P + 2
                for t in range(ntile):
                    kt = (w0 + t) if t < nl // P else SEQ // P + t - nl // P
                    mm = pe.matmul(ps[:, 6, at:at + 64], PT[:, h % 2, t * P:(t + 1) * P],
                                   v_att[:, bass.ds(kt, 1), vc:vc + 64].rearrange("p o d -> p (o d)"),
                                   start=(t == 0), stop=(t == ntile - 1))
                if h == HEADS - 1:
                    mm.then_inc(sem(s + "o_done"), 1)

            def turn_out(n, u):
                pe.wait_ge(sem(s + "o_norm"), n + 1)
                if not isinstance(n, int) or n > 0:
                    pe.wait_ge(sem(s + "o_staged"), n)
                for g in range(2):
                    mm = pe.transpose(ps[:, 7, g * P:(g + 1) * P], o_att[:, u, g * P:(g + 1) * P], ident[:])
                mm.then_inc(sem(s + "o_turned"), 1)

            def body(n, u, here, nxt):
                nl = KW[kind] * P if here[1] else 0
                for h in range(HEADS):
                    turn(n, h, nl)
                    if h + 2 < HEADS:
                        scores(n, u, h + 2, here)
                    elif nxt:
                        scores(n + 1, 1 - u, h - 2, nxt)
                    if h:
                        weigh(n, u, h - 1, here)
                    elif not (isinstance(n, int) and n == 0):
                        turn_out(n - 1, 1 - u)
                weigh(n, u, HEADS - 1, here)

            for h in range(2):
                scores(0, 0, h, (att_window(kind, 0), True))
            att_each(pe, l, kind, body)
            turn_out((10 if l == 0 else 8) - 1, 1)

        lr = U[0:32].rearrange("p n c -> p (n c)")[:, 0:T]
        logs = [kp[:, 0], kp[:, 1], qp[:, 0], qp[:, 1]]
        ROUNDS = (4, 4, 2)

        def gla_sp(sp, l):
            s = f"g{l}_"
            to = T if l == 0 else SEQ
            sp.dma_start(lr, proj_fm[LR * P:LR * P + 32, :]).then_inc(sem(s + "lr_in"), 16)
            sp.dma_start(gw[:], io["gate_w"][l].rearrange("h r c -> r h c")).then_inc(sem(s + "lr_in"), 16)
            sp.dma_start(gb[:], io["gate_b"][l]).then_inc(sem(s + "lr_in"), 16)
            sp.dma_start(smask[:], io["smask"]).then_inc(sem(s + "mask_in"), 16)
            sp.dma_start(mask_f[:], io["tri"][0]).then_inc(sem(s + "mask_in"), 16)
            sp.dma_start(mask_b[:], io["tri"][1]).then_inc(sem(s + "mask_in"), 16)

            def head(h):
                u = h % 2
                if h >= 2:
                    sp.wait_ge(sem(s + "qpp"), h - 1)
                    sp.wait_ge(sem(s + "kp"), h - 1)
                for dup in range(2):
                    half = slice(64 * dup, 64 * dup + 64)
                    for dst, base in ((kd, G_K), (qd, G_Q)):
                        sp.dma_start(dst[half, u, :], proj_fm[h * 64 + base * P:h * 64 + base * P + 64, :])\
                          .then_inc(sem(s + "qk_in"), 16)
                if h >= 2:
                    sp.wait_ge(sem(s + "o"), h - 1)
                sp.dma_start(v_g[:, u], proj_tm[:, :, h * P + G_V:h * P + G_V + P].rearrange("j p c -> p j c")).then_inc(sem(s + "v_in"), 16)
                if h >= 2:
                    sp.wait_ge(sem(s + "y"), h - 1)
                    sp.dma_start(mix_fm[4 + h - 2, :, 0:to], oT[:, h - 2, 0:to]).then_inc(sem(s + "y_out"), 16)
                sp.dma_start(gate[:, u, 0:to], proj_fm[(G_OUT + h) * P:(G_OUT + h + 1) * P, 0:to]).then_inc(sem(s + "gate_in"), 16)
                sp.wait_ge(sem(s + "qk_in"), 64 * (h + 1))
                sp.wait_ge(sem(s + "v_in"), 16 * (h + 1))
                sp.wait_ge(sem(s + "gate_in"), 16 * (h + 1))
            for h in range(HEADS):
                head(h)
            for h in range(HEADS - 2, HEADS):
                sp.wait_ge(sem(s + "y"), h + 1)
                sp.dma_start(mix_fm[4 + h, :, 0:to], oT[:, h, 0:to]).then_inc(sem(s + "y_out"), 16)
            sp.wait_ge(sem(s + "y_out"), 16 * HEADS)

        def gla_act(act, l):
            s = f"g{l}_"
            to = T if l == 0 else SEQ
            act.wait_ge(sem(s + "lr_in"), 48)
            for h in range(HEADS):
                act.wait_ge(sem(s + "logit"), h + 1)
                at = 1536 * (h % 2)
                act.activation(logs[h], flat[:, at:at + T], ACT.Abs, bias=gb[:, h, :]).then_inc(sem(s + "abs"), 1)
            for h in range(HEADS):
                act.wait_ge(sem(s + "abs"), h + 1)
                act.activation(logs[h], logs[h], ACT.Exp, scale=-1.0).then_inc(sem(s + "exp"), 1)
            for h in range(HEADS):
                act.wait_ge(sem(s + "exp"), h + 1)
                act.activation(logs[h], logs[h], ACT.Ln, bias=1.0).then_inc(sem(s + "log"), 1)

            def scale(h):
                u = h % 2
                act.wait_ge(sem(s + "x"), h + 1)
                if h >= 1:
                    act.wait_ge(sem(s + "kp"), h)
                    act.wait_ge(sem(s + "qp"), h)
                act.activation(ek[:], b[:], ACT.Exp, scale=-1.0 / TAU).then_inc(sem(s + "ek"), 1)
                act.activation(eq[:], b[:], ACT.Exp, scale=1.0 / TAU).then_inc(sem(s + "eq"), 1)
                act.activation(d_ref[:, u], c_ref[:], ACT.Exp, scale=1.0 / TAU)
                act.activation(d_last[:, u], b_last[:], ACT.Exp, scale=1.0 / TAU)
                act.activation(d_lr[:, u], dif[:], ACT.Exp, scale=1.0 / TAU).then_inc(sem(s + "decay"), 1)

            def turned(h):
                for r, n in enumerate(ROUNDS):
                    act.wait_ge(sem(s + "kt"), h * 3 + r + 1)
                    act.copy(kT[:, h % 2, 4 * r:4 * r + n, :], ps[:, 5, 0:n * P].rearrange("p (j c) -> p j c", c=P))\
                       .then_inc(sem(s + "kt_out"), 1)

            def square(h):
                act.wait_ge(sem(s + "o_out"), h + 1)
                if h:
                    act.wait_ge(sem(s + "y_step"), 2 * h)
                act.activation(var[:, 0:to], oT[:, h, 0:to], ACT.Square).then_inc(sem(s + "sq"), 1)

            def silu(h):
                act.wait_ge(sem(s + "gate_in"), 16 * (h + 1))
                act.activation(gate[:, h % 2, 0:to], gate[:, h % 2, 0:to], ACT.Silu).then_inc(sem(s + "gate"), 1)

            def root(h):
                act.wait_ge(sem(s + "var"), h + 1)
                act.activation(var[:, 0:to], var[:, 0:to], ACT.Sqrt).then_inc(sem(s + "std"), 1)

            scale(0)
            turned(0)
            for h in range(HEADS):
                if h:
                    square(h - 1)
                    silu(h - 1)
                    root(h - 1)
                if h + 1 < HEADS:
                    scale(h + 1)
                    turned(h + 1)
                act.wait_ge(sem(s + "o"), h + 1)
                act.mul(oT[:, h, 0:to], flat[:, 0:to], 0.125).then_inc(sem(s + "o_out"), 1)
            square(HEADS - 1)
            silu(HEADS - 1)
            root(HEADS - 1)

        def gla_pe(pe, l):
            s = f"g{l}_"
            to = T if l == 0 else SEQ
            no = to // P
            pe.wait_ge(sem(s + "lr_in"), 48)
            for h in range(HEADS):
                if h >= 2:
                    pe.wait_ge(sem(s + "abs"), h - 1)
                    pe.wait_ge(sem(s + "min"), h - 1)
                at = 1536 * (h % 2)
                for c, n in chunks(T):
                    mm = pe.matmul(flat[:, at + c:at + c + n], gw[:, h, :], lr[:, c:c + n], start=True, stop=True)
                mm.then_inc(sem(s + "logit"), 1)

            def turn(h):
                pe.wait_ge(sem(s + "kp"), h + 1)
                for r, n in enumerate(ROUNDS):
                    if 3 * h + r:
                        pe.wait_ge(sem(s + "kt_out"), h * 3 + r)
                    for j in range(n):
                        t = 4 * r + j
                        mm = pe.transpose(ps[:, 5, j * P:(j + 1) * P], kp[:, h % 2, t * P:(t + 1) * P], ident[:])
                    mm.then_inc(sem(s + "kt"), 1)

            pe.wait_ge(sem(s + "abs"), HEADS)
            pe.wait_ge(sem(s + "min"), HEADS)
            turn(0)
            for h in range(HEADS):
                u = h % 2
                pe.wait_ge(sem(s + "v_in"), 16 * (h + 1))
                pe.wait_ge(sem(s + "qp"), h + 1)
                for r, n in enumerate(ROUNDS):
                    if 3 * h + r:
                        pe.wait_ge(sem(s + "att_out"), h * 3 + r)
                    for j in range(2 * n):
                        ch = 8 * r + j
                        cols = slice(ch * CHUNK, (ch + 1) * CHUNK)
                        pe.matmul(ps[0:CHUNK, 6, j * CHUNK:(j + 1) * CHUNK], kp[0:64, u, cols], qp[0:64, u, cols], start=True, stop=True)
                        mm = pe.matmul(ps[0:CHUNK, 7, j * CHUNK:(j + 1) * CHUNK], kp[64:P, u, cols], qp[64:P, u, cols], start=True, stop=True)
                    mm.then_inc(sem(s + "att"), 1)
                    pe.wait_ge(sem(s + "kt_out"), h * 3 + r + 1)
                    if 3 * h + r:
                        pe.wait_ge(sem(s + "u_out"), h * 3 + r)
                    for j in range(n):
                        t = 4 * r + j
                        pe.matmul(ps[:, 3, j * P:(j + 1) * P], kT[0:64, u, t, :], v_g[0:64, u, t, :], start=True, stop=True)
                        mm = pe.matmul(ps[:, 4, j * P:(j + 1) * P], kT[64:P, u, t, :], v_g[64:P, u, t, :], start=True, stop=True)
                    mm.then_inc(sem(s + "u"), 1)
                    if r == 0 and h:
                        squares(pe, s, h - 1, to)
                if h + 1 < HEADS:
                    turn(h + 1)
                if h:
                    pe.wait_ge(sem(s + "var"), h)
                pe.wait_ge(sem(s + "att_out"), h * 3 + 3)
                pe.wait_ge(sem(s + "state_f"), (h + 1) * (NCH - 1))
                pe.wait_ge(sem(s + "state_b"), (h + 1) * (NCH - 1))
                pe.wait_ge(sem(s + "qpp"), h + 1)
                for t in range(no):
                    o = flat[:, t * P:(t + 1) * P]
                    pe.matmul(o, v_g[:, u, t, :], att_f[:, t, :], start=True, stop=False)
                    pe.matmul(o, v_g[:, u, t, :], att_b[:, t, :], start=False, stop=False)
                    for e in range(2):
                        ch = 2 * t + e
                        mm = pe.matmul(flat[:, ch * CHUNK:(ch + 1) * CHUNK], S[:, ch, :],
                                       qpp[:, u, ch * CHUNK:(ch + 1) * CHUNK], start=False, stop=(e == 1))
                mm.then_inc(sem(s + "o"), 1)
            squares(pe, s, HEADS - 1, to)

        def squares(pe, s, h, to):
            pe.wait_ge(sem(s + "o_out"), h + 1)
            pe.wait_ge(sem(s + "sq"), h + 1)
            for c, n in chunks(to):
                mm = pe.matmul(flat[:, c:c + n], ones[:], var[:, c:c + n], start=True, stop=True)
            mm.then_inc(sem(s + "ssq"), 1)

        order_f = list(range(NCH_LAT, NCH)) + list(range(NCH_LAT))
        order_b = list(range(NCH - 1, NCH_LAT - 1, -1)) + list(range(NCH_LAT - 1, -1, -1))

        def gla_states(eng, s, h, half, order, name):
            eng.wait_ge(sem(s + "u_out"), h * 3 + 3)
            eng.wait_ge(sem(s + "decay"), h + 1)
            if h:
                eng.wait_ge(sem(s + "o"), h)
            for m in range(NCH - 1):
                a, c = order[m], order[m + 1]
                if m:
                    eng.wait_ge(sem(s + name), h * (NCH - 1) + m)
                eng.scalar_tensor_tensor(S[half, c, :], S[half, a, :], d_last[half, h % 2, a:a + 1], U[half, a, :],
                                         ALU.mult, ALU.add).then_inc(sem(s + name), 1)

        def gla_pool(pool, l):
            s = f"g{l}_"
            pool.memset(S[0:64, order_f[0], :], 0.0).then_inc(sem(s + "zeroed"), 1)
            pool.wait_ge(sem(s + "zeroed"), 1)
            pool.memset(S[64:P, order_b[0], :], 0.0).then_inc(sem(s + "zeroed"), 1)
            pool.wait_ge(sem(s + "zeroed"), 2)
            pool.memset(att_f[:], 0.0).then_inc(sem(s + "zeroed"), 1)
            pool.memset(att_b[:], 0.0).then_inc(sem(s + "zeroed"), 1)

            def keys(h):
                pool.wait_ge(sem(s + "qk_in"), 64 * (h + 1))
                pool.wait_ge(sem(s + "ek"), h + 1)
                pool.tensor_tensor(kp[:, h % 2], kd[:, h % 2, :], ek[:], ALU.mult).then_inc(sem(s + "kp"), 1)

            def queries(h):
                u = h % 2
                pool.wait_ge(sem(s + "eq"), h + 1)
                pool.tensor_tensor(qp[:, u], qd[:, u, :], eq[:], ALU.mult).then_inc(sem(s + "qp"), 1)
                pool.wait_ge(sem(s + "qp"), h + 1)
                pool.wait_ge(sem(s + "decay"), h + 1)
                pool.tensor_tensor(qpp[:, u].rearrange("p (n c) -> p n c", c=CHUNK), qp[:, u].rearrange("p (n c) -> p n c", c=CHUNK),
                                   d_ref[:, u].unsqueeze(2).broadcast_to([P, NCH, CHUNK]), ALU.mult).then_inc(sem(s + "qpp"), 1)
            pool.wait_ge(sem(s + "sub"), HEADS)
            keys(0)
            queries(0)
            for h in range(HEADS):
                if h + 1 < HEADS:
                    keys(h + 1)
                    queries(h + 1)

        def gla_dve(dve, l):
            s = f"g{l}_"
            to = T if l == 0 else SEQ
            dve.wait_ge(sem(s + "lr_in"), 48)
            for h in range(HEADS):
                dve.wait_ge(sem(s + "logit"), h + 1)
                dve.wait_ge(sem(s + "abs"), h + 1)
                at = 1536 * (h % 2)
                dve.tensor_scalar(oT[:, h, :], flat[:, at:at + T], gb[:, h, :], 0.0, ALU.add, ALU.min).then_inc(sem(s + "min"), 1)
            for h in range(HEADS):
                dve.wait_ge(sem(s + "log"), h + 1)
                dve.wait_ge(sem(s + "min"), h + 1)
                dve.tensor_tensor(oT[:, h, :], oT[:, h, :], logs[h], ALU.subtract).then_inc(sem(s + "sub"), 1)
            bc = b[:].rearrange("p (n c) -> p n c", c=CHUNK)
            mid = CHUNK // 2
            st = [0]

            def chain(ins):
                st[0] += 1
                ins.then_inc(sem(s + "dve_step"), 1)
                dve.wait_ge(sem(s + "dve_step"), st[0])

            def scan(h):
                g = oT[:, h, :]
                dve.wait_ge(sem(s + "sub"), h + 1)
                if h == 0:
                    dve.wait_ge(sem(s + "mask_in"), 48)
                else:
                    dve.wait_ge(sem(s + "decay"), h)
                chain(dve.tensor_tensor_scan(b[0:64, :], smask[0:64, :], g[0:64, :], 0.0, ALU.mult, ALU.add))
                chain(dve.tensor_tensor_scan(b[64:P, ::-1], smask[64:P, ::-1], g[64:P, ::-1], 0.0, ALU.mult, ALU.add))

            def against_middle(h):
                chain(dve.tensor_copy(c_ref[0:64, :], bc[0:64, :, mid - 1]))
                chain(dve.tensor_copy(c_ref[64:P, :], bc[64:P, :, mid]))
                chain(dve.tensor_copy(b_last[0:64, :], bc[0:64, :, CHUNK - 1]))
                chain(dve.tensor_copy(b_last[64:P, :], bc[64:P, :, 0]))
                chain(dve.tensor_tensor(dif[:], b_last[:], c_ref[:], ALU.subtract))
                chain(dve.tensor_tensor(bc, bc, c_ref[:].unsqueeze(2).broadcast_to([P, NCH, CHUNK]), ALU.subtract))
                dve.tensor_scalar(b[:], b[:], -CLAMP, CLAMP, ALU.max, ALU.min).then_inc(sem(s + "x"), 1)

            U2 = U[:].rearrange("p (j e) c -> p j e c", e=2)

            def round_out(h, r, n):
                dve.wait_ge(sem(s + "att"), h * 3 + r + 1)
                for dst, bank, m in ((att_f, 6, mask_f), (att_b, 7, mask_b)):
                    src = ps[0:CHUNK, bank, 0:2 * n * CHUNK].rearrange("p (j e c) -> p j e c", e=2, c=CHUNK)
                    for e in range(2):
                        ins = dve.tensor_tensor(dst[64 * e:64 * e + 64, 4 * r:4 * r + n, 64 * e:64 * e + 64],
                                                src[:, :, e, :], m[:].unsqueeze(1).broadcast_to([CHUNK, n, CHUNK]), ALU.mult)
                ins.then_inc(sem(s + "att_out"), 1)
                dve.wait_ge(sem(s + "u"), h * 3 + r + 1)
                d2 = d_lr[:, h % 2].rearrange("p (j e) -> p j e", e=2)
                for e in range(2):
                    ins = dve.tensor_tensor(U2[:, 4 * r:4 * r + n, e, :],
                                            ps[:, 3 + e, 0:n * P].rearrange("p (j c) -> p j c", c=P),
                                            d2[:, 4 * r:4 * r + n, e].unsqueeze(2).broadcast_to([P, n, P]), ALU.mult)
                ins.then_inc(sem(s + "u_out"), 1)

            def variance(h):
                dve.wait_ge(sem(s + "ssq"), h + 1)
                dve.tensor_scalar(var[:, 0:to], flat[:, 0:to], 1.0 / P, EPS, ALU.mult, ALU.add).then_inc(sem(s + "var"), 1)

            def finish(h):
                o = oT[:, h, 0:to]
                dve.wait_ge(sem(s + "std"), h + 1)
                dve.reciprocal(var[:, 0:to], var[:, 0:to]).then_inc(sem(s + "y_step"), 1)
                dve.wait_ge(sem(s + "y_step"), 2 * h + 1)
                dve.tensor_tensor(o, o, var[:, 0:to], ALU.mult).then_inc(sem(s + "y_step"), 1)
                dve.wait_ge(sem(s + "y_step"), 2 * h + 2)
                dve.wait_ge(sem(s + "gate"), h + 1)
                dve.scalar_tensor_tensor(o, o, gla_gain[:, l:l + 1], gate[:, h % 2, 0:to], ALU.mult, ALU.mult)\
                   .then_inc(sem(s + "y"), 1)

            scan(0)
            against_middle(0)
            dve.wait_ge(sem(s + "zeroed"), 4)
            for h in range(HEADS):
                dve.wait_ge(sem(s + "decay"), h + 1)
                if h:
                    dve.wait_ge(sem(s + "o"), h)
                for r, n in enumerate(ROUNDS):
                    round_out(h, r, n)
                    if h + 1 < HEADS and r < 2:
                        (scan, against_middle)[r](h + 1)
                    if h and r == 1:
                        variance(h - 1)
                gla_states(dve, s, h, slice(0, 64), order_f, "state_f")
                gla_states(dve, s, h, slice(64, P), order_b, "state_b")
                if h:
                    finish(h - 1)
            variance(HEADS - 1)
            finish(HEADS - 1)

        def wo_tn(l):
            return T if l == 0 else SEQ

        def wo_sp(sp, l):
            s = f"o{l}_"
            tn = wo_tn(l)
            tile_load(sp, s, 0, 0, io["w_out"][l], None)
            tile_load(sp, s, 1, 1, io["w_out"][l], None)
            for k in range(KT):
                if k >= 2:
                    sp.wait_ge(sem(s + "y_lo"), k - 1)
                sp.dma_start(stage[:, k % 2, 0:tn], mix_fm[k, :, 0:tn]).then_inc(sem(f"{s}y_in{k % 2}"), 16)
            with sp.Fori(0, 3) as i:
                for u in range(2):
                    tile_load(sp, s, i * 2 + u + 2, u, io["w_out"][l], i * 2 + u + 1)

        def wo_act(act, l):
            s = f"o{l}_"
            tn = wo_tn(l)
            for t in range(2):
                tile_split_act(act, s, t, t)
            for k in range(KT):
                act.wait_ge(sem(f"{s}y_in{k % 2}"), 16 * (k // 2 + 1))
                act.copy(h_hi[:, k, 0:tn], stage[:, k % 2, 0:tn]).then_inc(sem(s + "y_hi"), 1)
            with act.Fori(1, 4) as i:
                for u in range(2):
                    tile_split_act(act, s, i * 2 + u, u)

        def wo_pool(pool, l):
            s = f"o{l}_"
            tn = wo_tn(l)
            for t in range(2):
                tile_split_pool(pool, s, t, t)
            with pool.Fori(1, 4) as i:
                for u in range(2):
                    tile_split_pool(pool, s, i * 2 + u, u)

        def wo_pe(pe, l):
            s = f"o{l}_"
            pe.sem_inc(sem(s + "w_free"), 2)
            pe.wait_ge(sem(s + "y_lo"), KT)
            with pe.Fori(0, 4) as i:
                for u in range(2):
                    tile_pe(pe, s, i * 2 + u, u, wo_tn(l))

        def wo_dve(dve, l):
            s = f"o{l}_"
            tn = wo_tn(l)
            dve.sem_inc(sem(s + "evac"), 2)
            for k in range(KT):
                dve.wait_ge(sem(s + "y_hi"), k + 1)
                dve.tensor_tensor(h_lo[:, k, 0:tn], stage[:, k % 2, 0:tn], h_hi[:, k, 0:tn], ALU.subtract)\
                   .then_inc(sem(s + "y_lo"), 1)
            with dve.Fori(0, 4) as i:
                for u in range(2):
                    t = i * 2 + u
                    dve.wait_ge(sem(s + "w_free"), t + 3)
                    for c, n, g in segments(tn):
                        xs = x[:, bass.ts(t, 1), c:c + n].rearrange("p o n -> p (o n)")
                        ins = dve.scalar_tensor_tensor(xs, flat[:, u * 1536 + c:u * 1536 + c + n],
                                                       mod[:, bass.ds(t + l * 48 + 2 * KT, 1), g:g + 1].rearrange("p o n -> p (o n)"),
                                                       xs, ALU.mult, ALU.add)
                    ins.then_inc(sem(s + "evac"), 1)

        GATE, VALUE, DOWN = 0, 1, 2

        def ffn_downs(tn):
            return [(m, c, n) for c, n in chunks(tn) for m in range(KT)]

        def ffn_sp(sp, l):
            s = f"u{l}_"
            with sp.Fori(0, NFF) as i:
                for kind in range(3):
                    src = io["w_up"][l] if kind < 2 else io["w_down"][l]
                    at = i * 2 + kind if kind < 2 else i
                    sp.wait_ge(sem(f"{s}raw_free{kind}"), i + 1)
                    sp.dma_start(fw_raw[:, kind:kind + 1, :], src[bass.ts(at, 1)].rearrange("o p n -> p o n"))\
                      .then_inc(sem(f"{s}w_in{kind}"), 16)

        def ffn_loop(eng, tile):
            tile(0, 0, False, False)
            with eng.Fori(0, NFF // 2 - 1) as i:
                tile(i * 2 + 1, 1, True, False)
                tile(i * 2 + 2, 0, True, False)
            tile(NFF - 1, 1, True, True)

        def ffn_act(act, l):
            s = f"u{l}_"
            tn = wo_tn(l)

            def split(i, kind, slot):
                act.wait_ge(sem(f"{s}w_in{kind}"), i * 16 + 16)
                act.wait_ge(sem(f"{s}w_free{kind}"), i + 1)
                act.copy(fw_hi[:, slot, :], fw_raw[:, kind, :]).then_inc(sem(f"{s}w_hi{kind}"), 1)

            def tile(i, u, down, last):
                split(i, VALUE, 1)
                split(i, DOWN, 2 + u)
                for j, (c, n) in enumerate(chunks(tn)):
                    act.wait_ge(sem(f"{s}gate{j}"), i + 1)
                    act.wait_ge(sem(s + "conv_free"), i + 1) if j == 0 else None
                    at = c + 1 if c < SEQ else c + 3
                    act.copy(G[:, at:at + n], ps[:, j, 0:n]).then_inc(sem(s + "g_out"), 1)
                if not last:
                    split(i + 1, GATE, 0)
                act.wait_ge(sem(s + "conv"), i + 1)
                act.activation(cv[:, 1:tn + 3 if tn > SEQ else tn + 1], cv[:, 1:tn + 3 if tn > SEQ else tn + 1], ACT.Gelu,
                               bias=conv_b[:, l, bass.ds(i, 1)]).then_inc(sem(s + "gelu"), 1)
                for j, (c, n) in enumerate(chunks(tn)):
                    act.wait_ge(sem(f"{s}hid{j}"), i + 1)
                    act.wait_ge(sem(s + "hid_free"), i + 1) if j == 0 else None
                    at = c + 1 if c < SEQ else c + 3
                    act.copy(hid_hi[:, u, c:c + n], cv[:, at:at + n]).then_inc(sem(f"{s}hid_hi{j}"), 1)

            act.wait_ge(sem(s + "pads"), 1)
            split(0, GATE, 0)
            ffn_loop(act, tile)

        def ffn_pool(pool, l):
            s = f"u{l}_"
            tn = wo_tn(l)
            pool.memset(G[:], 0.0).then_inc(sem(s + "pads"), 1)
            pool.sem_inc(sem(s + "conv_free"), 1)
            for kind in range(3):
                pool.sem_inc(sem(f"{s}raw_free{kind}"), 1)

            def split(i, kind, slot):
                pool.wait_ge(sem(f"{s}w_hi{kind}"), i + 1)
                pool.tensor_tensor(fw_lo[:, slot, :], fw_raw[:, kind, :], fw_hi[:, slot, :], ALU.subtract)\
                    .then_inc(sem(f"{s}w_lo{kind}"), 1)
                pool.wait_ge(sem(f"{s}w_lo{kind}"), i + 1)
                pool.sem_inc(sem(f"{s}raw_free{kind}"), 1)

            def tile(i, u, down, last):
                split(i, VALUE, 1)
                split(i, DOWN, 2 + u)
                if not last:
                    split(i + 1, GATE, 0)
                for j, (c, n) in enumerate(chunks(tn)):
                    at = c + 1 if c < SEQ else c + 3
                    pool.wait_ge(sem(f"{s}hid_hi{j}"), i + 1)
                    pool.tensor_tensor(hid_lo[:, u, c:c + n], cv[:, at:at + n], hid_hi[:, u, c:c + n], ALU.subtract)\
                        .then_inc(sem(f"{s}hid_lo{j}"), 1)
                pool.wait_ge(sem(f"{s}hid_lo{len(chunks(tn)) - 1}"), i + 1)
                pool.sem_inc(sem(s + "conv_free"), 1)

            split(0, GATE, 0)
            ffn_loop(pool, tile)

        def ffn_pe(pe, l):
            s = f"u{l}_"
            tn = wo_tn(l)
            cs = chunks(tn)
            downs = ffn_downs(tn)
            nd = len(downs)
            pe.sem_inc(sem(f"{s}w_free0"), 1)
            pe.sem_inc(sem(f"{s}w_free1"), 1)
            pe.sem_inc(sem(f"{s}w_free2"), 2)
            pe.sem_inc(sem(s + "hid_free"), 2)

            def down(i, u, d):
                m, c, n = downs[d]
                if d == 0:
                    pe.wait_ge(sem(f"{s}w_lo{DOWN}"), i + 1)
                if m == 0:
                    pe.wait_ge(sem(f"{s}hid_lo{c // 512}"), i + 1)
                pe.wait_ge(sem(s + "down_out"), i * nd + d + 1)
                o = ps[:, 6 + d % 2, 0:n]
                wc = slice(m * P, (m + 1) * P)
                pe.matmul(o, fw_hi[:, 2 + u, wc], hid_hi[:, u, c:c + n], start=True, stop=False)
                pe.matmul(o, fw_hi[:, 2 + u, wc], hid_lo[:, u, c:c + n], start=False, stop=False)
                pe.matmul(o, fw_lo[:, 2 + u, wc], hid_hi[:, u, c:c + n], start=False, stop=True).then_inc(sem(s + "down"), 1)
                if d == nd - 1:
                    pe.wait_ge(sem(s + "down"), i * nd + nd)
                    pe.sem_inc(sem(f"{s}w_free2"), 1)
                    pe.sem_inc(sem(s + "hid_free"), 1)

            def tile(i, u, with_down, last):
                d = 0
                for kind in (GATE, VALUE):
                    pe.wait_ge(sem(f"{s}w_lo{kind}"), i + 1)
                    wh = fw_hi[:, kind, :].rearrange("p (k m) -> p k m", m=P)
                    wl = fw_lo[:, kind, :].rearrange("p (k m) -> p k m", m=P)
                    for j, (c, n) in enumerate(cs):
                        if kind == GATE:
                            if not isinstance(i, int) or i > 0:
                                pe.wait_ge(sem(s + "g_out"), i * len(cs) - len(cs) + j + 1)
                        elif not isinstance(i, int) or i > 0:
                            pe.wait_ge(sem(f"{s}hid{j}"), i)
                        o = ps[:, 3 * kind + j, 0:n]
                        for k in range(KT):
                            pe.matmul(o, wh[:, k], h_hi[:, k, c:c + n], start=(k == 0), stop=False)
                            pe.matmul(o, wh[:, k], h_lo[:, k, c:c + n], start=False, stop=False)
                            mm = pe.matmul(o, wl[:, k], h_hi[:, k, c:c + n], start=False, stop=(k == KT - 1))
                            if k == KT - 1:
                                mm.then_inc(sem(f"{s}gate{j}" if kind == GATE else f"{s}value{j}"), 1)
                            if k % 2 and with_down:
                                down(i - 1, 1 - u, d)
                                d += 1
                    pe.wait_ge(sem(f"{s}gate{len(cs) - 1}" if kind == GATE else f"{s}value{len(cs) - 1}"), i + 1)
                    pe.sem_inc(sem(f"{s}w_free{kind}"), 1)
            ffn_loop(pe, tile)
            for d in range(nd):
                down(NFF - 1, 1, d)

        def ffn_dve(dve, l):
            s = f"u{l}_"
            tn = wo_tn(l)
            cs = chunks(tn)
            downs = ffn_downs(tn)
            nd = len(downs)
            wide = tn + 2 if tn > SEQ else tn
            dve.sem_inc(sem(s + "down_out"), 2)

            def down(i, d):
                m, c, n = downs[d]
                g = int(c >= SEQ)
                dve.wait_ge(sem(s + "down"), i * nd + d + 1)
                at = l * 48 + 5 * KT + m
                dve.scalar_tensor_tensor(x[:, m, c:c + n], ps[:, 6 + d % 2, 0:n], mod[:, at, g:g + 1], x[:, m, c:c + n],
                                         ALU.mult, ALU.add).then_inc(sem(s + "down_out"), 1)

            def tile(i, u, with_down, last):
                todo = list(range(nd)) if with_down else []

                def some(k):
                    for _ in range(min(k, len(todo))):
                        down(i - 1, todo.pop(0))
                some(nd // 2)
                dve.wait_ge(sem(s + "g_out"), i * len(cs) + len(cs))
                dve.wait_ge(sem(s + "conv_free"), i + 1)
                for tap, src in ((1, 1), (0, 0), (2, 2)):
                    wt = conv_w[:, l, bass.ds(i, 1), tap:tap + 1].rearrange("p o n -> p (o n)")
                    if tap == 1:
                        ins = dve.tensor_scalar(cv[:, 1:1 + wide], G[:, src:src + wide], wt, None, ALU.mult)
                    else:
                        ins = dve.scalar_tensor_tensor(cv[:, 1:1 + wide], G[:, src:src + wide], wt, cv[:, 1:1 + wide],
                                                       ALU.mult, ALU.add)
                    if tap == 2:
                        ins.then_inc(sem(s + "conv"), 1)
                    else:
                        ins.then_inc(sem(s + "conv_step"), 1)
                        dve.wait_ge(sem(s + "conv_step"), i * 2 + 1 + (tap == 0))
                    some(1)
                some(1)
                for j, (c, n) in enumerate(cs):
                    at = c + 1 if c < SEQ else c + 3
                    dve.wait_ge(sem(f"{s}value{j}"), i + 1)
                    dve.wait_ge(sem(s + "gelu"), i + 1)
                    dve.tensor_tensor(cv[:, at:at + n], cv[:, at:at + n], ps[:, 3 + j, 0:n], ALU.mult)\
                       .then_inc(sem(f"{s}hid{j}"), 1)
                    some(4 if j < len(cs) - 1 else nd)
            ffn_loop(dve, tile)
            for d in range(nd):
                down(NFF - 1, d)

        def last_pe(pe):
            norm_pe(pe, "last_", SEQ)

        def last_act(act):
            norm_act_head(act, "last_", SEQ)

        def last_dve(dve):
            norm_dve_head(dve, "last_", SEQ)
            for k in range(KT):
                if k >= 2:
                    dve.wait_ge(sem(f"last_out{k % 2}"), 16 * (k // 2))
                dve.scalar_tensor_tensor(fo[:, k % 2, 0:SEQ], x[:, k, 0:SEQ], gains[:, 2 * DEPTH, k:k + 1], rstd[:, 0:SEQ],
                                         ALU.mult, ALU.mult).then_inc(sem("last_y"), 1)

        def last_sp(sp):
            for k in range(KT):
                sp.wait_ge(sem("last_y"), k + 1)
                sp.dma_start(out[k], fo[:, k % 2, 0:SEQ]).then_inc(sem(f"last_out{k % 2}"), 16)
            for u in range(2):
                sp.wait_ge(sem(f"last_out{u}"), 16 * KT // 2)

        @block.sync
        def _(sp):
            mod_sp(sp)
            end_phase(sp, "sp")
            for l in range(DEPTH):
                end_phase(sp, "sp", f"n{l}0")
                proj_sp(sp, l)
                end_phase(sp, "sp", f"p{l}")
                att_sp(sp, l, 0)
                end_phase(sp, "sp", f"a{l}0")
                gla_sp(sp, l)
                end_phase(sp, "sp", f"g{l}")
                att_sp(sp, l, 1)
                end_phase(sp, "sp", f"a{l}1")
                wo_sp(sp, l)
                end_phase(sp, "sp", f"o{l}")
                end_phase(sp, "sp", f"n{l}1")
                ffn_sp(sp, l)
                end_phase(sp, "sp", f"u{l}")
            last_sp(sp)


        @block.scalar
        def _(act):
            mod_act(act)
            end_phase(act, "act")
            for l in range(DEPTH):
                norm_act(act, l, 0)
                end_phase(act, "act", f"n{l}0")
                proj_act(act, l)
                end_phase(act, "act", f"p{l}")
                att_act(act, l, 0)
                end_phase(act, "act", f"a{l}0")
                gla_act(act, l)
                end_phase(act, "act", f"g{l}")
                att_act(act, l, 1)
                end_phase(act, "act", f"a{l}1")
                wo_act(act, l)
                end_phase(act, "act", f"o{l}")
                norm_act(act, l, 1)
                end_phase(act, "act", f"n{l}1")
                ffn_act(act, l)
                end_phase(act, "act", f"u{l}")
            last_act(act)


        @block.tensor
        def _(pe):
            mod_pe(pe)
            end_phase(pe, "pe")
            for l in range(DEPTH):
                norm_pe(pe, f"n{l}0_", T)
                end_phase(pe, "pe", f"n{l}0")
                proj_pe(pe, l)
                end_phase(pe, "pe", f"p{l}")
                att_pe(pe, l, 0)
                end_phase(pe, "pe", f"a{l}0")
                gla_pe(pe, l)
                end_phase(pe, "pe", f"g{l}")
                att_pe(pe, l, 1)
                end_phase(pe, "pe", f"a{l}1")
                wo_pe(pe, l)
                end_phase(pe, "pe", f"o{l}")
                norm_pe(pe, f"n{l}1_", wo_tn(l))
                end_phase(pe, "pe", f"n{l}1")
                ffn_pe(pe, l)
                end_phase(pe, "pe", f"u{l}")
            last_pe(pe)


        @block.vector
        def _(dve):
            mod_dve(dve)
            end_phase(dve, "dve")
            for l in range(DEPTH):
                norm_dve(dve, l, 0)
                end_phase(dve, "dve", f"n{l}0")
                proj_dve(dve, l)
                end_phase(dve, "dve", f"p{l}")
                att_dve(dve, l, 0)
                end_phase(dve, "dve", f"a{l}0")
                gla_dve(dve, l)
                end_phase(dve, "dve", f"g{l}")
                att_dve(dve, l, 1)
                end_phase(dve, "dve", f"a{l}1")
                wo_dve(dve, l)
                end_phase(dve, "dve", f"o{l}")
                norm_dve(dve, l, 1)
                end_phase(dve, "dve", f"n{l}1")
                ffn_dve(dve, l)
                end_phase(dve, "dve", f"u{l}")
            last_dve(dve)


        @block.gpsimd
        def _(pool):
            mod_pool(pool)
            end_phase(pool, "pool")
            for l in range(DEPTH):
                norm_pool(pool, l, 0)
                end_phase(pool, "pool", f"n{l}0")
                proj_pool(pool, l)
                end_phase(pool, "pool", f"p{l}")
                att_pool(pool, l, 0)
                end_phase(pool, "pool", f"a{l}0")
                gla_pool(pool, l)
                end_phase(pool, "pool", f"g{l}")
                att_pool(pool, l, 1)
                end_phase(pool, "pool", f"a{l}1")
                wo_pool(pool, l)
                end_phase(pool, "pool", f"o{l}")
                norm_pool(pool, l, 1)
                end_phase(pool, "pool", f"n{l}1")
                ffn_pool(pool, l)
                end_phase(pool, "pool", f"u{l}")


def lay_out(inp):
    a = {k: np.asarray(v) for k, v in inp.items()}
    c = np.ascontiguousarray
    L = DEPTH
    io = {}
    io["xT"] = c(np.concatenate([a["x"][0], a["ctx"][0]], 0).T.reshape(KT, P, T).transpose(1, 0, 2))
    io["cc"] = c(np.stack([a["c"][0], a["c_ctx"]], -1).reshape(KT, P, 2).transpose(1, 0, 2))
    io["w_mod"] = c(a["w_mod"].reshape(L, KT, P, 12, 512).transpose(0, 3, 2, 1, 4).reshape(L * 12, P, KT, 512))
    io["b_mod"] = c(a["b_mod"].reshape(L * 48, P).T)
    g = np.stack([a[n][l] for l in range(L) for n in ("norm1_g", "norm2_g")] + [a["final_norm_g"]])
    io["gains"] = c(g.reshape(2 * L + 1, KT, P).transpose(2, 0, 1))
    w = a["w_in"]
    at, cut = 0, {}
    for name, n in (("na_q", 256), ("na_k", 256), ("na_v", 256), ("wa_q", 256), ("wa_k", 128), ("wa_v", 128),
                    ("g_q", 256), ("g_k", 256), ("g_v", 512), ("g_out", 512), ("lr", 32)):
        cut[name] = w[:, :, at:at + n]
        at += n
    pad = np.zeros((L, D, P - 32), w.dtype)
    fm = np.concatenate([cut["na_k"], cut["wa_k"], cut["g_k"], cut["lr"], pad, cut["na_q"], cut["wa_q"], cut["g_q"], cut["g_out"]], -1)
    io["w_fm"] = c(fm.reshape(L, KT, P, NFM, P).transpose(0, 3, 2, 1, 4).reshape(L, NFM, P, KT * P))
    tm = np.concatenate([cut["na_v"], cut["wa_v"], cut["g_v"]], -1)
    io["w_tm"] = c(tm.reshape(L, KT, P, 2, HALF).transpose(0, 3, 2, 1, 4))
    io["w_out"] = c(a["w_out"].reshape(L, KT, P, KT, P).transpose(0, 3, 2, 1, 4).reshape(L, KT, P, KT * P))
    up = a["ffn_w_up"].reshape(L, KT, P, 2, NFF, P)[:, :, :, ::-1]
    io["w_up"] = c(up.transpose(0, 4, 3, 2, 1, 5).reshape(L, NFF * 2, P, KT * P))
    io["w_down"] = c(a["ffn_w_down"].reshape(L, NFF, P, D))
    io["conv_w"] = c(a["ffn_conv_w"].reshape(L, 3, NFF, P).transpose(3, 0, 2, 1))
    io["conv_b"] = c(a["ffn_conv_b"].reshape(L, NFF, P).transpose(2, 0, 1))
    io["gla_gain"] = c(a["gla_norm_g"].T)
    gw = np.zeros((L, HEADS, 32, P), np.float32)
    gb = np.zeros((L, P, HEADS, 1), np.float32)
    for h in range(HEADS):
        for d in range(2):
            gw[:, h, 16 * d:16 * d + 16, 64 * d:64 * d + 64] = a["gla_gate_w"][:, d, :, 64 * h:64 * h + 64]
            gb[:, 64 * d:64 * d + 64, h, 0] = a["gla_gate_b"][:, d, 64 * h:64 * h + 64]
    io["gate_w"], io["gate_b"] = gw, gb
    sk = np.full((L, 2, HEADS), MASKED, np.float32)
    sk[:, 1] = a["wa_sink"]
    io["sinks"] = c(np.broadcast_to(sk[None], (P, L, 2, HEADS)))
    rpb = a["na_rpb"]
    nb = np.full((L, 8, P, HEADS, 10, 64), MASKED, np.float32)
    col = np.arange(64)
    cs = np.clip(col - 8, 0, 48)
    inside = (col[None, :] >= cs[:, None]) & (col[None, :] < cs[:, None] + 16)
    off = np.where(inside, col[None, :] - col[:, None] + 15, 0)
    for j in range(8):
        w0 = min(max(j - 2, 0), 4) * 2
        for e in range(2):
            r = 2 * j + e
            rs = min(max(r - 4, 0), 8)
            for kr in range(rs, rs + 8):
                v = rpb[:, :, kr - r + 7, :][:, :, off]
                nb[:, j, 64 * e:64 * e + 64, :, kr - w0, :] = np.where(inside, v, np.float32(MASKED)).transpose(0, 2, 1, 3)
    io["na_bias"] = nb.reshape(L, 8, P, HEADS * 640)
    wm = np.full((8, P, 384), MASKED, np.float32)
    for n in range(8):
        w0 = min(max(n - 1, 0), 5)
        q = n * P + np.arange(P)[:, None]
        k = w0 * P + np.arange(384)[None, :]
        wm[n][np.abs(q - k) <= 128] = 0.0
    io["wa_mask"] = wm
    t = np.arange(SEQ)
    inv = (np.float32(10000.0) ** (-np.arange(16, dtype=np.float32) / np.float32(16)))
    ang = np.concatenate([(t // 64).astype(np.float32)[:, None] * inv, (t % 64).astype(np.float32)[:, None] * inv], -1).T
    cos, sin = np.cos(ang).astype(np.float32), np.sin(ang).astype(np.float32)
    io["rope"] = c(np.stack([np.tile(cos, (4, 1)), np.tile(np.concatenate([-sin, sin]), (2, 1))]))
    sm = np.ones((P, T), np.float32)
    sm[0:64, 0::CHUNK] = 0
    sm[64:, CHUNK - 1::CHUNK] = 0
    io["smask"] = sm
    tri = np.tril(np.ones((CHUNK, CHUNK), np.float32))
    io["tri"] = c(np.stack([tri.T, tri]))
    return io


def kernel(**inputs):
    import concourse.bacc as bacc
    from concourse.bass_utils import run_bass_kernel_spmd
    arrays = lay_out(inputs)
    nc = bacc.Bacc("TRN2", target_bir_lowering=False, num_devices=1)
    io = {k: nc.dram_tensor(f"in_{k}", v.shape, F32, kind="ExternalInput").ap() for k, v in arrays.items()}
    out = nc.dram_tensor("out_0", (KT, P, SEQ), F32, kind="ExternalOutput").ap()
    build(nc, io, out)
    r = run_bass_kernel_spmd(nc, [{f"in_{k}": v for k, v in arrays.items()}], core_ids=[0])
    return r.results[0]["out_0"].reshape(KT * P, SEQ).T[None].copy()
```

```python
from contextlib import ExitStack

import numpy as np

import concourse.bass as bass
from concourse import mybir

F32 = mybir.dt.float32
F32R = mybir.dt.float32r
ALU = mybir.AluOpType
ACT = mybir.ActivationFunctionType
AX = mybir.AxisListType.X

P = 128
D = 1024
KT = D // P
DEPTH = 2
SEQ = 1024
CTX = 256
T = SEQ + CTX
NTOK = T // P
FF = 2816
NFF = FF // P
EPS = 1e-6
TAU = 16.0
HEADS = 4
CHUNK = 64
NCH = T // CHUNK
NCH_LAT = SEQ // CHUNK
NA_K, WA_K, G_K, LR, NA_Q, WA_Q, G_Q, G_OUT, NFM = 0, 2, 3, 5, 6, 8, 10, 12, 16
NA_V, WA_V, G_V, NTM = 0, 256, 384, 896
HALF = NTM // 2
OUT_SLOTS = 4
MASKED = -1e30
CLAMP = 40.0 * TAU


def chunks(n):
    return [(c, min(512, n - c)) for c in range(0, n, 512)]


def segments(n):
    return [(0, SEQ, 0)] + ([(SEQ, CTX, 1)] if n > SEQ else [])


def build(nc, io, out):
    ctx = ExitStack()
    with ctx:
        def sb(name, shape, dt=F32):
            return ctx.enter_context(nc.sbuf_tensor(name, shape, dt))

        def shared(*specs):
            with ExitStack() as s:
                return [s.enter_context(nc.sbuf_tensor(n, shp, dt)) for n, shp, dt in specs]

        RUNS = [r for l in range(DEPTH)
                for r in (f"p{l}", f"a{l}", f"g{l}", f"o{l}", f"u{l}")]
        sems = {}
        banks = ([], [])

        def sem(name):
            if name not in sems:
                run = name.split("_")[0]
                if run in RUNS:
                    bank = banks[RUNS.index(run) % 2]
                    used = sum(1 for k in sems if k.split("_")[0] == run)
                    if used == len(bank):
                        bank.append(ctx.enter_context(nc.semaphore(f"bank{RUNS.index(run) % 2}_{used}")))
                    sems[name] = bank[used]
                else:
                    sems[name] = ctx.enter_context(nc.semaphore(name))
            return sems[name]

        proj_fm = nc.dram_tensor("proj_fm", (NFM * P, T), F32, kind="Internal").ap()
        proj_tm = nc.dram_tensor("proj_tm", (NTOK, P, NTM), F32, kind="Internal").ap()
        mix_fm = nc.dram_tensor("mix_fm", (KT, P, T), F32, kind="Internal").ap()

        x = sb("x", [P, KT, T])
        mod = sb("mod", [P, DEPTH * 48, 2])
        gains = sb("gains", [P, 2 * DEPTH + 1, KT])
        coef = sb("coef", [P, DEPTH * 2, KT, 2])
        silu_c = sb("silu_c", [P, KT, 2])
        ident = sb("ident", [P, P])
        ones = sb("ones", [P, P])
        eps = sb("eps", [P, 1])
        rstd = sb("rstd", [P, T])
        sinks = sb("sinks", [P, DEPTH, 2, HEADS])
        gla_gain = sb("gla_gain", [P, DEPTH])
        conv_w = sb("conv_w", [P, DEPTH, NFF, 3])
        conv_b = sb("conv_b", [P, DEPTH, NFF])

        wm, sq_first, bmod, _, _, rows = shared(
            ("wm", [P, 3, KT * 512], F32), ("sq_first", [P, 4, T], F32), ("bmod", [P, DEPTH * 48], F32),
            ("to_w_raw", [P, KT * (2 * T - 3 * 512) - 4 * T - DEPTH * 48], F32), ("over_w_raw", [P, 2, KT * P], F32),
            ("rows", [2, DEPTH * 48 * P], F32))
        wm = wm[:].rearrange("p u (k n) -> p u k n", n=512)
        dense = ctx.enter_context(ExitStack())
        h_hi = dense.enter_context(nc.sbuf_tensor("h_hi", [P, KT, T], F32R))
        h_lo = dense.enter_context(nc.sbuf_tensor("h_lo", [P, KT, T], F32R))
        w_bufs = [("w_raw", [P, 2, KT * P], F32), ("w_hi", [P, 2, KT * P], F32R), ("w_lo", [P, 2, KT * P], F32R)]
        n_bufs = [("nt", [P, 4, T], F32), ("nfull", [P, 2, T], F32)]
        w_raw, w_hi, w_lo, stage, w2_raw, w2_hi, w2_lo, stage2 = shared(
            *w_bufs, ("stage", [P, 2, T], F32),
            ("w2_raw", [P, KT, HALF], F32), ("w2_hi", [P, KT, HALF], F32R), ("w2_lo", [P, KT, HALF], F32R),
            ("stage2", [P, 2, HALF], F32))
        nt_p, nfull_p = shared(*[(f"pad_{n}", shp, dt) for n, shp, dt in w_bufs], *n_bufs)[3:]
        (fo,) = shared(("fo", [P, OUT_SLOTS, SEQ], F32))
        (ow_raw, ow_hi, ow_lo, y_raw) = shared(
            ("ow_raw", [P, 2, KT * P], F32), ("ow_hi", [P, 2, KT * P], F32R), ("ow_lo", [P, 2, KT * P], F32R),
            ("y_raw", [P, KT, T], F32))
        f_bufs = [("fw_raw", [P, 3, KT * P], F32), ("fw_hi", [P, 4, KT * P], F32R), ("fw_lo", [P, 4, KT * P], F32R)]
        fw_raw, fw_hi, fw_lo, hid_hi, hid_lo, G, cv = shared(
            *f_bufs, ("hid_hi", [P, 2, T], F32R), ("hid_lo", [P, 2, T], F32R), ("G", [P, T + 4], F32), ("cv", [P, T + 4], F32))
        nt_f, nfull_f = shared(*[(f"pad_{n}", shp, dt) for n, shp, dt in f_bufs],
                               *[(f"{n}_f", shp, dt) for n, shp, dt in n_bufs])[3:]
        (sq,) = shared(*[(f"pad_{n}", shp, dt) for n, shp, dt in (("o0", [P, 2, KT * P], F32), ("o1", [P, 2, KT * P], F32R),
                         ("o2", [P, 2, KT * P], F32R), ("o3", [P, KT, T], F32))], ("sq", [P, 2, T], F32))[4:]
        dense.close()
        (k_raw, k_sw, k_hi, k_lo, v_att, wk_hi, wk_lo, wv_att, bias_t, Pm, PT, q_blk, q_swb, qb, mx, nmax, sums, tot, rec, o_att, o_st,
         rope_c, rope_s) = shared(
            ("k_raw", [P, 2, T], F32), ("k_sw", [P, 2, SEQ], F32),
            ("k_hi", [P, HEADS, T], F32R), ("k_lo", [P, HEADS, T], F32R), ("v_att", [P, NTOK, 256], F32),
            ("wk_hi", [P, 2, T], F32R), ("wk_lo", [P, 2, T], F32R), ("wv_att", [P, NTOK, P], F32),
            ("bias_t", [P, 2, HEADS * 640], F32), ("Pm", [P, 2, 896], F32), ("PT", [P, 2, 896], F32),
            ("q_blk", [P, 2, HEADS, P], F32), ("q_swb", [P, 2, HEADS, P], F32),
            ("qb", [P, 2, HEADS, P], F32R), ("mx", [P, HEADS, 4], F32), ("nmax", [P, HEADS], F32),
            ("sums", [P, 2, HEADS, 3], F32), ("tot", [P, HEADS], F32), ("rec", [P, HEADS], F32),
            ("o_att", [P, 2, 256], F32), ("o_st", [P, 2, 2, P], F32),
            ("rope_c", [P, SEQ], F32), ("rope_s", [P, SEQ], F32))
        (qd, kd, v_g, gw, gb, b, eq, ek, qp, kp, qpp, kT, att_f, att_b, U, S, oT, mask_f,
         mask_b, smask, c_ref, b_last, dif, d_last, d_ref, d_lr, var, gate) = shared(
            ("qd", [P, 2, T], F32), ("kd", [P, 2, T], F32), ("v_g", [P, 2, NTOK, P], F32),
            ("gw", [32, HEADS, P], F32), ("gb", [P, HEADS, 1], F32), ("b", [P, T], F32),
            ("eq", [P, T], F32), ("ek", [P, T], F32), ("qp", [P, 2, T], F32), ("kp", [P, 2, T], F32),
            ("qpp", [P, 2, T], F32), ("kT", [P, 2, NTOK, P], F32), ("att_f", [P, NTOK, P], F32),
            ("att_b", [P, NTOK, P], F32), ("U", [P, NCH, P], F32), ("S", [P, NCH, P], F32),
            ("oT", [P, HEADS, T], F32), ("mask_f", [CHUNK, CHUNK], F32), ("mask_b", [CHUNK, CHUNK], F32),
            ("smask", [P, T], F32), ("c_ref", [P, NCH], F32), ("b_last", [P, NCH], F32),
            ("dif", [P, NCH], F32), ("d_last", [P, 2, NCH], F32), ("d_ref", [P, 2, NCH], F32), ("d_lr", [P, 2, NCH], F32),
            ("var", [P, T], F32), ("gate", [P, 2, T], F32))

        ps = ctx.enter_context(nc.psum_tensor("ps", [P, 8, 512], F32))
        flat = ps[:, :, :].rearrange("p b n -> p (b n)")

        phase_done = sem("phase_done")
        count = {}

        def end_phase(eng, name, run=None):
            count[name] = count.get(name, 0) + 5
            eng.drain().then_inc(phase_done, 1)
            eng.wait_ge(phase_done, count[name])
            eng.drain()
            if name == "pool" and run:
                for handle in banks[RUNS.index(run) % 2]:
                    eng.sem_clear(handle)

        block = ctx.enter_context(nc.Block())

        NU = DEPTH * 12
        FIRST_SUM = 5 * 512

        def mod_sp(sp):
            sp.dma_start(silu_c[:], io["cc"]).then_inc(sem("c_in"), 16)

            def load(t, u):
                sp.dma_start(wm[:, u:u + 1], io["w_mod"][bass.ts(t, 1)].rearrange("o p k n -> p o k n"))\
                  .then_inc(sem(f"wm_in{u}"), 16)
            for u in range(3):
                load(u, u)
            for dst, src in ((x[:], io["xT"]), (bmod[:], io["b_mod"]), (gains[:], io["gains"]),
                             (sinks[:], io["sinks"]), (gla_gain[:], io["gla_gain"]), (conv_w[:], io["conv_w"]),
                             (conv_b[:], io["conv_b"])):
                sp.dma_start(dst, src).then_inc(sem("lasting_in"), 16)
            with sp.Fori(1, NU // 3) as i:
                for u in range(3):
                    sp.wait_ge(sem("row_done"), i * 3 + u + 1)
                    load(i * 3 + u, u)
            for t in range(2):
                tile_load(sp, "p0_", t, t, io["w_fm"][0], None)

        def mod_act(act):
            act.sem_inc(sem("row_out"), 3)
            act.wait_ge(sem("c_in"), 16)
            act.activation(silu_c[:], silu_c[:], ACT.Silu).then_inc(sem("silu_ready"), 1)

            def rows_out(first, last):
                with act.Fori(first, last) as i:
                    for u in range(3):
                        act.wait_ge(sem("row_done"), i * 3 + u + 4)
                        act.copy(rows[:, bass.ts(i * 3 + u, 512)], ps[0:2, u, :]).then_inc(sem("row_out"), 1)
            rows_out(0, NU // 6)
            act.wait_ge(sem("lasting_in"), 16 * 7)
            squares_act(act, "first_", T, sq_first)
            rows_out(NU // 6, NU // 3)
            rstd_act(act, "first_", T, FIRST_SUM)

        def mod_pe(pe):
            pe.sem_inc(sem("row_done"), 3)
            pe.wait_ge(sem("silu_ready"), 1)
            with pe.Fori(0, NU // 3) as i:
                for u in range(3):
                    pe.wait_ge(sem(f"wm_in{u}"), i * 16 + 16)
                    pe.wait_ge(sem("row_out"), i * 3 + u + 1)
                    for k in range(KT):
                        mm = pe.matmul(ps[0:2, u, :], silu_c[:, k, :], wm[:, u, k, :], start=(k == 0), stop=(k == KT - 1))
                    mm.then_inc(sem("row_done"), 1)
            pe.wait_ge(sem("consts"), 2)
            pe.wait_ge(sem("first_added"), KT - 1)
            norm_sum(pe, "first_", T, FIRST_SUM)
            pe.wait_ge(sem("row_out"), 3 + NU)
            for t in range(DEPTH * 48):
                mm = pe.transpose(ps[:, 4, 2 * t:2 * t + 2], rows[:, t * P:(t + 1) * P], ident[0:2, 0:2])
            mm.then_inc(sem("mod_t"), 1)

        def mod_dve(dve):
            dve.wait_ge(sem("lasting_in"), 16 * 7)
            squares_add(dve, "first_", T, sq_first)
            dve.wait_ge(sem("mod_t"), 1)
            dve.tensor_tensor(mod[:], ps[:, 4, 0:DEPTH * 96].rearrange("p (t s) -> p t s", s=2),
                              bmod[:].unsqueeze(2).broadcast_to([P, DEPTH * 48, 2]), ALU.add).then_inc(sem("mod_v"), 1)
            dve.wait_ge(sem("mod_v"), 1)
            for l in range(DEPTH):
                for w in range(2):
                    t0 = l * 48 + (3 * w + 1) * KT
                    dve.scalar_tensor_tensor(coef[:, 2 * l + w], mod[:, t0:t0 + KT, :], 1.0,
                                             gains[:, 2 * l + w, :].unsqueeze(2).broadcast_to([P, KT, 2]),
                                             ALU.add, ALU.mult)

        def mod_pool(pool):
            pool.memset(ident[:], 0.0).then_inc(sem("ident_0"), 1)
            pool.memset(ones[:], 1.0)
            pool.memset(eps[:], EPS).then_inc(sem("consts"), 1)
            pool.wait_ge(sem("ident_0"), 1)
            pool.affine_select(out=ident[:], in_=ident[:], compare_op=ALU.not_equal, fill=1.0, base=0,
                               pattern=[[-1, P]], channel_multiplier=1).then_inc(sem("consts"), 1)

        def norm_name(l, w):
            return f"{'pu'[w]}{l}_n_"

        def norm_tokens(l, w):
            return T if (l == 0 or w == 0) else SEQ

        def squares_act(act, s, tn, ring):
            slots = ring.shape[1]
            for k in range(KT):
                if k > slots:
                    act.wait_ge(sem(s + "added"), k - slots)
                act.activation(ring[:, (k - 1) % slots, :tn] if k else rstd[:, :tn], x[:, k, :tn], ACT.Square)\
                   .then_inc(sem(s + "sq"), 1)

        def squares_add(eng, s, tn, ring):
            slots = ring.shape[1]
            for k in range(1, KT):
                eng.wait_ge(sem(s + "sq"), k + 1)
                if k > 1:
                    eng.wait_ge(sem(s + "added"), k - 1)
                eng.tensor_tensor(rstd[:, :tn], rstd[:, :tn], ring[:, (k - 1) % slots, :tn], ALU.add).then_inc(sem(s + "added"), 1)

        def norm_sum(pe, s, tn, at=0):
            for c, n in chunks(tn):
                mm = pe.matmul(flat[:, at + c:at + c + n], ones[:], rstd[:, c:c + n], start=True, stop=True)
            mm.then_inc(sem(s + "ssq"), 1)

        def rstd_act(act, s, tn, at=0):
            act.wait_ge(sem(s + "ssq"), 1)
            act.activation(rstd[:, :tn], flat[:, at:at + tn], ACT.Ln, scale=1.0 / D, bias=eps[:]).then_inc(sem(s + "ln"), 1)
            act.wait_ge(sem(s + "ln"), 1)
            act.activation(rstd[:, :tn], rstd[:, :tn], ACT.Exp, scale=-0.5).then_inc(sem(s + "rstd"), 1)

        def norm_act(act, l, w):
            s, tn = norm_name(l, w), norm_tokens(l, w)
            nt, nfull = (nt_p, nfull_p) if w == 0 else (nt_f, nfull_f)
            for k in range(KT):
                act.wait_ge(sem(s + "xn"), k + 1)
                odd = k % 2
                if odd and k >= 4:
                    act.wait_ge(sem(s + "lo_odd"), k // 2 - 1)
                for c, n, g in segments(tn):
                    dst = nfull[:, (k // 2) % 2, c:c + n] if odd else h_hi[:, k, c:c + n]
                    a = act.activation(dst, nt[:, k % 4, c:c + n], ACT.Identity,
                                       bias=mod[:, l * 48 + 3 * w * KT + k, g:g + 1])
                if odd:
                    a.then_inc(sem(s + "full"), 1)
                    act.wait_ge(sem(s + "full"), k // 2 + 1)
                    act.copy(h_hi[:, k, :tn], nfull[:, (k // 2) % 2, :tn]).then_inc(sem(s + "hi_odd"), 1)
                else:
                    a.then_inc(sem(s + "hi_even"), 1)

        def norm_dve(dve, l, w):
            s, tn = norm_name(l, w), norm_tokens(l, w)
            nt = nt_p if w == 0 else nt_f
            if l or w:
                dve.wait_ge(sem(s + "rstd"), 1)

            def low(k):
                dve.wait_ge(sem(s + "hi_even"), k // 2 + 1)
                for c, n, g in segments(tn):
                    i = dve.scalar_tensor_tensor(h_lo[:, k, c:c + n], nt[:, k % 4, c:c + n],
                                                 mod[:, l * 48 + 3 * w * KT + k, g:g + 1], h_hi[:, k, c:c + n],
                                                 ALU.add, ALU.subtract)
                i.then_inc(sem(s + "lo_even"), 1)

            for k in range(KT):
                if k >= 4:
                    if k % 2:
                        dve.wait_ge(sem(s + "full"), k // 2 - 1)
                    else:
                        dve.wait_ge(sem(s + "lo_even"), k // 2 - 1)
                for c, n, g in segments(tn):
                    i = dve.scalar_tensor_tensor(nt[:, k % 4, c:c + n], x[:, k, c:c + n], coef[:, 2 * l + w, k, g:g + 1],
                                                 rstd[:, c:c + n], ALU.mult, ALU.mult)
                i.then_inc(sem(s + "xn"), 1)
                if k % 2:
                    low(k - 1)

        def norm_pool(pool, l, w):
            s, tn = norm_name(l, w), norm_tokens(l, w)
            nfull = nfull_p if w == 0 else nfull_f
            for k in range(1, KT, 2):
                pool.wait_ge(sem(s + "hi_odd"), k // 2 + 1)
                pool.tensor_tensor(h_lo[:, k, :tn], nfull[:, (k // 2) % 2, :tn], h_hi[:, k, :tn], ALU.subtract)\
                    .then_inc(sem(s + "lo_odd"), 1)

        def h_ready(eng, l, w, k):
            eng.wait_ge(sem(norm_name(l, w) + ("lo_odd" if k % 2 else "lo_even")), k // 2 + 1)

        FIRST_STEPS = [(0, 0), (0, 1), (1, 0), (0, 2), (1, 1), (0, 3), (0, 4), (0, 5), (1, 2), (0, 6), (0, 7)]
        FIRST_STEPS += [(1, k) for k in range(3, KT)]

        def tile_split_act(act, s, t, u):
            act.wait_ge(sem(f"{s}w_in{u}"), 8 * t + (16 if u == 0 else 8))
            act.wait_ge(sem(s + "w_free"), t + 1)
            act.copy(w_hi[:, u, :], w_raw[:, u, :]).then_inc(sem(s + "w_hi"), 1)

        def tile_split_pool(pool, s, t, u):
            pool.wait_ge(sem(s + "w_hi"), t + 1)
            pool.tensor_tensor(w_lo[:, u, :], w_raw[:, u, :], w_hi[:, u, :], ALU.subtract).then_inc(sem(s + "w_lo"), 1)

        def tile_load(sp, s, t, u, src, raw_free):
            if raw_free is not None:
                sp.wait_ge(sem(s + "w_lo"), raw_free)
            sp.dma_start(w_raw[:, u:u + 1, :], src[bass.ts(t, 1)].rearrange("o p n -> p o n"))\
              .then_inc(sem(f"{s}w_in{u}"), 16)

        def tile_pe(pe, s, t, u, tn):
            pe.wait_ge(sem(s + "w_lo"), t + 1)
            pe.wait_ge(sem(s + "evac"), t + 1)
            wh = w_hi[:, u, :].rearrange("p (k m) -> p k m", m=P)
            wl = w_lo[:, u, :].rearrange("p (k m) -> p k m", m=P)
            cs = chunks(tn)
            for c, n in cs:
                o = flat[:, u * 1536 + c:u * 1536 + c + n]
                for k in range(KT):
                    pe.matmul(o, wh[:, k], h_hi[:, k, c:c + n], start=(k == 0), stop=False)
                    pe.matmul(o, wh[:, k], h_lo[:, k, c:c + n], start=False, stop=False)
                    mm = pe.matmul(o, wl[:, k], h_hi[:, k, c:c + n], start=False, stop=(k == KT - 1))
            mm.then_inc(sem(s + "w_free"), 1)

        def proj_sp(sp, l):
            s = f"p{l}_"
            wfm = io["w_fm"][l]

            def store(t, u):
                sp.wait_ge(sem(s + "staged"), t + 1)
                sp.dma_start(proj_fm.rearrange("(t p) n -> t p n", p=P)[bass.ts(t, 1)].rearrange("o p n -> p o n"),
                             stage[:, u:u + 1, :]).then_inc(sem(f"{s}st_out{u}"), 16)

            def load_half(hf):
                if hf:
                    sp.wait_ge(sem(s + "w2_lo"), hf)
                sp.dma_start(w2_raw[:], io["w_tm"][l, hf]).then_inc(sem(s + "w2_in"), 16)

            def store_half(hf):
                for j in range(NTOK):
                    sp.wait_ge(sem(s + "staged2"), hf * NTOK + j + 1)
                    sp.dma_start(proj_tm[j, :, hf * HALF:(hf + 1) * HALF], stage2[:, j % 2, :])\
                      .then_inc(sem(f"{s}st2_out{j % 2}"), 16)

            if l:
                tile_load(sp, s, 0, 0, wfm, None)
                tile_load(sp, s, 1, 1, wfm, None)
            h_ready(sp, l, 0, KT - 2)
            h_ready(sp, l, 0, KT - 1)
            load_half(0)
            with sp.Fori(0, 4) as i:
                for u in range(2):
                    tile_load(sp, s, i * 2 + u + 2, u, wfm, i * 2 + u + 1)
                    store(i * 2 + u, u)
            store_half(0)
            load_half(1)
            with sp.Fori(4, 7) as i:
                for u in range(2):
                    tile_load(sp, s, i * 2 + u + 2, u, wfm, i * 2 + u + 1)
                    store(i * 2 + u, u)
            for t in (NFM - 2, NFM - 1):
                store(t, t % 2)
            store_half(1)
            for u in range(2):
                sp.wait_ge(sem(f"{s}st_out{u}"), 16 * NFM // 2)
                sp.wait_ge(sem(f"{s}st2_out{u}"), 16 * NTOK)

        def proj_act(act, l):
            s = f"p{l}_"
            if l:
                rstd_act(act, norm_name(l, 0), T)
            for t in range(2):
                tile_split_act(act, s, t, t)
            norm_act(act, l, 0)
            for half in range(2):
                with act.Fori(4 * half + (half == 0), 4 * half + 4) as i:
                    for u in range(2):
                        tile_split_act(act, s, i * 2 + u, u)
                act.wait_ge(sem(s + "w2_in"), 16 * (half + 1))
                if half:
                    act.wait_ge(sem(s + "w2_free"), 1)
                act.copy(w2_hi[:], w2_raw[:]).then_inc(sem(s + "w2_hi"), 1)

        def proj_pool(pool, l):
            s = f"p{l}_"
            for t in range(2):
                tile_split_pool(pool, s, t, t)
            norm_pool(pool, l, 0)
            for half in range(2):
                with pool.Fori(4 * half + (half == 0), 4 * half + 4) as i:
                    for u in range(2):
                        tile_split_pool(pool, s, i * 2 + u, u)
                pool.wait_ge(sem(s + "w2_hi"), half + 1)
                pool.tensor_tensor(w2_lo[:], w2_raw[:], w2_hi[:], ALU.subtract).then_inc(sem(s + "w2_lo"), 1)

        def proj_pe(pe, l):
            s = f"p{l}_"
            q_tokens = T if l < DEPTH - 1 else SEQ
            pe.sem_inc(sem(s + "w_free"), 2)
            if l:
                norm_sum(pe, norm_name(l, 0), T)
            pe.wait_ge(sem(s + "w_lo"), 1)
            pe.wait_ge(sem(s + "evac"), 2)
            for u, k in FIRST_STEPS:
                if u == 0:
                    h_ready(pe, l, 0, k)
                elif k == 0:
                    pe.wait_ge(sem(s + "w_lo"), 2)
                for c, n in chunks(T):
                    o = flat[:, u * 1536 + c:u * 1536 + c + n]
                    w = slice(k * P, (k + 1) * P)
                    pe.matmul(o, w_hi[:, u, w], h_hi[:, k, c:c + n], start=(k == 0), stop=False)
                    pe.matmul(o, w_hi[:, u, w], h_lo[:, k, c:c + n], start=False, stop=False)
                    mm = pe.matmul(o, w_lo[:, u, w], h_hi[:, k, c:c + n], start=False, stop=(k == KT - 1))
                if k == KT - 1:
                    mm.then_inc(sem(s + "w_free"), 1)
            for half in range(2):
                for lo, hi, tn in ((1, 3, T), (3, 4, q_tokens)) if half == 0 else ((4, 8, q_tokens),):
                    with pe.Fori(lo, hi) as i:
                        for u in range(2):
                            tile_pe(pe, s, i * 2 + u, u, tn)
                pe.wait_ge(sem(s + "w2_lo"), half + 1)
                for j in range(NTOK):
                    pe.wait_ge(sem(s + "evac2"), half * NTOK + j + 1)
                    tok = slice(j * P, (j + 1) * P)
                    o = ps[:, 6 + j % 2, 0:HALF]
                    for k in range(KT):
                        pe.matmul(o, h_hi[:, k, tok], w2_hi[:, k, :], start=(k == 0), stop=False)
                        pe.matmul(o, h_lo[:, k, tok], w2_hi[:, k, :], start=False, stop=False)
                        mm = pe.matmul(o, h_hi[:, k, tok], w2_lo[:, k, :], start=False, stop=(k == KT - 1))
                    mm.then_inc(sem(s + "done2"), 1)
                pe.wait_ge(sem(s + "done2"), NTOK * (half + 1))
                pe.sem_inc(sem(s + "w2_free"), 1)

        def proj_dve(dve, l):
            s = f"p{l}_"
            dve.sem_inc(sem(s + "evac"), 2)
            dve.sem_inc(sem(s + "evac2"), 2)
            norm_dve(dve, l, 0)

            def tile(t, u, first):
                dve.wait_ge(sem(s + "w_free"), t + 3)
                if not first:
                    dve.wait_ge(sem(f"{s}st_out{u}"), 8 * t + (0 if u == 0 else -8))
                dve.tensor_copy(stage[:, u, :], flat[:, u * 1536:u * 1536 + T]).then_inc(sem(s + "staged"), 1)
                dve.wait_ge(sem(s + "staged"), t + 1)
                dve.sem_inc(sem(s + "evac"), 1)

            for half in range(2):
                if half == 0:
                    tile(0, 0, True)
                    tile(1, 1, True)
                with dve.Fori(4 * half + (half == 0), 4 * half + 4) as i:
                    for u in range(2):
                        tile(i * 2 + u, u, False)
                for j in range(NTOK):
                    n = half * NTOK + j
                    dve.wait_ge(sem(s + "done2"), n + 1)
                    if n >= 2:
                        dve.wait_ge(sem(f"{s}st2_out{j % 2}"), 16 * (n // 2))
                    dve.tensor_copy(stage2[:, j % 2, :], ps[:, 6 + j % 2, 0:HALF]).then_inc(sem(s + "staged2"), 1)
                    dve.wait_ge(sem(s + "staged2"), n + 1)
                    dve.sem_inc(sem(s + "evac2"), 1)

        KW = (5, 3)
        PIECES = ([(512, 256, 384), (0, 0, 256)], [(512, 0, 384)])
        KH = (4, 2)

        def att_name(l, kind):
            return f"a{l}_{kind}"

        def att_blocks(l):
            return 10 if l == 0 else 8

        def att_done(eng, l, name, blocks, per=1):
            eng.wait_ge(sem(att_name(l, 0) + name), blocks * per)

        def att_window(kind, n):
            last, off = (4, 5)[kind], 2 - kind
            return min(max(n - off, 0), last)

        def att_each(eng, l, kind, body):
            def geom(n):
                if n >= (10 if l == 0 else 8):
                    return None
                return (att_window(kind, n), True) if n < 8 else (0, False)
            for n in range(2):
                body(n, n, geom(n), geom(n + 1))
            with eng.Fori(1, 3) as i:
                for u in range(2):
                    n = i * 2 + u
                    body(n, u, (n - (2 - kind), True), (n + 1 - (2 - kind), True))
            for n in range(6, 10 if l == 0 else 8):
                body(n, n % 2, geom(n), geom(n + 1))

        def att_sp(sp, l, kind):
            s = att_name(l, kind)
            qbase = (NA_Q, WA_Q)[kind] * P
            nblk = att_blocks(l)

            def keys(kind, h):
                sk, kb = att_name(l, kind), (NA_K, WA_K)[kind] * P + 64 * h
                if kind == 1 or h >= 2:
                    att_done(sp, l, "k_lo", (h + 3 if kind else h - 1))
                for dup in range(2):
                    sp.dma_start(k_raw[64 * dup:64 * dup + 64, h % 2, :], proj_fm[kb:kb + 64, :])\
                      .then_inc(sem(f"{sk}k_in{h}"), 16)
                if kind == 1:
                    for dup in range(2):
                        for r in range(2):
                            src = kb + 32 * (1 - r)
                            sp.dma_start(k_sw[64 * dup + 32 * r:64 * dup + 32 * r + 32, h, :], proj_fm[src:src + 32, 0:SEQ])\
                              .then_inc(sem(f"{sk}k_in{h}"), 16)

            def queries(n, u):
                qsrc = proj_fm[qbase:qbase + 256, :].rearrange("(h r d) t -> r d h t", d=32, r=2)
                for dup in range(2):
                    sp.dma_start(q_blk[64 * dup:64 * dup + 64, u],
                                 proj_fm[qbase:qbase + 256, bass.ts(n, P)].rearrange("(h d) t -> d h t", d=64))\
                      .then_inc(sem(f"{s}q_in{u}"), 16)
                if kind == 1:
                    for dup in range(2):
                        for r in range(2):
                            sp.dma_start(q_swb[64 * dup + 32 * r:64 * dup + 32 * r + 32, u], qsrc[1 - r][:, :, bass.ts(n, P)])\
                              .then_inc(sem(f"{s}q_in{u}"), 16)

            def bias(n, u):
                if kind == 0:
                    sp.dma_start(bias_t[:, u:u + 1, :], io["na_bias"][l, bass.ts(n, 1)].rearrange("o p n -> p o n"))\
                      .then_inc(sem(f"{s}bias_in{u}"), 16)
                else:
                    sp.dma_start(bias_t[:, u:u + 1, 0:384], io["wa_mask"][bass.ts(n, 1)].rearrange("o p n -> p o n"))\
                      .then_inc(sem(f"{s}bias_in{u}"), 16)

            def step(n, u, more_q, more_bias):
                if more_q:
                    sp.wait_ge(sem(s + "q_split"), n + 1)
                    queries(n + 2, u)
                if more_bias:
                    sp.wait_ge(sem(s + "max"), n * HEADS + HEADS)
                    bias(n + 2, u)

            if kind == 0:
                for u in range(2):
                    sp.sem_inc(sem(f"{s}o_out{u}"), 16)
                keys(0, 0)
            for u in range(2):
                if kind == 1:
                    att_done(sp, l, "q_split", nblk - 1 + u)
                queries(u, u)
                if kind == 1:
                    att_done(sp, l, "max", 7 + u, HEADS)
                bias(u, u)
                if kind == 0 and u == 0:
                    sp.dma_start(v_att[:], proj_tm[:, :, NA_V:NA_V + 256].rearrange("j p c -> p j c")).then_inc(sem(s + "v_in"), 16)
                    keys(0, 1)
            if kind == 0:
                for h in range(2, KH[0]):
                    keys(0, h)
                sp.dma_start(rope_c[:], io["rope"][0]).then_inc(sem(att_name(l, 1) + "rope_in"), 16)
                sp.dma_start(rope_s[:], io["rope"][1]).then_inc(sem(att_name(l, 1) + "rope_in"), 16)
                sp.dma_start(wv_att[:], proj_tm[:, :, WA_V:WA_V + P].rearrange("j p c -> p j c"))\
                  .then_inc(sem(att_name(l, 1) + "v_in"), 16)
                for h in range(KH[1]):
                    keys(1, h)
            else:
                for u in range(2):
                    att_done(sp, l, f"o_out{u}", nblk // 2 + 1, 16)
                    sp.sem_inc(sem(f"{s}o_out{u}"), 16)
            with sp.Fori(0, 3) as i:
                for u in range(2):
                    step(i * 2 + u, u, True, True)
            for n in range(6, nblk):
                step(n, n % 2, n + 2 < nblk, False)
            if kind == 1:
                for u in range(2):
                    sp.wait_ge(sem(f"{s}o_out{u}"), 16 * (nblk // 2 + 1))

        def att_act(act, l, kind):
            s = att_name(l, kind)
            if kind == 0:
                act.copy(mx[:, :, 3], sinks[:, l, 1, :]).then_inc(sem(att_name(l, 1) + "sink"), 1)
                for h in range(KH[0]):
                    act.wait_ge(sem(f"{s}k_in{h}"), 32)
                    act.mul(k_hi[:, h, :], k_raw[:, h % 2, :], 0.125).then_inc(sem(s + "k_hi"), 1)

            def window_keys(step):
                if step % 4 == 2:
                    act.wait_ge(sem(att_name(l, 1) + "k_rot"), step // 4 + 1)
                    act.mul(wk_hi[:, step // 4, :], k_raw[:, step // 4, :], 0.125).then_inc(sem(att_name(l, 1) + "k_hi"), 1)

            def exps(n, u, h, nl):
                p = h % 2
                act.wait_ge(sem(s + "max"), n * HEADS + h + 1)
                if nl:
                    act.activation(Pm[:, p, 0:nl], Pm[:, p, 0:nl], ACT.Exp, bias=nmax[:, h:h + 1],
                                   accum_out=sums[:, u, h, 0:1])
                a = act.activation(Pm[:, p, nl:nl + CTX], ps[:, 2 * p, 256:512], ACT.Exp, bias=nmax[:, h:h + 1],
                                   accum_out=sums[:, u, h, 1:2])
                if kind == 1:
                    a = act.activation(sums[:, u, h, 2:3], mx[:, h, 3:4], ACT.Exp, bias=nmax[:, h:h + 1])
                a.then_inc(sem(s + "p_ready"), 1)

            def out_block(n, u):
                act.wait_ge(sem(s + "o_turned"), n + 1)
                act.wait_ge(sem(f"{s}o_out{u}"), 8 * n - 8 * u + 16)
                act.copy(o_st[:, u], ps[:, 6 + u, 256:512].rearrange("p (o t) -> p o t", o=2)).then_inc(sem(s + "o_staged"), 1)
                act.wait_ge(sem(s + "o_staged"), n + 1)
                act.dma_start(mix_fm[2 * kind:2 * kind + 2, :, bass.ts(n, P)].rearrange("o p t -> p o t"), o_st[:, u])\
                   .then_inc(sem(f"{s}o_out{u}"), 16)

            def body(n, u, here, nxt):
                nl = KW[kind] * P if here[1] else 0
                for h in range(HEADS):
                    act.wait_ge(sem(s + "turned"), n * HEADS + h + 1)
                    act.copy(PT[:, h % 2, 0:min(512, nl + CTX)], ps[:, 4, 0:min(512, nl + CTX)]).then_inc(sem(s + "pt_a"), 1)
                    if h + 2 < HEADS:
                        exps(n, u, h + 2, nl)
                    elif nxt:
                        exps(n + 1, 1 - u, h - 2, KW[kind] * P if nxt[1] else 0)
                    if h == 1 and not (isinstance(n, int) and n == 0):
                        out_block(n - 1, 1 - u)
                    if kind == 0 and isinstance(n, int) and n in (6, 7):
                        window_keys(4 * (n - 6) + h)

            for h in range(2):
                exps(0, 0, h, KW[kind] * P)
            att_each(act, l, kind, body)
            out_block(att_blocks(l) - 1, 1)

        def att_dve(dve, l, kind):
            s = att_name(l, kind)
            if kind == 0:
                for h in range(KH[0]):
                    dve.wait_ge(sem(s + "k_hi"), h + 1)
                    dve.scalar_tensor_tensor(k_lo[:, h], k_raw[:, h % 2], 0.125, k_hi[:, h], ALU.mult, ALU.subtract)\
                       .then_inc(sem(s + "k_lo"), 1)

            def window_keys(step):
                h, part = step // 4, step % 4
                sw = att_name(l, 1)
                k = k_raw[:, h, 0:SEQ]
                if part == 0:
                    dve.wait_ge(sem(sw + "rope_in"), 32)
                    dve.wait_ge(sem(f"{sw}k_in{h}"), 96)
                    dve.tensor_tensor(k, k, rope_c[:], ALU.mult).then_inc(sem(sw + "k_step"), 1)
                elif part == 1:
                    dve.tensor_tensor(k_sw[:, h], k_sw[:, h], rope_s[:], ALU.mult).then_inc(sem(sw + "k_step"), 1)
                elif part == 2:
                    dve.wait_ge(sem(sw + "k_step"), 2 * h + 2)
                    dve.tensor_tensor(k, k, k_sw[:, h], ALU.add).then_inc(sem(sw + "k_rot"), 1)
                else:
                    dve.wait_ge(sem(sw + "k_rot"), h + 1)
                    dve.wait_ge(sem(sw + "k_hi"), h + 1)
                    dve.scalar_tensor_tensor(wk_lo[:, h], k_raw[:, h], 0.125, wk_hi[:, h], ALU.mult, ALU.subtract)\
                       .then_inc(sem(sw + "k_lo"), 1)

            def maxes(n, u, h, nl):
                p = h % 2
                unit = n * HEADS + h
                if nl and h == 0:
                    dve.wait_ge(sem(f"{s}bias_in{u}"), 8 * n + (16 if u == 0 else 8))
                dve.wait_ge(sem(s + "s_done"), unit + 1)
                if not isinstance(n, int) or unit >= 2:
                    dve.wait_ge(sem(s + "turned"), unit - 1)
                dve.tensor_reduce(mx[:, h, 2:3], ps[:, 2 * p, 256:512], AX, ALU.max).then_inc(sem(s + "mx"), 1)
                k = 0
                if nl:
                    for col, off, cnt in PIECES[kind]:
                        bo = h * 640 + off if kind == 0 else off
                        dve.tensor_tensor_reduce(Pm[:, p, off:off + cnt], flat[:, 1024 * p + col:1024 * p + col + cnt],
                                                 bias_t[:, u, bo:bo + cnt], 1.0, MASKED, ALU.add, ALU.max,
                                                 mx[:, h, 1 - k:2 - k]).then_inc(sem(s + "mx"), 1)
                        k += 1
                for _ in range(2 - k):
                    dve.sem_inc(sem(s + "mx"), 1)
                dve.wait_ge(sem(s + "mx"), unit * 3 + 3)
                dve.tensor_reduce(nmax[:, h:h + 1], mx[:, h, 2 - k:3 + kind], AX, ALU.max, negate=True).then_inc(sem(s + "max"), 1)

            def body(n, u, here, nxt):
                nl = KW[kind] * P if here[1] else 0
                for h in range(HEADS):
                    if nl + CTX > 512:
                        dve.wait_ge(sem(s + "turned"), n * HEADS + h + 1)
                        dve.tensor_copy(PT[:, h % 2, 512:nl + CTX], ps[:, 5, 0:nl + CTX - 512]).then_inc(sem(s + "pt_b"), 1)
                    else:
                        dve.sem_inc(sem(s + "pt_b"), 1)
                    if h + 2 < HEADS:
                        maxes(n, u, h + 2, nl)
                    elif nxt:
                        maxes(n + 1, 1 - u, h - 2, KW[kind] * P if nxt[1] else 0)
                    if kind == 0 and isinstance(n, int) and n in (6, 7):
                        window_keys(4 * (n - 6) + h)
                dve.wait_ge(sem(s + "p_ready"), n * HEADS + HEADS)
                dve.tensor_reduce(tot[:], sums[:, u, :, 0 if here[1] else 1:2 + kind], AX, ALU.add).then_inc(sem(s + "tot"), 1)
                dve.wait_ge(sem(s + "tot"), n + 1)
                dve.reciprocal(rec[:], tot[:]).then_inc(sem(s + "rec"), 1)
                dve.wait_ge(sem(s + "rec"), n + 1)
                dve.wait_ge(sem(s + "o_done"), n + 1)
                dve.tensor_tensor(o_att[:, u, :].rearrange("p (h d) -> p h d", h=HEADS),
                                  ps[:, 6 + u, 0:256].rearrange("p (h d) -> p h d", h=HEADS),
                                  rec[:].unsqueeze(2).broadcast_to([P, HEADS, 64]), ALU.mult).then_inc(sem(s + "o_norm"), 1)

            if kind == 1:
                att_done(dve, l, "turned", att_blocks(l), HEADS)
                dve.wait_ge(sem(s + "sink"), 1)
            for h in range(2):
                maxes(0, 0, h, KW[kind] * P)
            att_each(dve, l, kind, body)

        def att_pool(pool, l, kind):
            s = att_name(l, kind)
            steps = 3 + 3 * kind
            nin = 16 * (2 + 4 * kind)
            if kind == 1:
                pool.wait_ge(sem(s + "rope_in"), 32)

            def body(n, u, here, nxt):
                st = [0]

                def chain(ins=None):
                    st[0] += 1
                    if ins is None:
                        pool.sem_inc(sem(s + "q_step"), 1)
                    else:
                        ins.then_inc(sem(s + "q_step"), 1)
                        pool.wait_ge(sem(s + "q_step"), n * steps + st[0])
                q, qsw = q_blk[:, u], q_swb[:, u]
                pool.wait_ge(sem(f"{s}q_in{u}"), (n - u) * (nin // 2) + nin)
                if kind == 1:
                    if here[1]:
                        cols = bass.ts(n, P)
                        chain(pool.tensor_tensor(q, q, rope_c[:, cols].unsqueeze(1).broadcast_to([P, HEADS, P]), ALU.mult))
                        chain(pool.tensor_tensor(qsw, qsw, rope_s[:, cols].unsqueeze(1).broadcast_to([P, HEADS, P]), ALU.mult))
                        chain(pool.tensor_tensor(q, q, qsw, ALU.add))
                    else:
                        for _ in range(3):
                            chain()
                if not isinstance(n, int) or n >= 2:
                    pool.wait_ge(sem(s + "s_done"), n * HEADS - HEADS)
                elif kind == 1:
                    att_done(pool, l, "s_done", att_blocks(l) - 1 + n, HEADS)
                chain()
                chain(pool.tensor_copy(qb[:, u], q))
                chain(pool.tensor_tensor(qb[64:P, u], q[64:P], qb[64:P, u], ALU.subtract))
                assert st[0] == steps
                pool.sem_inc(sem(s + "q_split"), 1)
            att_each(pool, l, kind, body)

        def att_pe(pe, l, kind):
            s = att_name(l, kind)
            gqa = HEADS // KH[kind]

            def scores(n, u, h, geom):
                p = h % 2
                w0, local = geom
                kh = h // gqa
                if isinstance(n, int) and n == 0:
                    pe.wait_ge(sem(s + "k_lo"), kh + 1)
                if h == 0:
                    pe.wait_ge(sem(s + "q_split"), n + 1)
                lhs = qb[:, u, h, :]
                pieces = [(256, SEQ, 256)]
                if local:
                    pieces += [(col, w0 * P + off, cnt) for col, off, cnt in PIECES[kind]]
                for col, k0, cnt in pieces:
                    o = flat[:, 1024 * p + col:1024 * p + col + cnt]
                    pe.matmul(o, lhs, (k_hi, wk_hi)[kind][:, kh, bass.ds(k0, cnt)], start=True, stop=False)
                    mm = pe.matmul(o, lhs, (k_lo, wk_lo)[kind][:, kh, bass.ds(k0, cnt)], start=False, stop=True)
                mm.then_inc(sem(s + "s_done"), 1)

            def turn(n, h, nl):
                unit = n * HEADS + h
                pe.wait_ge(sem(s + "p_ready"), unit + 1)
                if not isinstance(n, int) or unit > 0:
                    pe.wait_ge(sem(s + "pt_a"), unit)
                    pe.wait_ge(sem(s + "pt_b"), unit)
                for t in range(nl // P + 2):
                    mm = pe.transpose(ps[:, 4 + t // 4, (t % 4) * P:(t % 4 + 1) * P], Pm[:, h % 2, t * P:(t + 1) * P], ident[:])
                mm.then_inc(sem(s + "turned"), 1)

            def weigh(n, u, h, geom):
                unit = n * HEADS + h
                w0, local = geom
                nl = KW[kind] * P if local else 0
                pe.wait_ge(sem(s + "pt_a"), unit + 1)
                if h == 0:
                    pe.wait_ge(sem(s + "v_in"), 16)
                pe.wait_ge(sem(s + "pt_b"), unit + 1)
                vc = (h // gqa) * 64
                at = h * 64
                ntile = nl // P + 2
                for t in range(ntile):
                    kt = (w0 + t) if t < nl // P else SEQ // P + t - nl // P
                    mm = pe.matmul(ps[:, 6 + u, at:at + 64], PT[:, h % 2, t * P:(t + 1) * P],
                                   (v_att, wv_att)[kind][:, bass.ds(kt, 1), vc:vc + 64].rearrange("p o d -> p (o d)"),
                                   start=(t == 0), stop=(t == ntile - 1))
                if h == HEADS - 1:
                    mm.then_inc(sem(s + "o_done"), 1)

            def turn_out(n, u):
                pe.wait_ge(sem(s + "o_norm"), n + 1)
                for g in range(2):
                    mm = pe.transpose(ps[:, 6 + u, 256 + g * P:256 + (g + 1) * P], o_att[:, u, g * P:(g + 1) * P], ident[:])
                mm.then_inc(sem(s + "o_turned"), 1)

            def body(n, u, here, nxt):
                nl = KW[kind] * P if here[1] else 0
                if not isinstance(n, int) or n >= 2:
                    pe.wait_ge(sem(s + "o_staged"), n - 1)
                for h in range(HEADS):
                    turn(n, h, nl)
                    if h + 2 < HEADS:
                        scores(n, u, h + 2, here)
                    elif nxt:
                        scores(n + 1, 1 - u, h - 2, nxt)
                    if h:
                        weigh(n, u, h - 1, here)
                    elif not (isinstance(n, int) and n == 0):
                        turn_out(n - 1, 1 - u)
                weigh(n, u, HEADS - 1, here)

            for h in range(2):
                scores(0, 0, h, (att_window(kind, 0), True))
            if kind == 1:
                att_done(pe, l, "o_staged", att_blocks(l))
            att_each(pe, l, kind, body)
            turn_out(att_blocks(l) - 1, 1)

        lr = U[0:32].rearrange("p n c -> p (n c)")[:, 0:T]
        logs = [kp[:, 0], kp[:, 1], qpp[:, 1], var[:]]
        ROUNDS = ((8, 2), (0, 4), (4, 4))

        def gla_sp(sp, l):
            s = f"g{l}_"
            to = T if l == 0 else SEQ
            sp.dma_start(lr, proj_fm[LR * P:LR * P + 32, :]).then_inc(sem(s + "lr_in"), 16)
            sp.dma_start(gw[:], io["gate_w"][l].rearrange("h r c -> r h c")).then_inc(sem(s + "lr_in"), 16)
            sp.dma_start(gb[:], io["gate_b"][l]).then_inc(sem(s + "lr_in"), 16)
            sp.dma_start(smask[:], io["smask"]).then_inc(sem(s + "mask_in"), 16)
            sp.dma_start(mask_f[:], io["tri"][0]).then_inc(sem(s + "mask_in"), 16)
            sp.dma_start(mask_b[:], io["tri"][1]).then_inc(sem(s + "mask_in"), 16)

            def head(h):
                u = h % 2
                if h >= 2:
                    sp.wait_ge(sem(s + "qpp"), 2 * h - 2)
                    sp.wait_ge(sem(s + "kp"), h - 1)
                for dup in range(2):
                    half = slice(64 * dup, 64 * dup + 64)
                    for dst, base in ((kd, G_K), (qd, G_Q)):
                        sp.dma_start(dst[half, u, :], proj_fm[h * 64 + base * P:h * 64 + base * P + 64, :])\
                          .then_inc(sem(s + "qk_in"), 16)
                if h >= 2:
                    sp.wait_ge(sem(s + "o"), h - 1)
                sp.dma_start(v_g[:, u], proj_tm[:, :, h * P + G_V:h * P + G_V + P].rearrange("j p c -> p j c")).then_inc(sem(s + "v_in"), 16)
                if h >= 2:
                    sp.wait_ge(sem(s + "y"), h - 1)
                    sp.dma_start(mix_fm[4 + h - 2, :, 0:to], oT[:, h - 2, 0:to]).then_inc(sem(s + "y_out"), 16)
                sp.dma_start(gate[:, u, 0:to], proj_fm[(G_OUT + h) * P:(G_OUT + h + 1) * P, 0:to]).then_inc(sem(s + "gate_in"), 16)
                sp.wait_ge(sem(s + "qk_in"), 64 * (h + 1))
                sp.wait_ge(sem(s + "v_in"), 16 * (h + 1))
                sp.wait_ge(sem(s + "gate_in"), 16 * (h + 1))
            for h in range(HEADS):
                head(h)
            for h in range(HEADS - 2, HEADS):
                sp.wait_ge(sem(s + "y"), h + 1)
                sp.dma_start(mix_fm[4 + h, :, 0:to], oT[:, h, 0:to]).then_inc(sem(s + "y_out"), 16)
            sp.wait_ge(sem(s + "y_out"), 16 * HEADS)

        def gla_act(act, l):
            s = f"g{l}_"
            to = T if l == 0 else SEQ
            act.wait_ge(sem(s + "lr_in"), 48)

            def absolute(h):
                act.wait_ge(sem(s + "logit"), h + 1)
                at = 1536 * (h % 2)
                act.activation(logs[h], flat[:, at:at + T], ACT.Abs, bias=gb[:, h, :]).then_inc(sem(s + "abs"), 1)

            def exponential(h):
                act.wait_ge(sem(s + "abs"), h + 1)
                act.activation(logs[h], logs[h], ACT.Exp, scale=-1.0).then_inc(sem(s + "exp"), 1)

            def logs_end(heads):
                for h in heads:
                    act.wait_ge(sem(s + "exp"), h + 1)
                    act.activation(logs[h], logs[h], ACT.Ln, bias=1.0).then_inc(sem(s + "log"), 1)

            def scale(h):
                u = h % 2
                act.wait_ge(sem(s + "x"), h + 1)
                if h >= 1:
                    act.wait_ge(sem(s + "kp"), h)
                    act.wait_ge(sem(s + "qp"), 2 * h)
                act.activation(ek[:], b[:], ACT.Exp, scale=-1.0 / TAU).then_inc(sem(s + "ek"), 1)
                act.activation(eq[:], b[:], ACT.Exp, scale=1.0 / TAU).then_inc(sem(s + "eq"), 1)
                act.activation(d_ref[:, u], c_ref[:], ACT.Exp, scale=1.0 / TAU)
                act.activation(d_last[:, u], b_last[:], ACT.Exp, scale=1.0 / TAU)
                act.activation(d_lr[:, u], dif[:], ACT.Exp, scale=1.0 / TAU).then_inc(sem(s + "decay"), 1)

            def turned(h):
                for r, (t0, n) in enumerate(ROUNDS):
                    act.wait_ge(sem(s + "kt"), h * 3 + r + 1)
                    for e in range(2):
                        half = slice(64 * e, 64 * e + 64)
                        a = act.copy(kT[half, e, t0:t0 + n, :], ps[half, 5, 0:n * P].rearrange("p (j c) -> p j c", c=P))
                    a.then_inc(sem(s + "kt_out"), 1)

            def square(h):
                act.wait_ge(sem(s + "o_out"), h + 1)
                if h:
                    act.wait_ge(sem(s + "y_step"), h)
                act.activation(var[:, 0:to], oT[:, h, 0:to], ACT.Square).then_inc(sem(s + "sq"), 1)

            def silu(h):
                act.wait_ge(sem(s + "gate_in"), 16 * (h + 1))
                act.activation(gate[:, h % 2, 0:to], gate[:, h % 2, 0:to], ACT.Silu).then_inc(sem(s + "gate"), 1)

            def rstd_of(h):
                act.wait_ge(sem(s + "ssq"), h + 1)
                act.activation(var[:, 0:to], flat[:, 0:to], ACT.Ln, scale=1.0 / P, bias=eps[:]).then_inc(sem(s + "var"), 1)
                act.wait_ge(sem(s + "var"), h + 1)
                act.activation(var[:, 0:to], var[:, 0:to], ACT.Exp, scale=-0.5).then_inc(sem(s + "std"), 1)

            absolute(0)
            exponential(0)
            logs_end([0])
            for h in range(1, HEADS):
                absolute(h)
            scale(0)
            for h in range(1, HEADS):
                exponential(h)
            logs_end(range(1, HEADS))
            turned(0)
            for h in range(HEADS):
                if h:
                    square(h - 1)
                if h + 1 < HEADS:
                    scale(h + 1)
                if h:
                    rstd_of(h - 1)
                if h + 1 < HEADS:
                    turned(h + 1)
                if h:
                    silu(h - 1)
                act.wait_ge(sem(s + "o"), h + 1)
                act.mul(oT[:, h, 0:to], flat[:, 0:to], 0.125).then_inc(sem(s + "o_out"), 1)
            square(HEADS - 1)
            rstd_of(HEADS - 1)
            silu(HEADS - 1)

        def gla_pe(pe, l):
            s = f"g{l}_"
            to = T if l == 0 else SEQ
            no = to // P
            pe.wait_ge(sem(s + "lr_in"), 48)
            for h in range(HEADS):
                if h >= 2:
                    pe.wait_ge(sem(s + "abs"), h - 1)
                    pe.wait_ge(sem(s + "min"), h - 1)
                at = 1536 * (h % 2)
                for c, n in chunks(T):
                    mm = pe.matmul(flat[:, at + c:at + c + n], gw[:, h, :], lr[:, c:c + n], start=True, stop=True)
                mm.then_inc(sem(s + "logit"), 1)

            def turn(h):
                pe.wait_ge(sem(s + "kp"), h + 1)
                for r, (t0, n) in enumerate(ROUNDS):
                    if 3 * h + r:
                        pe.wait_ge(sem(s + "kt_out"), h * 3 + r)
                    for j in range(n):
                        t = t0 + j
                        mm = pe.transpose(ps[:, 5, j * P:(j + 1) * P], kp[:, h % 2, t * P:(t + 1) * P], ident[:])
                    mm.then_inc(sem(s + "kt"), 1)

            pe.wait_ge(sem(s + "abs"), HEADS)
            pe.wait_ge(sem(s + "min"), HEADS)
            pe.wait_ge(sem(s + "zeroed"), 6)
            turn(0)
            for h in range(HEADS):
                u = h % 2
                pe.wait_ge(sem(s + "v_in"), 16 * (h + 1))
                pe.wait_ge(sem(s + "zeroed"), 7)
                pe.wait_ge(sem(s + "qp"), 2 * h + 2)
                for r, (t0, n) in enumerate(ROUNDS):
                    if 3 * h + r:
                        pe.wait_ge(sem(s + "att_out"), h * 3 + r)
                    for j in range(2 * n):
                        ch = 2 * t0 + j
                        cols = slice(ch * CHUNK, (ch + 1) * CHUNK)
                        pe.matmul(ps[0:CHUNK, 6, j * CHUNK:(j + 1) * CHUNK], kp[:, u, cols], qp[:, 0, cols], start=True, stop=True)
                        mm = pe.matmul(ps[0:CHUNK, 7, j * CHUNK:(j + 1) * CHUNK], kp[:, u, cols], qp[:, 1, cols], start=True, stop=True)
                    mm.then_inc(sem(s + "att"), 1)
                    pe.wait_ge(sem(s + "kt_out"), h * 3 + r + 1)
                    if 3 * h + r:
                        pe.wait_ge(sem(s + "u_out"), h * 3 + r)
                    for j in range(n):
                        t = t0 + j
                        pe.matmul(ps[:, 3, j * P:(j + 1) * P], kT[:, 0, t, :], v_g[:, u, t, :], start=True, stop=True)
                        mm = pe.matmul(ps[:, 4, j * P:(j + 1) * P], kT[:, 1, t, :], v_g[:, u, t, :], start=True, stop=True)
                    mm.then_inc(sem(s + "u"), 1)
                    if r == 0 and h:
                        squares(pe, s, h - 1, to)
                if h + 1 < HEADS:
                    turn(h + 1)
                if h:
                    pe.wait_ge(sem(s + "var"), h)
                pe.wait_ge(sem(s + "att_out"), h * 3 + 3)
                for t in range(no):
                    o = flat[:, t * P:(t + 1) * P]
                    pe.matmul(o, v_g[:, u, t, :], att_f[:, t, :], start=(t % 4 == 0), stop=False)
                    pe.matmul(o, v_g[:, u, t, :], att_b[:, t, :], start=False, stop=False)
                pe.wait_ge(sem(s + "state_f"), (h + 1) * (NCH - 1))
                pe.wait_ge(sem(s + "state_b"), (h + 1) * (NCH - 1))
                pe.wait_ge(sem(s + "qpp"), 2 * h + 2)
                for t in range(no):
                    for e in range(2):
                        ch = 2 * t + e
                        mm = pe.matmul(flat[:, ch * CHUNK:(ch + 1) * CHUNK], S[:, ch, :],
                                       qpp[:, u, ch * CHUNK:(ch + 1) * CHUNK], start=False,
                                       stop=(e == 1 and (t % 4 == 3 or t == no - 1)))
                mm.then_inc(sem(s + "o"), 1)
            squares(pe, s, HEADS - 1, to)

        def squares(pe, s, h, to):
            pe.wait_ge(sem(s + "o_out"), h + 1)
            pe.wait_ge(sem(s + "sq"), h + 1)
            for c, n in chunks(to):
                mm = pe.matmul(flat[:, c:c + n], ones[:], var[:, c:c + n], start=True, stop=True)
            mm.then_inc(sem(s + "ssq"), 1)

        order_f = list(range(NCH_LAT, NCH)) + list(range(NCH_LAT))
        order_b = list(range(NCH - 1, NCH_LAT - 1, -1)) + list(range(NCH_LAT - 1, -1, -1))

        STEPS = ((range(0, 4), range(0, 4)), (range(4, 12), ()), (range(12, NCH - 1), range(4, NCH - 1)))

        def gla_states(dve, s, h, r):
            dve.wait_ge(sem(s + "u_out"), h * 3 + r + 1)
            steps_f, steps_b = (list(x_) for x_ in STEPS[r])
            while steps_f or steps_b:
                for half, order, name, steps in ((slice(0, 64), order_f, "state_f", steps_f), (slice(64, P), order_b, "state_b", steps_b)):
                    if steps:
                        m = steps.pop(0)
                        a, c = order[m], order[m + 1]
                        if m:
                            dve.wait_ge(sem(s + name), h * (NCH - 1) + m)
                        dve.scalar_tensor_tensor(S[half, c, :], S[half, a, :], d_last[half, h % 2, a:a + 1], U[half, a, :],
                                                 ALU.mult, ALU.add).then_inc(sem(s + name), 1)

        def gla_pool(pool, l):
            s = f"g{l}_"
            zeroed = [0]

            def zero(buf):
                if zeroed[0]:
                    pool.wait_ge(sem(s + "zeroed"), zeroed[0])
                zeroed[0] += 1
                pool.memset(buf, 0.0).then_inc(sem(s + "zeroed"), 1)
            zero(S[0:64, order_f[0], :])
            zero(S[64:P, order_b[0], :])
            zero(kT[:])
            zero(att_f[:])
            zero(att_b[:])
            zero(qp[:, 0])
            zero(qp[:, 1])
            pool.wait_ge(sem(s + "zeroed"), 7)

            def keys(h):
                pool.wait_ge(sem(s + "qk_in"), 64 * (h + 1))
                pool.wait_ge(sem(s + "ek"), h + 1)
                pool.tensor_tensor(kp[:, h % 2], kd[:, h % 2, :], ek[:], ALU.mult).then_inc(sem(s + "kp"), 1)

            def queries(h):
                u = h % 2
                pool.wait_ge(sem(s + "kp"), h + 1)
                pool.wait_ge(sem(s + "eq"), h + 1)
                if h:
                    pool.wait_ge(sem(s + "att"), 3 * h)
                for e in range(2):
                    half = slice(64 * e, 64 * e + 64)
                    pool.tensor_tensor(qp[half, e], qd[half, u, :], eq[half], ALU.mult).then_inc(sem(s + "qp"), 1)
                    pool.wait_ge(sem(s + "qp"), 2 * h + e + 1)
                pool.wait_ge(sem(s + "decay"), h + 1)
                for e in range(2):
                    half = slice(64 * e, 64 * e + 64)
                    pool.tensor_tensor(qpp[half, u].rearrange("p (n c) -> p n c", c=CHUNK), qp[half, e].rearrange("p (n c) -> p n c", c=CHUNK),
                                       d_ref[half, u].unsqueeze(2).broadcast_to([64, NCH, CHUNK]), ALU.mult).then_inc(sem(s + "qpp"), 1)
                    pool.wait_ge(sem(s + "qpp"), 2 * h + e + 1)
            pool.wait_ge(sem(s + "sub"), 1)
            keys(0)
            queries(0)
            pool.wait_ge(sem(s + "sub"), HEADS)
            for h in range(1, HEADS):
                keys(h)
                queries(h)

        def gla_dve(dve, l):
            s = f"g{l}_"
            to = T if l == 0 else SEQ
            dve.wait_ge(sem(s + "lr_in"), 48)

            def minimum(h):
                dve.wait_ge(sem(s + "logit"), h + 1)
                dve.wait_ge(sem(s + "abs"), h + 1)
                at = 1536 * (h % 2)
                dve.tensor_scalar(oT[:, h, :], flat[:, at:at + T], gb[:, h, :], 0.0, ALU.add, ALU.min).then_inc(sem(s + "min"), 1)

            def log_decay(h):
                dve.wait_ge(sem(s + "log"), h + 1)
                dve.wait_ge(sem(s + "min"), h + 1)
                dve.tensor_tensor(oT[:, h, :], oT[:, h, :], logs[h], ALU.subtract).then_inc(sem(s + "sub"), 1)
            bc = b[:].rearrange("p (n c) -> p n c", c=CHUNK)
            mid = CHUNK // 2
            st = [0]

            def chain(ins):
                st[0] += 1
                ins.then_inc(sem(s + "dve_step"), 1)
                dve.wait_ge(sem(s + "dve_step"), st[0])

            def scan(h):
                g = oT[:, h, :]
                dve.wait_ge(sem(s + "sub"), h + 1)
                if h == 0:
                    dve.wait_ge(sem(s + "mask_in"), 48)
                else:
                    dve.wait_ge(sem(s + "decay"), h)
                chain(dve.tensor_tensor_scan(b[0:64, :], smask[0:64, :], g[0:64, :], 0.0, ALU.mult, ALU.add))
                chain(dve.tensor_tensor_scan(b[64:P, ::-1], smask[64:P, ::-1], g[64:P, ::-1], 0.0, ALU.mult, ALU.add))

            def against_middle():
                chain(dve.tensor_copy(c_ref[0:64, :], bc[0:64, :, mid - 1]))
                chain(dve.tensor_copy(c_ref[64:P, :], bc[64:P, :, mid]))
                chain(dve.tensor_copy(b_last[0:64, :], bc[0:64, :, CHUNK - 1]))
                chain(dve.tensor_copy(b_last[64:P, :], bc[64:P, :, 0]))
                chain(dve.tensor_tensor(dif[:], b_last[:], c_ref[:], ALU.subtract))
                chain(dve.tensor_tensor(bc, bc, c_ref[:].unsqueeze(2).broadcast_to([P, NCH, CHUNK]), ALU.subtract))
                dve.tensor_scalar(b[:], b[:], -CLAMP, CLAMP, ALU.max, ALU.min).then_inc(sem(s + "x"), 1)

            U2 = U[:].rearrange("p (j e) c -> p j e c", e=2)

            def round_out(h, r, t0, n):
                dve.wait_ge(sem(s + "att"), h * 3 + r + 1)
                for dst, bank, m in ((att_f, 6, mask_f), (att_b, 7, mask_b)):
                    src = ps[0:CHUNK, bank, 0:2 * n * CHUNK].rearrange("p (j e c) -> p j e c", e=2, c=CHUNK)
                    for e in range(2):
                        ins = dve.tensor_tensor(dst[64 * e:64 * e + 64, t0:t0 + n, 64 * e:64 * e + 64],
                                                src[:, :, e, :], m[:].unsqueeze(1).broadcast_to([CHUNK, n, CHUNK]), ALU.mult)
                ins.then_inc(sem(s + "att_out"), 1)
                dve.wait_ge(sem(s + "u"), h * 3 + r + 1)
                d2 = d_lr[:, h % 2].rearrange("p (j e) -> p j e", e=2)
                for e in range(2):
                    ins = dve.tensor_tensor(U2[:, t0:t0 + n, e, :],
                                            ps[:, 3 + e, 0:n * P].rearrange("p (j c) -> p j c", c=P),
                                            d2[:, t0:t0 + n, e].unsqueeze(2).broadcast_to([P, n, P]), ALU.mult)
                ins.then_inc(sem(s + "u_out"), 1)

            def finish(h):
                o = oT[:, h, 0:to]
                dve.wait_ge(sem(s + "std"), h + 1)
                dve.tensor_tensor(o, o, var[:, 0:to], ALU.mult).then_inc(sem(s + "y_step"), 1)
                dve.wait_ge(sem(s + "y_step"), h + 1)
                dve.wait_ge(sem(s + "gate"), h + 1)
                dve.scalar_tensor_tensor(o, o, gla_gain[:, l:l + 1], gate[:, h % 2, 0:to], ALU.mult, ALU.mult)\
                   .then_inc(sem(s + "y"), 1)

            minimum(0)
            log_decay(0)
            minimum(1)
            scan(0)
            against_middle()
            for h in range(2, HEADS):
                minimum(h)
            for h in range(1, HEADS):
                log_decay(h)
            dve.wait_ge(sem(s + "zeroed"), 7)
            for h in range(HEADS):
                dve.wait_ge(sem(s + "decay"), h + 1)
                if h + 1 < HEADS:
                    scan(h + 1)
                    against_middle()
                if h:
                    dve.wait_ge(sem(s + "o"), h)
                for r, (t0, n) in enumerate(ROUNDS):
                    round_out(h, r, t0, n)
                    gla_states(dve, s, h, r)
                if h:
                    finish(h - 1)
            finish(HEADS - 1)

        def wo_tn(l):
            return T if l == 0 else SEQ

        def wo_sp(sp, l):
            s = f"o{l}_"
            tn = wo_tn(l)
            src = io["w_out"][l]

            def load(t, u):
                sp.dma_start(ow_raw[:, u:u + 1, :], src[bass.ts(t, 1)].rearrange("o p n -> p o n")).then_inc(sem(f"{s}w_in{u}"), 16)
            load(0, 0)
            for k in range(KT):
                sp.dma_start(y_raw[:, k, 0:tn], mix_fm[k, :, 0:tn]).then_inc(sem(f"{s}y_in{k}"), 16)
                if k == 1:
                    load(1, 1)
            with sp.Fori(0, 3) as i:
                for u in range(2):
                    sp.wait_ge(sem(s + "w_lo"), i * 2 + u + 1)
                    load(i * 2 + u + 2, u)

        def wo_act(act, l):
            s = f"o{l}_"
            tn = wo_tn(l)

            def split(t, u):
                act.wait_ge(sem(f"{s}w_in{u}"), 8 * t + (16 if u == 0 else 8))
                if not isinstance(t, int):
                    act.wait_ge(sem(s + "tile"), t - 1)
                act.copy(ow_hi[:, u, :], ow_raw[:, u, :]).then_inc(sem(s + "w_hi"), 1)

            def square(t, u):
                act.wait_ge(sem(s + "evac"), t + 1)
                act.wait_ge(sem(s + "added"), t + 1)
                act.activation(sq[:, u, 0:tn], x[:, bass.ts(t, 1), 0:tn].rearrange("p o n -> p (o n)"), ACT.Square)\
                   .then_inc(sem(s + "sq"), 1)
            split(0, 0)
            for k in range(KT):
                act.wait_ge(sem(f"{s}y_in{k}"), 16)
                act.copy(h_hi[:, k, 0:tn], y_raw[:, k, 0:tn]).then_inc(sem(s + "y_hi"), 1)
                if k == 1:
                    split(1, 1)
            with act.Fori(1, 4) as i:
                for u in range(2):
                    split(i * 2 + u, u)
                    square(i * 2 + u - 2, u)
            for u in range(2):
                square(6 + u, u)

        def wo_pool(pool, l):
            s = f"o{l}_"
            tn = wo_tn(l)
            pool.memset(rstd[:, 0:tn], 0.0).then_inc(sem(s + "added"), 2)

            def split(t, u):
                pool.wait_ge(sem(s + "w_hi"), t + 1)
                pool.tensor_tensor(ow_lo[:, u, :], ow_raw[:, u, :], ow_hi[:, u, :], ALU.subtract).then_inc(sem(s + "w_lo"), 1)

            def add(t, u):
                pool.wait_ge(sem(s + "sq"), t + 1)
                pool.wait_ge(sem(s + "added"), t + 2)
                pool.tensor_tensor(rstd[:, 0:tn], rstd[:, 0:tn], sq[:, u, 0:tn], ALU.add).then_inc(sem(s + "added"), 1)
            for u in range(2):
                split(u, u)
            with pool.Fori(1, 4) as i:
                for u in range(2):
                    split(i * 2 + u, u)
                    add(i * 2 + u - 2, u)
            add(KT - 2, 0)

        def wo_pe(pe, l):
            s = f"o{l}_"
            tn = wo_tn(l)

            def step(u, k):
                w = slice(k * P, (k + 1) * P)
                for c, n in chunks(tn):
                    o = flat[:, u * 1536 + c:u * 1536 + c + n]
                    pe.matmul(o, ow_hi[:, u, w], h_hi[:, k, c:c + n], start=(k == 0), stop=False)
                    pe.matmul(o, ow_hi[:, u, w], h_lo[:, k, c:c + n], start=False, stop=False)
                    mm = pe.matmul(o, ow_lo[:, u, w], h_hi[:, k, c:c + n], start=False, stop=(k == KT - 1))
                if k == KT - 1:
                    mm.then_inc(sem(s + "tile"), 1)

            pe.wait_ge(sem(s + "w_lo"), 1)
            for k in range(KT + 2):
                if k < KT:
                    pe.wait_ge(sem(s + "y_lo"), k + 1)
                    step(0, k)
                if k == 2:
                    pe.wait_ge(sem(s + "w_lo"), 2)
                if k >= 2:
                    step(1, k - 2)
            with pe.Fori(1, 4) as i:
                for u in range(2):
                    pe.wait_ge(sem(s + "w_lo"), i * 2 + u + 1)
                    pe.wait_ge(sem(s + "evac"), i * 2 + u - 1)
                    for k in range(KT):
                        step(u, k)

        def wo_dve(dve, l):
            s = f"o{l}_"
            tn = wo_tn(l)
            for k in range(KT):
                dve.wait_ge(sem(s + "y_hi"), k + 1)
                dve.tensor_tensor(h_lo[:, k, 0:tn], y_raw[:, k, 0:tn], h_hi[:, k, 0:tn], ALU.subtract)\
                   .then_inc(sem(s + "y_lo"), 1)
            with dve.Fori(0, 4) as i:
                for u in range(2):
                    t = i * 2 + u
                    dve.wait_ge(sem(s + "tile"), t + 1)
                    for c, n, g in segments(tn):
                        xs = x[:, bass.ts(t, 1), c:c + n].rearrange("p o n -> p (o n)")
                        ins = dve.scalar_tensor_tensor(xs, flat[:, u * 1536 + c:u * 1536 + c + n],
                                                       mod[:, bass.ds(t + l * 48 + 2 * KT, 1), g:g + 1].rearrange("p o n -> p (o n)"),
                                                       xs, ALU.mult, ALU.add)
                    ins.then_inc(sem(s + "evac"), 1)
            dve.wait_ge(sem(s + "sq"), KT)
            dve.wait_ge(sem(s + "added"), 2 + KT - 1)
            dve.tensor_tensor(rstd[:, 0:tn], rstd[:, 0:tn], sq[:, 1, 0:tn], ALU.add)

        GATE, VALUE, DOWN = 0, 1, 2

        def ffn_downs(tn):
            return [(m, c, n) for c, n in chunks(tn) for m in range(KT)]

        SQ_SLOTS = {"added": 4, "added_dve": 2}

        def add_of(tn, m, c):
            if c == chunks(tn)[-1][0]:
                return "added_dve", m - 1
            return "added", c // 512 * (KT - 1) + m - 1

        def sq_slot(own, i, n):
            half = slice(i % 2 * 512, i % 2 * 512 + n)
            return fw_raw[:, VALUE if own == "added_dve" else (GATE, DOWN)[i // 2 % 2], half]

        def square_add(eng, s, tn, d):
            m, c, n = ffn_downs(tn)[d]
            own, i = add_of(tn, m, c)
            eng.wait_ge(sem(s + "sq"), d + 1)
            if i:
                eng.wait_ge(sem(s + own), i)
            eng.tensor_tensor(rstd[:, c:c + n], rstd[:, c:c + n], sq_slot(own, i, n), ALU.add).then_inc(sem(s + own), 1)

        def ffn_sp(sp, l):
            s = f"u{l}_"
            with sp.Fori(0, NFF) as i:
                for kind in range(3):
                    src = io["w_up"][l] if kind < 2 else io["w_down"][l]
                    at = i * 2 + kind if kind < 2 else i
                    sp.wait_ge(sem(f"{s}raw_free{kind}"), i + 1)
                    sp.dma_start(fw_raw[:, kind:kind + 1, :], src[bass.ts(at, 1)].rearrange("o p n -> p o n"))\
                      .then_inc(sem(f"{s}w_in{kind}"), 16)

        def ffn_loop(eng, tile):
            tile(0, 0, False, False)
            with eng.Fori(0, NFF // 2 - 1) as i:
                tile(i * 2 + 1, 1, True, False)
                tile(i * 2 + 2, 0, True, False)
            tile(NFF - 1, 1, True, True)

        def ffn_act(act, l):
            s = f"u{l}_"
            tn = wo_tn(l)

            def split(i, kind, slot):
                act.wait_ge(sem(f"{s}w_in{kind}"), i * 16 + 16)
                act.wait_ge(sem(s + ("gate_free" if kind == GATE else "tile_free")), i + 1)
                act.copy(fw_hi[:, slot, :], fw_raw[:, kind, :]).then_inc(sem(f"{s}w_hi{kind}"), 1)

            def tile(i, u, down, last):
                if not isinstance(i, int) or i > 0:
                    split(i, VALUE, 1)
                    split(i, DOWN, 2 + u)
                for j, (c, n) in enumerate(chunks(tn)):
                    act.wait_ge(sem(f"{s}gate{j}"), i + 1)
                    if j == 0:
                        act.wait_ge(sem(s + "conv_free"), i + 1)
                    at = c + 1 if c < SEQ else c + 3
                    act.copy(G[:, at:at + n], ps[:, j, 0:n]).then_inc(sem(s + "g_out"), 1)
                if not last:
                    split(i + 1, GATE, 0)
                act.wait_ge(sem(s + "conv"), i + 1)
                act.activation(cv[:, 1:tn + 3 if tn > SEQ else tn + 1], cv[:, 1:tn + 3 if tn > SEQ else tn + 1], ACT.Gelu,
                               bias=conv_b[:, l, bass.ds(i, 1)]).then_inc(sem(s + "gelu"), 1)
                for j, (c, n) in enumerate(chunks(tn)):
                    act.wait_ge(sem(f"{s}hid{j}"), i + 1)
                    if j == 0:
                        act.wait_ge(sem(s + "tile_free"), i + 1)
                    at = c + 1 if c < SEQ else c + 3
                    act.copy(hid_hi[:, u, c:c + n], cv[:, at:at + n]).then_inc(sem(f"{s}hid_hi{j}"), 1)

            rstd_act(act, norm_name(l, 1), tn)
            split(0, GATE, 0)
            split(0, VALUE, 1)
            norm_act(act, l, 1)
            split(0, DOWN, 2)
            act.wait_ge(sem(s + "pads"), 1)
            ffn_loop(act, tile)

            for kind in (GATE, VALUE, DOWN):
                act.wait_ge(sem(f"{s}w_lo{kind}"), NFF)
            downs = ffn_downs(tn)
            for d, (m, c, n) in enumerate(downs):
                act.wait_ge(sem(s + "down_out"), 2 + (NFF - 1) * len(downs) + d + 1)
                dst = rstd[:, c:c + n]
                if m:
                    own, i = add_of(tn, m, c)
                    if i >= SQ_SLOTS[own]:
                        act.wait_ge(sem(s + own), i - SQ_SLOTS[own] + 1)
                    dst = sq_slot(own, i, n)
                act.activation(dst, x[:, m, c:c + n], ACT.Square).then_inc(sem(s + "sq"), 1)

        def ffn_pool(pool, l):
            s = f"u{l}_"
            tn = wo_tn(l)
            pool.sem_inc(sem(s + "conv_free"), 1)
            for kind in range(3):
                pool.sem_inc(sem(f"{s}raw_free{kind}"), 1)

            def split(i, kind, slot):
                pool.wait_ge(sem(f"{s}w_hi{kind}"), i + 1)
                pool.tensor_tensor(fw_lo[:, slot, :], fw_raw[:, kind, :], fw_hi[:, slot, :], ALU.subtract)\
                    .then_inc(sem(f"{s}w_lo{kind}"), 1)
                pool.wait_ge(sem(f"{s}w_lo{kind}"), i + 1)
                pool.sem_inc(sem(f"{s}raw_free{kind}"), 1)

            def tile(i, u, down, last):
                if not isinstance(i, int) or i > 0:
                    split(i, VALUE, 1)
                    split(i, DOWN, 2 + u)
                if not last:
                    split(i + 1, GATE, 0)
                for j, (c, n) in enumerate(chunks(tn)):
                    at = c + 1 if c < SEQ else c + 3
                    pool.wait_ge(sem(f"{s}hid_hi{j}"), i + 1)
                    pool.tensor_tensor(hid_lo[:, u, c:c + n], cv[:, at:at + n], hid_hi[:, u, c:c + n], ALU.subtract)\
                        .then_inc(sem(f"{s}hid_lo{j}"), 1)
                pool.wait_ge(sem(f"{s}hid_lo{len(chunks(tn)) - 1}"), i + 1)
                pool.sem_inc(sem(s + "conv_free"), 1)

            split(0, GATE, 0)
            split(0, VALUE, 1)
            norm_pool(pool, l, 1)
            h_ready(pool, l, 1, KT - 2)
            h_ready(pool, l, 1, KT - 1)
            pool.memset(G[:], 0.0).then_inc(sem(s + "pads"), 1)
            split(0, DOWN, 2)
            ffn_loop(pool, tile)
            for d, (m, c, n) in enumerate(ffn_downs(tn)):
                if m and c != chunks(tn)[-1][0]:
                    square_add(pool, s, tn, d)

        def ffn_pe(pe, l):
            s = f"u{l}_"
            tn = wo_tn(l)
            cs = chunks(tn)
            downs = ffn_downs(tn)
            nd = len(downs)
            pe.sem_inc(sem(s + "gate_free"), 1)
            pe.sem_inc(sem(s + "tile_free"), 1)
            norm_sum(pe, norm_name(l, 1), tn)

            def down(i, u, d):
                m, c, n = downs[d]
                if d == 0:
                    pe.wait_ge(sem(f"{s}w_lo{DOWN}"), i + 1)
                if m == 0:
                    pe.wait_ge(sem(f"{s}hid_lo{c // 512}"), i + 1)
                pe.wait_ge(sem(s + "down_out"), i * nd + d + 1)
                o = ps[:, 6 + d % 2, 0:n]
                wc = slice(m * P, (m + 1) * P)
                pe.matmul(o, fw_hi[:, 2 + u, wc], hid_hi[:, u, c:c + n], start=True, stop=False)
                pe.matmul(o, fw_hi[:, 2 + u, wc], hid_lo[:, u, c:c + n], start=False, stop=False)
                pe.matmul(o, fw_lo[:, 2 + u, wc], hid_hi[:, u, c:c + n], start=False, stop=True).then_inc(sem(s + "down"), 1)

            def first_tile():
                def step(kind, k):
                    w = slice(k * P, (k + 1) * P)
                    for j, (c, n) in enumerate(cs):
                        o = ps[:, 3 * kind + j, 0:n]
                        pe.matmul(o, fw_hi[:, kind, w], h_hi[:, k, c:c + n], start=(k == 0), stop=False)
                        pe.matmul(o, fw_hi[:, kind, w], h_lo[:, k, c:c + n], start=False, stop=False)
                        mm = pe.matmul(o, fw_lo[:, kind, w], h_hi[:, k, c:c + n], start=False, stop=(k == KT - 1))
                        if k == KT - 1:
                            mm.then_inc(sem(f"{s}gate{j}" if kind == GATE else f"{s}value{j}"), 1)
                pe.wait_ge(sem(f"{s}w_lo{GATE}"), 1)
                for kind, k in FIRST_STEPS:
                    if kind == GATE:
                        h_ready(pe, l, 1, k)
                    elif k == 0:
                        pe.wait_ge(sem(f"{s}w_lo{VALUE}"), 1)
                    step(kind, k)
                    if (kind, k) == (VALUE, 3):
                        pe.wait_ge(sem(f"{s}gate{len(cs) - 1}"), 1)
                        pe.sem_inc(sem(s + "gate_free"), 1)

            def tile(i, u, with_down, last):
                if isinstance(i, int) and i == 0:
                    return first_tile()
                d = 0
                for kind in (GATE, VALUE):
                    pe.wait_ge(sem(f"{s}w_lo{kind}"), i + 1)
                    wh = fw_hi[:, kind, :].rearrange("p (k m) -> p k m", m=P)
                    wl = fw_lo[:, kind, :].rearrange("p (k m) -> p k m", m=P)
                    for j, (c, n) in enumerate(cs):
                        if kind == GATE:
                            if not isinstance(i, int) or i > 0:
                                pe.wait_ge(sem(s + "g_out"), i * len(cs) - len(cs) + j + 1)
                        elif not isinstance(i, int) or i > 0:
                            pe.wait_ge(sem(f"{s}hid{j}"), i)
                        o = ps[:, 3 * kind + j, 0:n]
                        for k in range(KT):
                            pe.matmul(o, wh[:, k], h_hi[:, k, c:c + n], start=(k == 0), stop=False)
                            pe.matmul(o, wh[:, k], h_lo[:, k, c:c + n], start=False, stop=False)
                            mm = pe.matmul(o, wl[:, k], h_hi[:, k, c:c + n], start=False, stop=(k == KT - 1))
                            if k == KT - 1:
                                mm.then_inc(sem(f"{s}gate{j}" if kind == GATE else f"{s}value{j}"), 1)
                            if k % 2 == 0 and with_down:
                                down(i - 1, 1 - u, d)
                                d += 1
                            if j == 0 and k == 1 and kind == GATE:
                                pe.wait_ge(sem(f"{s}value{len(cs) - 1}"), i)
                                pe.sem_inc(sem(s + "tile_free"), 1)
                            if j == 0 and k == 1 and kind == VALUE:
                                pe.wait_ge(sem(f"{s}gate{len(cs) - 1}"), i + 1)
                                pe.sem_inc(sem(s + "gate_free"), 1)
            ffn_loop(pe, tile)
            for d in range(nd):
                down(NFF - 1, 1, d)

        def ffn_dve(dve, l):
            s = f"u{l}_"
            tn = wo_tn(l)
            cs = chunks(tn)
            downs = ffn_downs(tn)
            nd = len(downs)
            wide = tn + 2 if tn > SEQ else tn
            dve.sem_inc(sem(s + "down_out"), 2)
            norm_dve(dve, l, 1)

            def down(i, d):
                m, c, n = downs[d]
                g = int(c >= SEQ)
                dve.wait_ge(sem(s + "down"), i * nd + d + 1)
                at = l * 48 + 5 * KT + m
                dve.scalar_tensor_tensor(x[:, m, c:c + n], ps[:, 6 + d % 2, 0:n], mod[:, at, g:g + 1], x[:, m, c:c + n],
                                         ALU.mult, ALU.add).then_inc(sem(s + "down_out"), 1)

            def tile(i, u, with_down, last):
                todo = list(range(nd)) if with_down else []

                def some(k):
                    for _ in range(min(k, len(todo))):
                        down(i - 1, todo.pop(0))
                some(nd // 2)
                dve.wait_ge(sem(s + "g_out"), i * len(cs) + len(cs))
                dve.wait_ge(sem(s + "conv_free"), i + 1)
                for tap, src in ((1, 1), (0, 0), (2, 2)):
                    wt = conv_w[:, l, bass.ds(i, 1), tap:tap + 1].rearrange("p o n -> p (o n)")
                    if tap == 1:
                        ins = dve.tensor_scalar(cv[:, 1:1 + wide], G[:, src:src + wide], wt, None, ALU.mult)
                    else:
                        ins = dve.scalar_tensor_tensor(cv[:, 1:1 + wide], G[:, src:src + wide], wt, cv[:, 1:1 + wide],
                                                       ALU.mult, ALU.add)
                    if tap == 2:
                        ins.then_inc(sem(s + "conv"), 1)
                    else:
                        ins.then_inc(sem(s + "conv_step"), 1)
                        dve.wait_ge(sem(s + "conv_step"), i * 2 + 1 + (tap == 0))
                    some(1)
                some(1)
                for j, (c, n) in enumerate(cs):
                    at = c + 1 if c < SEQ else c + 3
                    dve.wait_ge(sem(f"{s}value{j}"), i + 1)
                    dve.wait_ge(sem(s + "gelu"), i + 1)
                    dve.tensor_tensor(cv[:, at:at + n], cv[:, at:at + n], ps[:, 3 + j, 0:n], ALU.mult)\
                       .then_inc(sem(f"{s}hid{j}"), 1)
                    some(4 if j < len(cs) - 1 else nd)
            ffn_loop(dve, tile)
            for d in range(nd + 2):
                if d < nd:
                    down(NFF - 1, d)
                if d - 2 > nd - KT:
                    square_add(dve, s, tn, d - 2)

        def last_pe(pe):
            norm_sum(pe, "last_", SEQ)

        def last_act(act):
            rstd_act(act, "last_", SEQ)

        def last_dve(dve):
            dve.wait_ge(sem("last_rstd"), 1)
            for k in range(KT):
                if k >= OUT_SLOTS:
                    dve.wait_ge(sem(f"last_out{k % OUT_SLOTS}"), 16 * (k // OUT_SLOTS))
                dve.scalar_tensor_tensor(fo[:, k % OUT_SLOTS, :], x[:, k, 0:SEQ], gains[:, 2 * DEPTH, k:k + 1], rstd[:, 0:SEQ],
                                         ALU.mult, ALU.mult).then_inc(sem("last_y"), 1)

        def last_sp(sp):
            for k in range(KT):
                sp.wait_ge(sem("last_y"), k + 1)
                sp.dma_start(out[k], fo[:, k % OUT_SLOTS, :]).then_inc(sem(f"last_out{k % OUT_SLOTS}"), 16)
            for u in range(OUT_SLOTS):
                sp.wait_ge(sem(f"last_out{u}"), 16 * KT // OUT_SLOTS)

        @block.sync
        def _(sp):
            mod_sp(sp)
            end_phase(sp, "sp")
            for l in range(DEPTH):
                proj_sp(sp, l)
                end_phase(sp, "sp", f"p{l}")
                att_sp(sp, l, 0)
                att_sp(sp, l, 1)
                end_phase(sp, "sp", f"a{l}")
                gla_sp(sp, l)
                end_phase(sp, "sp", f"g{l}")
                wo_sp(sp, l)
                end_phase(sp, "sp", f"o{l}")
                ffn_sp(sp, l)
                end_phase(sp, "sp", f"u{l}")
            last_sp(sp)

        @block.scalar
        def _(act):
            mod_act(act)
            end_phase(act, "act")
            for l in range(DEPTH):
                proj_act(act, l)
                end_phase(act, "act", f"p{l}")
                att_act(act, l, 0)
                att_act(act, l, 1)
                end_phase(act, "act", f"a{l}")
                gla_act(act, l)
                end_phase(act, "act", f"g{l}")
                wo_act(act, l)
                end_phase(act, "act", f"o{l}")
                ffn_act(act, l)
                end_phase(act, "act", f"u{l}")
            last_act(act)

        @block.tensor
        def _(pe):
            mod_pe(pe)
            end_phase(pe, "pe")
            for l in range(DEPTH):
                proj_pe(pe, l)
                end_phase(pe, "pe", f"p{l}")
                att_pe(pe, l, 0)
                att_pe(pe, l, 1)
                end_phase(pe, "pe", f"a{l}")
                gla_pe(pe, l)
                end_phase(pe, "pe", f"g{l}")
                wo_pe(pe, l)
                end_phase(pe, "pe", f"o{l}")
                ffn_pe(pe, l)
                end_phase(pe, "pe", f"u{l}")
            last_pe(pe)

        @block.vector
        def _(dve):
            mod_dve(dve)
            end_phase(dve, "dve")
            for l in range(DEPTH):
                proj_dve(dve, l)
                end_phase(dve, "dve", f"p{l}")
                att_dve(dve, l, 0)
                att_dve(dve, l, 1)
                end_phase(dve, "dve", f"a{l}")
                gla_dve(dve, l)
                end_phase(dve, "dve", f"g{l}")
                wo_dve(dve, l)
                end_phase(dve, "dve", f"o{l}")
                ffn_dve(dve, l)
                end_phase(dve, "dve", f"u{l}")
            last_dve(dve)

        @block.gpsimd
        def _(pool):
            mod_pool(pool)
            end_phase(pool, "pool")
            for l in range(DEPTH):
                proj_pool(pool, l)
                end_phase(pool, "pool", f"p{l}")
                att_pool(pool, l, 0)
                att_pool(pool, l, 1)
                end_phase(pool, "pool", f"a{l}")
                gla_pool(pool, l)
                end_phase(pool, "pool", f"g{l}")
                wo_pool(pool, l)
                end_phase(pool, "pool", f"o{l}")
                ffn_pool(pool, l)
                end_phase(pool, "pool", f"u{l}")


def lay_out(inp):
    a = {k: np.asarray(v) for k, v in inp.items()}
    c = np.ascontiguousarray
    L = DEPTH
    io = {}
    io["xT"] = c(np.concatenate([a["x"][0], a["ctx"][0]], 0).T.reshape(KT, P, T).transpose(1, 0, 2))
    io["cc"] = c(np.stack([a["c"][0], a["c_ctx"]], -1).reshape(KT, P, 2).transpose(1, 0, 2))
    io["w_mod"] = c(a["w_mod"].reshape(L, KT, P, 12, 512).transpose(0, 3, 2, 1, 4).reshape(L * 12, P, KT, 512))
    io["b_mod"] = c(a["b_mod"].reshape(L * 48, P).T)
    g = np.stack([a[n][l] for l in range(L) for n in ("norm1_g", "norm2_g")] + [a["final_norm_g"]])
    io["gains"] = c(g.reshape(2 * L + 1, KT, P).transpose(2, 0, 1))
    w = a["w_in"]
    at, cut = 0, {}
    for name, n in (("na_q", 256), ("na_k", 256), ("na_v", 256), ("wa_q", 256), ("wa_k", 128), ("wa_v", 128),
                    ("g_q", 256), ("g_k", 256), ("g_v", 512), ("g_out", 512), ("lr", 32)):
        cut[name] = w[:, :, at:at + n]
        at += n
    pad = np.zeros((L, D, P - 32), w.dtype)
    fm = np.concatenate([cut["na_k"], cut["wa_k"], cut["g_k"], cut["lr"], pad, cut["na_q"], cut["wa_q"], cut["g_q"], cut["g_out"]], -1)
    io["w_fm"] = c(fm.reshape(L, KT, P, NFM, P).transpose(0, 3, 2, 1, 4).reshape(L, NFM, P, KT * P))
    tm = np.concatenate([cut["na_v"], cut["wa_v"], cut["g_v"]], -1)
    io["w_tm"] = c(tm.reshape(L, KT, P, 2, HALF).transpose(0, 3, 2, 1, 4))
    io["w_out"] = c(a["w_out"].reshape(L, KT, P, KT, P).transpose(0, 3, 2, 1, 4).reshape(L, KT, P, KT * P))
    up = a["ffn_w_up"].reshape(L, KT, P, 2, NFF, P)[:, :, :, ::-1]
    io["w_up"] = c(up.transpose(0, 4, 3, 2, 1, 5).reshape(L, NFF * 2, P, KT * P))
    io["w_down"] = c(a["ffn_w_down"].reshape(L, NFF, P, D))
    io["conv_w"] = c(a["ffn_conv_w"].reshape(L, 3, NFF, P).transpose(3, 0, 2, 1))
    io["conv_b"] = c(a["ffn_conv_b"].reshape(L, NFF, P).transpose(2, 0, 1))
    io["gla_gain"] = c(a["gla_norm_g"].T)
    gw = np.zeros((L, HEADS, 32, P), np.float32)
    gb = np.zeros((L, P, HEADS, 1), np.float32)
    for h in range(HEADS):
        for d in range(2):
            gw[:, h, 16 * d:16 * d + 16, 64 * d:64 * d + 64] = a["gla_gate_w"][:, d, :, 64 * h:64 * h + 64]
            gb[:, 64 * d:64 * d + 64, h, 0] = a["gla_gate_b"][:, d, 64 * h:64 * h + 64]
    io["gate_w"], io["gate_b"] = gw, gb
    sk = np.full((L, 2, HEADS), MASKED, np.float32)
    sk[:, 1] = a["wa_sink"]
    io["sinks"] = c(np.broadcast_to(sk[None], (P, L, 2, HEADS)))
    rpb = a["na_rpb"]
    nb = np.full((L, 8, P, HEADS, 10, 64), MASKED, np.float32)
    col = np.arange(64)
    cs = np.clip(col - 8, 0, 48)
    inside = (col[None, :] >= cs[:, None]) & (col[None, :] < cs[:, None] + 16)
    off = np.where(inside, col[None, :] - col[:, None] + 15, 0)
    for j in range(8):
        w0 = min(max(j - 2, 0), 4) * 2
        for e in range(2):
            r = 2 * j + e
            rs = min(max(r - 4, 0), 8)
            for kr in range(rs, rs + 8):
                v = rpb[:, :, kr - r + 7, :][:, :, off]
                nb[:, j, 64 * e:64 * e + 64, :, kr - w0, :] = np.where(inside, v, np.float32(MASKED)).transpose(0, 2, 1, 3)
    io["na_bias"] = nb.reshape(L, 8, P, HEADS * 640)
    wm = np.full((8, P, 384), MASKED, np.float32)
    for n in range(8):
        w0 = min(max(n - 1, 0), 5)
        q = n * P + np.arange(P)[:, None]
        k = w0 * P + np.arange(384)[None, :]
        wm[n][np.abs(q - k) <= 128] = 0.0
    io["wa_mask"] = wm
    t = np.arange(SEQ)
    inv = (np.float32(10000.0) ** (-np.arange(16, dtype=np.float32) / np.float32(16)))
    ang = np.concatenate([(t // 64).astype(np.float32)[:, None] * inv, (t % 64).astype(np.float32)[:, None] * inv], -1).T
    cos, sin = np.cos(ang).astype(np.float32), np.sin(ang).astype(np.float32)
    io["rope"] = c(np.stack([np.tile(cos, (4, 1)), np.tile(np.concatenate([-sin, sin]), (2, 1))]))
    sm = np.ones((P, T), np.float32)
    sm[0:64, 0::CHUNK] = 0
    sm[64:, CHUNK - 1::CHUNK] = 0
    io["smask"] = sm
    tri = np.tril(np.ones((CHUNK, CHUNK), np.float32))
    io["tri"] = c(np.stack([tri.T, tri]))
    return io


def kernel(**inputs):
    import concourse.bacc as bacc
    from concourse.bass_utils import run_bass_kernel_spmd
    arrays = lay_out(inputs)
    nc = bacc.Bacc("TRN2", target_bir_lowering=False, num_devices=1)
    io = {k: nc.dram_tensor(f"in_{k}", v.shape, F32, kind="ExternalInput").ap() for k, v in arrays.items()}
    out = nc.dram_tensor("out_0", (KT, P, SEQ), F32, kind="ExternalOutput").ap()
    build(nc, io, out)
    r = run_bass_kernel_spmd(nc, [{f"in_{k}": v for k, v in arrays.items()}], core_ids=[0])
    return r.results[0]["out_0"].reshape(KT * P, SEQ).T[None].copy()
```
